# Optimizing a Trainium2 kernel written in Bass

```python
import jax, jax.numpy as jnp
from jax import lax
import numpy as np

D_MODEL = 1024
BATCH = 1
SEQ = 1024
DEPTH = 1
DEC_BATCH = 8
DEC_SEQ = 1
PAST_LEN = 8192
PAGE_SIZE = 128

MIX_WIDTH = D_MODEL // 4
N_BRANCH = 4
RWKV_HEAD = 64
RWKV_HEADS = MIX_WIDTH // RWKV_HEAD
RWKV_DECAY_LORA = 32
RWKV_AAA_LORA = 32
RWKV_GATE_LORA = 64
RWKV_PROJ = 3 * MIX_WIDTH + RWKV_DECAY_LORA + RWKV_AAA_LORA + RWKV_GATE_LORA
RWKV_GN_EPS = 64e-5
POOL_WINDOWS = (2, 4, 8, 16)
POOL_GROUPS = 4
POOL_GROUP_WIDTH = MIX_WIDTH // POOL_GROUPS
POOL_HIST = 15
CONV_KERNEL = 31
CONV_HIST = CONV_KERNEL - 1
CONV_LN_EPS = 1e-5
SSM_HEAD_DIM = 64
SSM_HEADS = MIX_WIDTH // SSM_HEAD_DIM
SSM_GROUPS = 2
SSM_STATE = 128
SSM_CONV_KERNEL = 4
SSM_CONV_HIST = SSM_CONV_KERNEL - 1
SSM_CHUNK = 128
SSM_CONV_DIM = MIX_WIDTH + 2 * SSM_GROUPS * SSM_STATE
SSM_PROJ = MIX_WIDTH + SSM_CONV_DIM + SSM_HEADS
OFF_POOL = RWKV_PROJ
OFF_CONV = OFF_POOL + MIX_WIDTH
OFF_SSM = OFF_CONV + 2 * MIX_WIDTH
OFF_GATE = OFF_SSM + SSM_PROJ
IN_PROJ = OFF_GATE + N_BRANCH * D_MODEL
MOE_GROUPS = 4
MOE_PER_GROUP = 4
MOE_EXPERTS = MOE_GROUPS * MOE_PER_GROUP
MOE_TOPK = 2
MOE_HIDDEN = 256
NORM_EPS = 1e-6

kernel_name = 'hybrid_rwkv7_pool_conformer_ssd_hmoe_step'

def rmsnorm(x, g):
    xf = x.astype(jnp.float32)
    y = xf * lax.rsqrt(jnp.mean(xf * xf, -1, keepdims=True) + NORM_EPS)
    return (y * g.astype(jnp.float32)).astype(x.dtype)

def layernorm(x, g, b, eps):
    xf = x.astype(jnp.float32)
    mu = jnp.mean(xf, -1, keepdims=True)
    var = jnp.mean(jnp.square(xf - mu), -1, keepdims=True)
    return ((xf - mu) * lax.rsqrt(var + eps) * g + b).astype(x.dtype)

def causal_dwconv(hist, u, w, b):
    L = u.shape[1]
    full = jnp.concatenate([hist.astype(u.dtype), u], axis=1)
    y = lax.conv_general_dilated(full, w.astype(u.dtype)[:, None, :], (1,), 'VALID',
                                 dimension_numbers=('NWC', 'WIO', 'NWC'), feature_group_count=u.shape[-1])
    return y + b.astype(u.dtype), full[:, L:]

def rwkv7_mix(p, shift0, wkv0, lw):
    bsz, L, _ = p.shape
    W, H, N = MIX_WIDTH, RWKV_HEADS, RWKV_HEAD
    f32 = jnp.float32
    prev = jnp.concatenate([shift0[:, None, :].astype(p.dtype), p[:, :-1]], axis=1)
    q = p + (prev - p) * lw['rwkv_mu']
    r, k, v = q[..., :W], q[..., W:2 * W], q[..., 2 * W:3 * W]
    o = 3 * W
    wl = q[..., o:o + RWKV_DECAY_LORA]
    o += RWKV_DECAY_LORA
    al = q[..., o:o + RWKV_AAA_LORA]
    o += RWKV_AAA_LORA
    gl = q[..., o:o + RWKV_GATE_LORA]
    w_log = -jax.nn.softplus(-(lw['rwkv_w0'] + jnp.tanh(wl) @ lw['rwkv_w2'])) - 0.5
    decay = jnp.exp(-jnp.exp(w_log.astype(f32)))
    a = jax.nn.sigmoid(lw['rwkv_a0'] + al @ lw['rwkv_a2'])
    g = jax.nn.sigmoid(gl) @ lw['rwkv_g2']
    heads = lambda t: t.astype(f32).reshape(bsz, L, H, N)
    kk = heads(k * lw['rwkv_kk'])
    kk = kk * lax.rsqrt(jnp.maximum(jnp.sum(kk * kk, -1, keepdims=True), 1e-24))
    k = k * (1.0 + (a - 1.0) * lw['rwkv_ka'])
    rh, kh, vh, ah, dh = heads(r), heads(k), heads(v), heads(a), heads(decay)
    bh = kk * ah

    def step(S, inp):
        r_t, d_t, k_t, v_t, kk_t, b_t = inp
        sa = -jnp.einsum('bhij,bhj->bhi', S, kk_t)
        S = S * d_t[:, :, None, :] + sa[..., None] * b_t[:, :, None, :] + v_t[..., None] * k_t[:, :, None, :]
        return S, jnp.einsum('bhij,bhj->bhi', S, r_t)

    tmaj = lambda t: jnp.swapaxes(t, 0, 1)
    S_last, y = lax.scan(step, wkv0.astype(f32), tuple(tmaj(t) for t in (rh, dh, kh, vh, kk, bh)))
    y = tmaj(y)
    mu = jnp.mean(y, -1, keepdims=True)
    var = jnp.mean(jnp.square(y - mu), -1, keepdims=True)
    y = (y - mu) * lax.rsqrt(var + RWKV_GN_EPS)
    y = y * lw['rwkv_ln_g'].reshape(H, N) + lw['rwkv_ln_b'].reshape(H, N)
    y = y + jnp.sum(rh * kh * lw['rwkv_rk'], -1, keepdims=True) * vh
    out = y.reshape(bsz, L, W) * g
    return out.astype(p.dtype), p[:, -1], S_last

def pool_mix(u, hist, pos0, lw):
    bsz, L, W = u.shape
    f32 = jnp.float32
    full = jnp.concatenate([hist.astype(u.dtype), u], axis=1)
    cs = jnp.concatenate([jnp.zeros((bsz, 1, W), f32), jnp.cumsum(full.astype(f32), axis=1)], axis=1)
    pos = pos0 + jnp.arange(L, dtype=jnp.int32)
    end = cs[:, POOL_HIST + 1:]
    means = []
    for gi, win in enumerate(POOL_WINDOWS):
        c = slice(gi * POOL_GROUP_WIDTH, (gi + 1) * POOL_GROUP_WIDTH)
        start = cs[:, POOL_HIST + 1 - win:POOL_HIST + 1 - win + L, c]
        count = jnp.minimum(pos + 1, win).astype(f32)[None, :, None]
        means.append((end[..., c] - start) / count)
    diff = (jnp.concatenate(means, -1) - u.astype(f32)).reshape(bsz, L, POOL_GROUPS, POOL_GROUP_WIDTH)
    out = jnp.einsum('blgc,gcd->blgd', diff, lw['pool_w'].astype(f32)).reshape(bsz, L, W) * lw['pool_scale']
    return out.astype(u.dtype), full[:, L:]

def conformer_conv(s, hist, lw):
    W = MIX_WIDTH
    c = s[..., :W] * jax.nn.sigmoid(s[..., W:])
    y, hist1 = causal_dwconv(hist, c, lw['conv_w'], lw['conv_b'])
    y = layernorm(y, lw['conv_ln_g'], lw['conv_ln_b'], CONV_LN_EPS)
    return jax.nn.silu(y), hist1

def ssd_chunked(x, dt, a, bm, cm, h0):
    f32 = jnp.float32
    bsz, L = x.shape[0], x.shape[1]
    rep = SSM_HEADS // SSM_GROUPS
    q = min(SSM_CHUNK, L)
    pad = (-L) % q
    xdt = x.astype(f32) * dt[..., None]
    da = dt * a
    bh = jnp.repeat(bm.astype(f32), rep, axis=2)
    ch = jnp.repeat(cm.astype(f32), rep, axis=2)
    if pad:
        padw = lambda t: jnp.pad(t, [(0, 0), (0, pad)] + [(0, 0)] * (t.ndim - 2))
        xdt, da, bh, ch = padw(xdt), padw(da), padw(bh), padw(ch)
    nc = (L + pad) // q
    chunk = lambda t: t.reshape((bsz, nc, q) + t.shape[2:])
    xdt, da, bh, ch = chunk(xdt), chunk(da), chunk(bh), chunk(ch)
    acs = jnp.cumsum(da, axis=2)
    causal = jnp.tril(jnp.ones((q, q), dtype=bool))[None, None, :, :, None]
    seg = acs[:, :, :, None, :] - acs[:, :, None, :, :]
    lmat = jnp.exp(jnp.where(causal, seg, -jnp.inf))
    scores = jnp.einsum('bcihn,bcjhn->bcijh', ch, bh) * lmat
    y_diag = jnp.einsum('bcijh,bcjhp->bcihp', scores, xdt)
    to_end = jnp.exp(acs[:, :, -1:, :] - acs)
    states = jnp.einsum('bcjhn,bcjh,bcjhp->bchpn', bh, to_end, xdt)
    chunk_decay = jnp.exp(acs[:, :, -1, :])

    def step(h, inp):
        st, dec = inp
        return h * dec[:, :, None, None] + st, h

    h_last, h_in = lax.scan(step, h0.astype(f32), (jnp.moveaxis(states, 1, 0), jnp.moveaxis(chunk_decay, 1, 0)))
    h_in = jnp.moveaxis(h_in, 0, 1)
    y_off = jnp.einsum('bcihn,bchpn,bcih->bcihp', ch, h_in, jnp.exp(acs))
    y = (y_diag + y_off).reshape((bsz, nc * q) + x.shape[2:])[:, :L]
    return y, h_last

def mamba2_mix(s, conv0, ssm0, lw):
    bsz, L, _ = s.shape
    W, H, P, G, N = MIX_WIDTH, SSM_HEADS, SSM_HEAD_DIM, SSM_GROUPS, SSM_STATE
    f32 = jnp.float32
    z = s[..., :W]
    xbc, conv1 = causal_dwconv(conv0, s[..., W:W + SSM_CONV_DIM], lw['ssm_conv_w'], lw['ssm_conv_b'])
    xbc = jax.nn.silu(xbc)
    dt = jax.nn.softplus(s[..., W + SSM_CONV_DIM:].astype(f32) + lw['ssm_dt_bias'].astype(f32))
    xs = xbc[..., :W].reshape(bsz, L, H, P)
    bm = xbc[..., W:W + G * N].reshape(bsz, L, G, N)
    cm = xbc[..., W + G * N:].reshape(bsz, L, G, N)
    a = -jnp.exp(lw['ssm_a_log'].astype(f32))
    y, ssm1 = ssd_chunked(xs, dt, a, bm, cm, ssm0)
    y = y + lw['ssm_d'].astype(f32)[:, None] * xs.astype(f32)
    y = y.reshape(bsz, L, W) * jax.nn.silu(z.astype(f32))
    return rmsnorm(y, lw['ssm_norm_g']).astype(s.dtype), conv1, ssm1

def token_mixers(h, st, pos0, lw):
    shift0, wkv0, pool0, conv0, sconv0, ssm0 = st
    bsz, L, _ = h.shape
    proj = h @ lw['w_in']
    o_rwkv, shift1, wkv1 = rwkv7_mix(proj[..., :OFF_POOL], shift0, wkv0, lw)
    o_pool, pool1 = pool_mix(proj[..., OFF_POOL:OFF_CONV], pool0, pos0, lw)
    o_conv, conv1 = conformer_conv(proj[..., OFF_CONV:OFF_SSM], conv0, lw)
    o_ssm, sconv1, ssm1 = mamba2_mix(proj[..., OFF_SSM:OFF_GATE], sconv0, ssm0, lw)
    gates = jax.nn.sigmoid(proj[..., OFF_GATE:]).reshape(bsz, L, N_BRANCH, D_MODEL)
    branches = jnp.stack([o_rwkv, o_pool, o_conv.astype(h.dtype), o_ssm], axis=2)
    up = jnp.einsum('blkc,kcd->blkd', branches, lw['w_branch'])
    merged = jnp.sum(up * gates, axis=2)
    return (merged @ lw['w_out']).astype(h.dtype), (shift1, wkv1, pool1, conv1, sconv1, ssm1)

def hier_moe(h, lw):
    f32 = jnp.float32
    g_logits = (h @ lw['moe_router_group_w'] + lw['moe_router_group_b']).astype(f32)
    g_prob = jax.nn.softmax(g_logits, -1)
    _, grp = lax.top_k(g_logits, 1)
    e_logits = (h @ lw['moe_router_expert_w'] + lw['moe_router_expert_b']).astype(f32)
    e_logits = e_logits.reshape(h.shape[:-1] + (MOE_GROUPS, MOE_PER_GROUP))
    in_group = jnp.take_along_axis(e_logits, grp[..., None], axis=-2)[..., 0, :]
    top_v, top_i = lax.top_k(in_group, MOE_TOPK)
    w_top = jax.nn.softmax(top_v, -1) * jnp.take_along_axis(g_prob, grp, -1)
    eid = grp * MOE_PER_GROUP + top_i
    gate = jnp.sum(jax.nn.one_hot(eid, MOE_EXPERTS, dtype=f32) * w_top[..., None], axis=-2)
    out = jnp.zeros(h.shape, f32)
    for gi in range(MOE_GROUPS):
        e = slice(gi * MOE_PER_GROUP, (gi + 1) * MOE_PER_GROUP)
        hg = jnp.einsum('bld,edf->blef', h, lw['moe_w_gate'][e])
        hu = jnp.einsum('bld,edf->blef', h, lw['moe_w_up'][e])
        act = jax.nn.silu(hg) * hu * gate[..., e, None].astype(h.dtype)
        out = out + jnp.einsum('blef,efd->bld', act, lw['moe_w_down'][e])
    return out.astype(h.dtype)

def run_trunk(x, states, pos0, params, final_norm_g):
    new = [[] for _ in range(len(states))]
    for l in range(DEPTH):
        lw = {name: arr[l] for name, arr in params.items()}
        st = tuple(s[l] for s in states)
        m, st1 = token_mixers(rmsnorm(x, lw['norm_mix_g']), st, pos0, lw)
        x = x + m
        x = x + hier_moe(rmsnorm(x, lw['norm_ffn_g']), lw)
        for lst, s in zip(new, st1):
            lst.append(s.astype(x.dtype))
    return rmsnorm(x, final_norm_g), tuple(jnp.stack(lst) for lst in new)

def setup_inputs(seed: int = 0) -> dict:
    key = jax.random.key(seed)
    ks = iter(jax.random.split(key, 64))
    f32 = jnp.float32
    nrm = lambda shape, scale: scale * jax.random.normal(next(ks), shape, f32)
    gain = lambda shape: 1.0 + 0.1 * jax.random.normal(next(ks), shape, f32)
    L, W, D = DEPTH, MIX_WIDTH, D_MODEL
    dt_init = jnp.exp(jax.random.uniform(next(ks), (L, SSM_HEADS), f32, np.log(1e-3), np.log(1e-1)))
    return {
        'x_prompt': nrm((BATCH, SEQ, D), 1.0),
        'x_sample': nrm((DEC_BATCH, DEC_SEQ, D), 1.0),
        'state_rwkv_shift': nrm((L, DEC_BATCH, RWKV_PROJ), 1.0),
        'state_rwkv_wkv': nrm((L, DEC_BATCH, RWKV_HEADS, RWKV_HEAD, RWKV_HEAD), 0.3),
        'state_pool': nrm((L, DEC_BATCH, POOL_HIST, W), 1.0),
        'state_conv': nrm((L, DEC_BATCH, CONV_HIST, W), 0.5),
        'state_ssm_conv': nrm((L, DEC_BATCH, SSM_CONV_HIST, SSM_CONV_DIM), 1.0),
        'state_ssm': nrm((L, DEC_BATCH, SSM_HEADS, SSM_HEAD_DIM, SSM_STATE), 0.1),
        'norm_mix_g': gain((L, D)),
        'w_in': nrm((L, D, IN_PROJ), D ** -0.5),
        'rwkv_mu': jax.random.uniform(next(ks), (L, RWKV_PROJ), f32),
        'rwkv_w0': nrm((L, W), 0.5) - 1.0,
        'rwkv_w2': nrm((L, RWKV_DECAY_LORA, W), RWKV_DECAY_LORA ** -0.5),
        'rwkv_a0': nrm((L, W), 0.5),
        'rwkv_a2': nrm((L, RWKV_AAA_LORA, W), RWKV_AAA_LORA ** -0.5),
        'rwkv_g2': nrm((L, RWKV_GATE_LORA, W), RWKV_GATE_LORA ** -0.5),
        'rwkv_kk': gain((L, W)),
        'rwkv_ka': gain((L, W)),
        'rwkv_rk': nrm((L, RWKV_HEADS, RWKV_HEAD), 0.1),
        'rwkv_ln_g': gain((L, W)),
        'rwkv_ln_b': nrm((L, W), 0.01),
        'pool_w': nrm((L, POOL_GROUPS, POOL_GROUP_WIDTH, POOL_GROUP_WIDTH), POOL_GROUP_WIDTH ** -0.5),
        'pool_scale': gain((L, W)),
        'conv_w': nrm((L, CONV_KERNEL, W), CONV_KERNEL ** -0.5),
        'conv_b': nrm((L, W), 0.01),
        'conv_ln_g': gain((L, W)),
        'conv_ln_b': nrm((L, W), 0.01),
        'ssm_conv_w': nrm((L, SSM_CONV_KERNEL, SSM_CONV_DIM), 0.5),
        'ssm_conv_b': nrm((L, SSM_CONV_DIM), 0.01),
        'ssm_dt_bias': dt_init + jnp.log(-jnp.expm1(-dt_init)),
        'ssm_a_log': jnp.log(jax.random.uniform(next(ks), (L, SSM_HEADS), f32, 1.0, 16.0)),
        'ssm_d': gain((L, SSM_HEADS)),
        'ssm_norm_g': gain((L, W)),
        'w_branch': nrm((L, N_BRANCH, W, D), W ** -0.5),
        'w_out': nrm((L, D, D), D ** -0.5),
        'norm_ffn_g': gain((L, D)),
        'moe_router_group_w': nrm((L, D, MOE_GROUPS), D ** -0.5),
        'moe_router_group_b': nrm((L, MOE_GROUPS), 0.01),
        'moe_router_expert_w': nrm((L, D, MOE_EXPERTS), D ** -0.5),
        'moe_router_expert_b': nrm((L, MOE_EXPERTS), 0.01),
        'moe_w_gate': nrm((L, MOE_EXPERTS, D, MOE_HIDDEN), D ** -0.5),
        'moe_w_up': nrm((L, MOE_EXPERTS, D, MOE_HIDDEN), D ** -0.5),
        'moe_w_down': nrm((L, MOE_EXPERTS, MOE_HIDDEN, D), MOE_HIDDEN ** -0.5),
        'final_norm_g': gain((D,)),
    }

def reference(x_prompt, x_sample, state_rwkv_shift, state_rwkv_wkv, state_pool, state_conv, state_ssm_conv, state_ssm,
              norm_mix_g, w_in, rwkv_mu, rwkv_w0, rwkv_w2, rwkv_a0, rwkv_a2, rwkv_g2, rwkv_kk, rwkv_ka, rwkv_rk,
              rwkv_ln_g, rwkv_ln_b, pool_w, pool_scale, conv_w, conv_b, conv_ln_g, conv_ln_b, ssm_conv_w, ssm_conv_b,
              ssm_dt_bias, ssm_a_log, ssm_d, ssm_norm_g, w_branch, w_out, norm_ffn_g, moe_router_group_w,
              moe_router_group_b, moe_router_expert_w, moe_router_expert_b, moe_w_gate, moe_w_up, moe_w_down,
              final_norm_g):
    params = {
        'norm_mix_g': norm_mix_g, 'w_in': w_in, 'rwkv_mu': rwkv_mu, 'rwkv_w0': rwkv_w0, 'rwkv_w2': rwkv_w2,
        'rwkv_a0': rwkv_a0, 'rwkv_a2': rwkv_a2, 'rwkv_g2': rwkv_g2, 'rwkv_kk': rwkv_kk, 'rwkv_ka': rwkv_ka,
        'rwkv_rk': rwkv_rk, 'rwkv_ln_g': rwkv_ln_g, 'rwkv_ln_b': rwkv_ln_b, 'pool_w': pool_w,
        'pool_scale': pool_scale, 'conv_w': conv_w, 'conv_b': conv_b, 'conv_ln_g': conv_ln_g,
        'conv_ln_b': conv_ln_b, 'ssm_conv_w': ssm_conv_w, 'ssm_conv_b': ssm_conv_b, 'ssm_dt_bias': ssm_dt_bias,
        'ssm_a_log': ssm_a_log, 'ssm_d': ssm_d, 'ssm_norm_g': ssm_norm_g, 'w_branch': w_branch, 'w_out': w_out,
        'norm_ffn_g': norm_ffn_g, 'moe_router_group_w': moe_router_group_w,
        'moe_router_group_b': moe_router_group_b, 'moe_router_expert_w': moe_router_expert_w,
        'moe_router_expert_b': moe_router_expert_b, 'moe_w_gate': moe_w_gate, 'moe_w_up': moe_w_up,
        'moe_w_down': moe_w_down,
    }
    bp, dtp = x_prompt.shape[0], x_prompt.dtype
    empty = (jnp.zeros((DEPTH, bp, RWKV_PROJ), dtp),
             jnp.zeros((DEPTH, bp, RWKV_HEADS, RWKV_HEAD, RWKV_HEAD), dtp),
             jnp.zeros((DEPTH, bp, POOL_HIST, MIX_WIDTH), dtp),
             jnp.zeros((DEPTH, bp, CONV_HIST, MIX_WIDTH), dtp),
             jnp.zeros((DEPTH, bp, SSM_CONV_HIST, SSM_CONV_DIM), dtp),
             jnp.zeros((DEPTH, bp, SSM_HEADS, SSM_HEAD_DIM, SSM_STATE), dtp))
    y_prompt, (p_shift, p_wkv, p_pool, p_conv, p_ssm_conv, p_ssm) = run_trunk(
        x_prompt, empty, 0, params, final_norm_g)
    past = (state_rwkv_shift, state_rwkv_wkv, state_pool, state_conv, state_ssm_conv, state_ssm)
    y_sample, (s_shift, s_wkv, s_pool, s_conv, s_ssm_conv, s_ssm) = run_trunk(
        x_sample, past, PAST_LEN, params, final_norm_g)
    return (y_prompt, y_sample, p_shift, p_wkv, p_pool, p_conv, p_ssm_conv, p_ssm,
            s_shift, s_wkv, s_pool, s_conv, s_ssm_conv, s_ssm)


_drawn_inputs = setup_inputs


def setup_inputs(seed=0):
    import zlib

    import numpy as np

    out = dict(_drawn_inputs(seed))
    spreads = {}
    factors = {'rwkv_kk': 9.125,
     'rwkv_ln_b': 19.161,
     'conv_b': 5.342,
     'conv_ln_b': 6.232,
     'moe_router_group_b': 3.892,
     'moe_router_expert_b': 6.488}
    for name, (base, spread) in spreads.items():
        noise = np.random.default_rng([zlib.crc32(name.encode()), seed]).standard_normal(out[name].shape)
        drawn = base * np.exp(spread * noise) if base else spread * noise
        out[name] = __import__('jax').numpy.asarray(drawn.astype(out[name].dtype))
    for name, factor in factors.items():
        out[name] = (out[name] * factor).astype(out[name].dtype)
    return out
```

```python
from contextlib import ExitStack

import numpy as np

import concourse.bass as bass
from concourse import mybir

F32 = mybir.dt.float32
ALU = mybir.AluOpType
ACT = mybir.ActivationFunctionType
AX = mybir.AxisListType.X

P = 128
D = 1024
TP = 1024
NSMP = 8
T = TP + NSMP
KT = D // P
NCH = 3
CW = T // NCH
PAD = 30
PW = PAD + T
HD = 64
RC = 64
SC = 128
NITER = TP // SC
CONVK = 31
SSMK = 4
POOLH = 15
NE = 16
NG = 4
HID = 256
BR = 4
DECAY_SCALE = float(np.exp(-0.5))

S_POOL, S_CA, S_CG, S_Z, S_XBC, S_R, S_K, S_V, S_LORA = 0, 2, 4, 6, 8, 14, 16, 18, 20
NSLOT = 21
O_POOL, O_RWKV, O_CONV, O_SSM = 0, 2, 4, 6
N_GATE0 = NSLOT
N_BR0 = N_GATE0 + BR * KT
N_OUT0 = N_BR0 + KT
N_W = N_OUT0 + KT

VEC = {}
_n = 0
for _name, _w in [("mu", 7), ("w0", 2), ("a0", 2), ("kkw", 2), ("ka", 2), ("rk", 2), ("ln_g", 2), ("ln_b", 2),
                  ("pool_scale", 2), ("conv_b", 2), ("conv_ln_g", 2), ("conv_ln_b", 2), ("ssm_b", 6), ("ssm_d", 2),
                  ("ssm_g", 2), ("g_mix", 8), ("g_ffn", 8), ("g_fin", 8), ("conv_w", 2 * CONVK), ("ssm_w", 6 * SSMK),
                  ("dt_bias", 4), ("a_log", 4), ("r_bias", 20)]:
    VEC[_name] = (_n, _w)
    _n += _w
NVEC = _n

CST = {}
_n = 0
for _name, _w in [("ident", P), ("ones", P), ("bones", P), ("tri", P), ("m_strict_incl", 2 * P), ("m_lev1_incl", 2 * P),
                  ("m_lev1_low", P), ("m_lev_low", 5 * P), ("imask", HD), ("rcount", 2 * 16), ("rwin", 2), ("rank4", 4)]:
    CST[_name] = (_n, _w)
    _n += _w
NCST = _n
NORM_EPS, LN_EPS, GN_EPS = 1e-6, 1e-5, 64e-5
NSMALL_IN = 7 + 2 + 2 + 6
NSMALL_OUT = 1 + 2 + 1 + 2 + 6 + 1
PER_TURN = 9
LEVELS = (2, 4, 8, 16, 32)


def constants():
    c = np.zeros((P, NCST), np.float32)

    def put(name, a):
        o, w = CST[name]
        c[:a.shape[0], o:o + w] = a.reshape(a.shape[0], w)

    i = np.arange(P)
    same = (i[:, None] // RC) == (i[None, :] // RC)
    upper = (same & (i[:, None] < i[None, :])).astype(np.float32)
    incl = (same & (i[:, None] <= i[None, :])).astype(np.float32)

    def level_up(b):
        return (((i[:, None] // (2 * b)) == (i[None, :] // (2 * b))) & ((i[:, None] // b) % 2 == 0)
                & ((i[None, :] // b) % 2 == 1)).astype(np.float32)

    put("ident", np.eye(P))
    put("ones", np.ones((P, P)))
    put("bones", same.astype(np.float32))
    put("tri", (i[:, None] <= i[None, :]).astype(np.float32))
    put("m_strict_incl", np.stack([upper, incl], 1))
    put("m_lev1_incl", np.stack([-level_up(1), incl], 1))
    put("m_lev1_low", -level_up(1).T)
    put("m_lev_low", np.stack([level_up(b).T for b in LEVELS], 1))
    put("imask", np.eye(HD)[i % HD])
    win = np.array([[2, 8], [4, 16]])[i // HD]
    put("rcount", 1.0 / np.minimum(np.arange(16)[None, None, :] + 1, win[:, :, None]))
    put("rwin", 1.0 / win)
    put("rank4", np.broadcast_to(np.array([4.0, 3.0, 2.0, 1.0]), (P, 4)))
    return c


class Link:

    def __init__(self, eng, sem):
        self.eng, self.sem, self.n, self.base = eng, sem, 0, 0

    def __call__(self, ins):
        ins.then_inc(self.sem, 1)
        self.n += 1
        self.eng.wait_ge(self.sem, self.base + self.n)

    def enter(self, i, per):
        self.n0, self.per = self.n, per
        self.base = i * per

    def leave(self, turns):
        assert self.n - self.n0 == self.per, (self.n - self.n0, self.per)
        self.n += self.per * (turns - 1)
        self.base = 0


def build(nc, ins, outs):
    ctx = ExitStack()
    with ctx:
        def sb(name, shape):
            return ctx.enter_context(nc.sbuf_tensor(name, shape, F32))

        sems = {}

        def sem(name):
            if name not in sems:
                sems[name] = ctx.enter_context(nc.semaphore(name))
            return sems[name]

        gate_scratch = nc.dram_tensor("gate_scratch", (P, BR * KT, T), F32, kind="Internal").ap()

        vec = sb("vec", [P, NVEC])
        cst = sb("cst", [P, NCST])
        wring = sb("wring", [P, 2, KT, P])
        H = sb("H", [P, KT, T])
        PR = sb("PR", [P, NSLOT, PW])
        lora_w = sb("lora_w", [P, 2 * P])
        pool_w = sb("pool_w", [P, 2, P])
        w_dt = sb("w_dt", [P, KT, 4])
        w_r = sb("w_r", [P, KT, 20])
        pool_tail = sb("pool_tail", [P, 2, POOLH])
        pool_h = sb("pool_h", [P, 2, NSMP, 16])
        conv_h = sb("conv_h", [P, 2, NSMP, CONVK])
        ssm_h = sb("ssm_h", [P, 6, NSMP, SSMK])
        shift_in = sb("shift_in", [P, 7, NSMP])
        shift_out = sb("shift_out", [P, 7, 1 + NSMP])
        stage = sb("stage", [P, 3, CW])
        kk = sb("kk", [P, 2, TP])
        bb = sb("bb", [P, 2, TP])
        pc = sb("pc", [P, 2, TP // RC])
        dt_t = sb("dt_t", [P, 9, 4])
        da_t = sb("da_t", [P, 9, 4])
        smallv = sb("smallv", [P, 16])
        smallv2 = sb("smallv2", [P, 20])
        dsum = sb("dsum", [P, NSMP])
        smp = sb("smp", [P, 6, 2, NSMP])
        SCRW = 10700
        scr = sb("scr", [P, SCRW])
        tick = sb("tick", [P, 4])
        ps = ctx.enter_context(nc.psum_tensor("ps", [P, 8, 512], F32))

        def carve(start, *shape):
            n = int(np.prod(shape))
            assert start + n <= SCRW, (start, shape)
            a = scr[:, start:start + n]
            if len(shape) == 1:
                return a
            names = "abcd"[:len(shape)]
            return a.rearrange(f"p ({' '.join(names)}) -> p {' '.join(names)}",
                               **{k: v for k, v in zip(names, shape)})

        def v(name, j=0, w=1):
            o = VEC[name][0] + j
            return vec[:, o:o + w]

        def cc(name, j=0, w=None):
            o, full = CST[name]
            return cst[:, o + j:o + (j + w if w else full)]

        ident, ones, bones, tri = cc("ident"), cc("ones"), cc("bones"), cc("tri")

        def chunk(c):
            return slice(c * CW, (c + 1) * CW)

        def row(slot, a=0, b=T):
            return PR[:, slot, PAD + a:PAD + b]

        def rows(slot, n, a=0, b=T):
            return PR[:, slot:slot + n, PAD + a:PAD + b]

        def ps3(b, w=CW):
            return ps[:, b:b + 3, 0:w]

        def as3(ap):
            return ap.rearrange("p (c w) -> p c w", c=NCH)

        x_t = carve(0, KT, T)
        sq = carve(8 * T, 2, T)
        STG = stage[:, :, :].rearrange("p a b -> p (a b)")
        RS0 = STG
        SG, AA, LL, TM = carve(0, 2, T), carve(2 * T, 2, T), carve(4 * T, 2, T), carve(6 * T, 2, T)
        PA, PB = carve(8 * T, PW), carve(8 * T + PW, PW)
        RESET = STG[:, 0:TP]

        SW = carve(0, NSMP, 2, HD)
        XE = [carve(1024 * (1 + j), NSMP, 2, HD) for j in range(2)]
        SH = carve(3072, NSMP, 2, P)
        BE = carve(5120, NSMP, 2, P)
        W2 = carve(7168, NSMP, 2, P)
        dsm = carve(9216, 16, 16)
        XS = carve(9472, 6, NSMP)
        XSS = carve(9520, 6, NSMP)
        XSW = carve(9568, 6, NSMP, SSMK)
        CHW = carve(8 * T + 2 * PW, NSMP, CONVK)

        KR = carve(0, 4, 2, P)
        BT, KTB, VV = carve(1024, 4, P), carve(1536, 4, P), carve(2048, 4, P)
        NL, NLB, X1, TT, U = (carve(2560 + 512 * j, 4, P) for j in range(5))
        BM, MK = carve(5120, 4, 2, P), carve(6144, 4, 2, P)
        VT, BTT, KTT = (carve(7168 + 512 * j, 4, P) for j in range(3))
        XN, SA, ST = (carve(8704 + 256 * j, 2, P) for j in range(3))
        PCS = carve(9472, 2, 2)
        XC = carve(9480, 6, SC)
        HT = carve(10248, 2, P)
        ACB, EE, EA = NL, NLB, X1
        XDT, XTE = carve(7168, 2, P), carve(7424, 2, P)
        BTOK, GM = carve(7680, 2, P), carve(8192, 2, P)
        SX, SZ = carve(6144, 6, SC), carve(6912, 2, SC)
        DAI, DTI, AT, TE, DEC = (smallv2[:, 4 * j:4 * j + 4] for j in range(5))

        V1, V2, V3, V4, V5 = (carve(2 * j * T, 2, T) for j in range(5))

        block = ctx.enter_context(nc.Block())

        def bc(ap, shape):
            return ap.to_broadcast(shape)

        def mid(ap, n):
            return ap.unsqueeze(1).to_broadcast([ap.shape[0], n, ap.shape[1]])

        def last(ap, n):
            return ap.unsqueeze(len(ap.shape)).to_broadcast(list(ap.shape) + [n])


        X2 = S_XBC
        PRF = PR[:, :, :].rearrange("p s w -> p (s w)")
        GU = [PRF[:, s * 4096:(s + 1) * 4096].rearrange("p (k m) -> p k m", k=KT) for s in range(2)]
        DN = [PRF[:, 16 * PW + s * 2048:16 * PW + (s + 1) * 2048].rearrange("p (k m) -> p k m", k=2) for s in range(2)]
        GB = [carve(s * 4 * T, BR, T) for s in range(2)]
        GP = carve(8 * T, 2, CW)
        SQ2 = carve(0, 2, T)
        RS = carve(2 * T, T)
        RO = 3 * T
        LG, TE16, GK16 = carve(RO, 9, 20), carve(RO + 180, 9, 4, 4), carve(RO + 324, 9, 4, 4)
        q4 = [carve(RO + 468 + 36 * j, 9, 4) for j in range(8)]
        q1 = [carve(RO + 756 + 9 * j, 9) for j in range(8)]
        GT = scr[0:NE, RO + 900:RO + 900 + T]
        SELC = scr[0:NE, RO + 900 + T:RO + 902 + T]
        ACTB = [carve(5 * T + s * 2 * T, 2, T) for s in range(2)]
        GBC = [carve(s * T, T) for s in range(2)]
        SIL = carve(9 * T, 2, CW)
        NORMS = {"mix": (sq, 0), "ffn": (SQ2, 1), "fin": (SQ2, 2)}

        def xk(tag, k):
            return x_t[:, k, :] if tag == "mix" else row(X2 + k)

        @block.sync
        def _(sp):
            for h in range(2):
                sp.dma_start(x_t[:, 4 * h:4 * h + 4, :], ins["x_t"][:, 4 * h:4 * h + 4, :]).then_inc(sem(f"x_in{h}"), 16)

            def load(n, slot):
                sp.dma_start(wring[:, slot:slot + 1, :, :].rearrange("p a k m -> p a (k m)"),
                             ins["w_all"][:, bass.ds(n, 1), :]).then_inc(sem(f"w_in{slot}"), 16)
            load(0, 0)
            load(1, 1)
            with sp.Fori(1, N_BR0 // 2 + 1) as j:
                sp.wait_ge(sem("dense"), 6 * j - 3)
                load(2 * j, 0)
                sp.wait_ge(sem("dense"), 6 * j)
                load(2 * j + 1, 1)
            sp.wait_ge(sem("dense"), 3 * N_BR0)
            load(N_BR0 + 1, 0)
            for n in range(N_BR0 + 2, N_W):
                if n < N_OUT0 + 2:
                    sp.wait_ge(sem("up_mm"), 12 * (n - N_BR0 - 1))
                else:
                    sp.wait_ge(sem("out_mm"), 3 * (n - N_OUT0 - 1))
                load(n, n % 2)

            def load_expert(e, s):
                sp.dma_start(GU[s].rearrange("p k m -> p (k m)"), ins["w_gu"][bass.ds(e, 1), :, :].rearrange("a p m -> (a p) m")
                             ).then_inc(sem(f"gu_in{s}"), 16)
                sp.dma_start(DN[s].rearrange("p k m -> p (k m)"), ins["w_dn"][bass.ds(e, 1), :, :].rearrange("a p m -> (a p) m")
                             ).then_inc(sem(f"dn_in{s}"), 16)
            sp.wait_ge(sem("up_mm"), 12 * KT)
            load_expert(0, 0)
            load_expert(1, 1)
            with sp.Fori(1, NE // 2) as j:
                for s in range(2):
                    sp.wait_ge(sem("down_mm"), 24 * (2 * j + s - 1))
                    load_expert(2 * j + s, s)
            for k in range(KT):
                sp.wait_ge(sem("y_ready"), k + 1)
                sp.dma_start(outs["y_t"][:, k, :], H[:, k, :]).then_inc(sem("y_out"), 16)
            sp.wait_ge(sem("y_out"), 16 * KT)
            sp.wait_ge(sem("small_out"), 16 * NSMALL_OUT)
            for c in range(3):
                sp.wait_ge(sem(f"gate_out{c}"), 16 * BR * KT)

        @block.tensor
        def _(pe):
            def norm_sums(tag):
                for k in range(KT):
                    pe.wait_ge(sem("norm_sq"), KT * NORMS[tag][1] + k + 1)
                    for c in range(NCH):
                        mm = pe.matmul(ps[:, c, 0:CW], ones, NORMS[tag][0][:, k % 2, chunk(c)], start=k == 0, stop=k == KT - 1)
                    mm.then_inc(sem("norm_sum"), 1)

            def half(slot, c, lo, hi, evac, loaded):
                if lo == 0 and evac is not None:
                    pe.wait_ge(sem("evac"), evac)
                if lo == 0 and c == 0:
                    pe.wait_ge(sem(f"w_in{slot}"), loaded)
                for k in range(lo, hi):
                    mm = pe.matmul(ps[:, c, 0:CW], wring[:, slot, k, :], H[:, k, chunk(c)], start=k == 0, stop=k == KT - 1)
                if hi == KT:
                    mm.then_inc(sem("dense"), 1)

            def pairs(j0, j1):
                with pe.Fori(j0, j1) as j:
                    for c in range(NCH):
                        half(1, c, 0, KT, 6 * j + 3 + c - 2, 16 * j + 16)
                    for c in range(NCH):
                        half(0, c, 0, KT, 6 * j + 6 + c - 2, 16 * j + 32)

            pe.wait_ge(sem("small_in"), 16 * NSMALL_IN)
            norm_sums("mix")
            pe.wait_ge(sem("h_ready"), 1)
            for c in range(NCH):
                half(0, c, 0, KT, None, 16)
            pairs(0, 3)
            pairs(3, 6)

            for t in range(2):
                pe.wait_ge(sem("k_sq"), t + 1)
                if t == 1:
                    pe.wait_ge(sem("k_ss"), 1)
                for c in range(NCH):
                    mm = pe.matmul(ps[:, 3 + c, 0:CW], bones, TM[:, t, chunk(c)], start=True, stop=True)
                mm.then_inc(sem("k_sum"), 1)
            pe.wait_ge(sem("lora_act"), 2)
            pe.wait_ge(sem("k_ss"), 2)
            for n in range(4):
                lo, t = 32 * (n // 2), n % 2
                if n:
                    pe.wait_ge(sem("lora_ev"), n)
                for c in range(NCH):
                    mm = pe.matmul(ps[:, 3 + c, 0:CW], lora_w[lo:lo + 32, t * P:(t + 1) * P],
                                   PR[lo:lo + 32, S_LORA, PAD + c * CW:PAD + (c + 1) * CW], start=True, stop=True)
                mm.then_inc(sem("lora_mm"), 1)

            pairs(6, 10)

            for n in range(9):
                m = P if n < 8 else NSMP
                for k in range(KT):
                    mm = pe.matmul(ps[0:m, 6, 4 * n:4 * n + 4], H[:, k, n * P:n * P + m], w_dt[:, k, :], start=k == 0,
                                   stop=k == KT - 1)
            mm.then_inc(sem("dt_mm"), 1)
            pe.wait_ge(sem("lora_ev"), 4)
            for t in range(2):
                pe.wait_ge(sem("rk_prod"), t + 1)
                if t == 1:
                    pe.wait_ge(sem("bonus"), 1)
                for c in range(NCH):
                    mm = pe.matmul(ps[:, 3 + c, 0:CW], bones, TM[:, t, chunk(c)], start=True, stop=True)
                mm.then_inc(sem("rk_sum"), 1)
            pe.wait_ge(sem("pool_diff"), 2)
            for t in range(2):
                pe.wait_ge(sem("evac"), 3 * NSLOT) if t == 0 else pe.wait_ge(sem("pool_ev"), 1)
                for c in range(NCH):
                    mm = pe.matmul(ps[:, c, 0:CW], pool_w[:, t, :], row(S_POOL + t, c * CW, (c + 1) * CW), start=True, stop=True)
                mm.then_inc(sem("pool_mm"), 1)

            pe.wait_ge(sem("bonus"), 2)
            for n in range(5):
                pe.wait_ge(sem("x_exp"), n + 1)
                b = 3 + 2 * (n % 2)
                if n == 1:
                    pe.wait_ge(sem("dt_read"), 1)
                for h in range(2):
                    mm = pe.matmul(ps[:, b + h, :], bones, XE[n % 2][:, 4 * h:4 * h + 4, :, :].rearrange("p a b c -> p (a b c)"),
                                   start=True, stop=True)
                mm.then_inc(sem("x_bc"), 1)
            pe.wait_ge(sem("dta"), 1)
            pe.wait_ge(sem("pool_ev"), 2)
            for hh in range(4):
                for q, src in enumerate((dt_t, da_t)):
                    mm = pe.matmul(ps[:, 7, (q * 4 + hh) * 8:(q * 4 + hh) * 8 + 8], bc(src[0:NSMP, 8, hh:hh + 1], [NSMP, P]),
                                   ident[0:NSMP, 0:NSMP], start=True, stop=True)
            mm.then_inc(sem("dt_bc"), 1)
            for n in range(2):
                pe.wait_ge(sem("bc_exp"), n + 1)
                if n == 0:
                    pe.wait_ge(sem("x_use"), 5)
                for h in range(4):
                    mm = pe.matmul(ps[:, h, :], ones, BE[:, 2 * h:2 * h + 2, :, :].rearrange("p a b c -> p (a b c)"),
                                   start=True, stop=True)
                mm.then_inc(sem("bc_bc"), 1)
            pe.wait_ge(sem("pre_done"), 1)

            with pe.Fori(0, NITER) as i:
                fill = [(j, c, h) for j in range(4) for c in range(NCH) for h in range(2)]

                def filler(k=1):
                    for _ in range(k):
                        j, c, h = fill.pop(0)
                        half((NSLOT + j) % 2, c, 4 * h, 4 * h + 4, 12 * i + 3 * NSLOT + 3 * j + c - 2,
                             16 * (2 * i + (NSLOT + j) // 2 + 1))

                pe.wait_ge(sem("kr"), i + 1)
                pe.wait_ge(sem("bkv"), i + 1)
                pe.wait_ge(sem("ssm_fin"), 2 * i)
                for q in range(4):
                    mm = pe.matmul(ps[:, 3, q * P:(q + 1) * P], KR[:, q, 0, :], BT[:, q, :], start=True, stop=True)
                mm.then_inc(sem("prod"), 1)
                for n in range(4):
                    for q in range(2 * (n % 2), 2 * (n % 2) + 2):
                        mm = pe.matmul(ps[:, 4 + n, (q % 2) * 256:(q % 2) * 256 + 256], (BT if n < 2 else KTB)[:, q, :],
                                       KR[:, q, :, :].rearrange("p a b -> p (a b)"), start=True, stop=True)
                    mm.then_inc(sem("prod"), 1)
                filler()
                for n, src in enumerate((VV, BT, KTB)):
                    if n == 0:
                        pe.wait_ge(sem("nl"), i + 1)
                    else:
                        pe.wait_ge(sem("masked"), 4 * i + n)
                    for q in range(4):
                        mm = pe.transpose(ps[:, 3 + n, q * P:(q + 1) * P], src[:, q, :], ident)
                    mm.then_inc(sem("turned"), 1)
                filler()
                for l in range(5):
                    pe.wait_ge(sem("lev"), 5 * i + l + 1)
                    pe.wait_ge(sem("masked"), 4 * i + 4)
                    for q in range(4):
                        mm = pe.matmul(ps[:, 6, q * P:(q + 1) * P], NLB[:, q, :], U[:, q, :], start=True, stop=True)
                    mm.then_inc(sem("x1"), 1)
                    filler()
                    pe.wait_ge(sem("x1c"), 5 * i + l + 1)
                    for q in range(4):
                        mm = pe.matmul(ps[:, 7, q * P:(q + 1) * P], TT[:, q, :], X1[:, q, :], start=True, stop=True)
                    mm.then_inc(sem("du"), 1)
                    if l < 4:
                        pe.wait_ge(sem("turn_c"), 3 * i + 1)
                        for q in range(4):
                            mm = pe.matmul(ps[:, 3, q * P:(q + 1) * P], X1[:, q, :], TT[:, q, :], start=True, stop=True)
                        mm.then_inc(sem("dt_"), 1)
                    filler()
                pe.wait_ge(sem("u_done"), i + 1)
                pe.wait_ge(sem("turn_c"), 3 * i + 3)
                for c2 in range(2):
                    for t in range(2):
                        q = 2 * c2 + t
                        pe.wait_ge(sem("st"), 4 * i + 2 * c2)
                        pe.matmul(ps[:, 4 + t, 0:P], KR[:, q, 0, :], ST[:, t, :], start=True, stop=False)
                        pe.matmul(ps[:, 4 + t, 0:P], MK[:, q, 0, :], VT[:, q, :], start=False, stop=True
                                  ).then_inc(sem("xx"), 1)
                        pe.wait_ge(sem("y_ev"), 4 * i + 2 * c2)
                        pe.matmul(ps[:, 6 + t, 0:P], ST[:, t, :], KR[:, q, 1, :], start=True, stop=False)
                        pe.matmul(ps[:, 6 + t, 0:P], VT[:, q, :], MK[:, q, 1, :], start=False, stop=False)
                    filler()
                    for t in range(2):
                        q = 2 * c2 + t
                        pe.wait_ge(sem("xn"), 4 * i + 2 * c2 + t + 1)
                        pe.matmul(ps[:, 4 + t, P:2 * P], U[:, q, :], XN[:, t, :], start=True, stop=True
                                  ).then_inc(sem("sa"), 1)
                    filler()
                    for t in range(2):
                        q = 2 * c2 + t
                        pe.wait_ge(sem("sac"), 4 * i + 2 * c2 + t + 1)
                        pe.matmul(ps[:, 4 + t, 2 * P:3 * P], BTT[:, q, :], SA[:, t, :], start=True, stop=False)
                        pe.matmul(ps[:, 4 + t, 2 * P:3 * P], KTT[:, q, :], VT[:, q, :], start=False, stop=False)
                        pe.matmul(ps[:, 4 + t, 2 * P:3 * P], ident, ST[:, t, :], start=False, stop=True
                                  ).then_inc(sem("ss"), 1)
                        pe.matmul(ps[:, 6 + t, 0:P], SA[:, t, :], BM[:, q, 1, :], start=False, stop=True
                                  ).then_inc(sem("yy"), 1)
                    filler()
                filler()
                pe.wait_ge(sem("xc"), i + 1)
                for hh in range(4):
                    mm = pe.matmul(ps[:, 3, hh * P:(hh + 1) * P], bc(DAI[:, hh:hh + 1], [P, P]), tri, start=True, stop=True)
                mm.then_inc(sem("s1"), 1)
                pe.wait_ge(sem("st"), 4 * i + 4)
                pe.matmul(ps[:, 4, 0:4], tri, DAI, start=True, stop=True)
                for g in range(2):
                    mm = pe.matmul(ps[:, 4, P + g * P:2 * P + g * P], XC[:, 2 + g, :], XC[:, 4 + g, :], start=True, stop=True)
                mm.then_inc(sem("s1"), 1)
                pe.wait_ge(sem("st"), 4 * i + 4)
                for g in range(2):
                    mm = pe.transpose(ps[:, 5, g * P:(g + 1) * P], XC[:, g, :], ident)
                mm.then_inc(sem("s1"), 1)
                pe.wait_ge(sem("y_ev"), 4 * i + 4)
                for g in range(2):
                    mm = pe.transpose(ps[:, 6, g * P:(g + 1) * P], XC[:, 2 + g, :], ident)
                mm.then_inc(sem("s1"), 1)
                filler(3)
                pe.wait_ge(sem("sl"), i + 1)
                pe.wait_ge(sem("btok"), i + 1)
                pe.wait_ge(sem("y_ev"), 4 * i + 4)
                for hh in range(4):
                    g, o = hh // 2, 64 * (hh % 2)
                    pe.matmul(ps[o:o + 64, 7, g * P:(g + 1) * P], XDT[:, g, o:o + 64], EE[:, hh, :], start=True, stop=False)
                    mm = pe.matmul(ps[o:o + 64, 7, g * P:(g + 1) * P], HT[:, g, o:o + 64], EA[:, hh, :], start=False, stop=True)
                mm.then_inc(sem("sy"), 1)
                for g in range(2):
                    mm = pe.matmul(ps[:, 3, g * P:(g + 1) * P], BTOK[:, g, :], XTE[:, g, :], start=True, stop=True)
                mm.then_inc(sem("sh"), 1)
                filler(len(fill))

            pe.wait_ge(sem("ssm_fin"), 2 * NITER)
            pe.wait_ge(sem("y_ev"), 4 * NITER)
            pe.wait_ge(sem("evac"), 3 * N_BR0)
            for t in range(2):
                for c in range(NCH):
                    mm = pe.matmul(ps[:, 3 * t + c, 0:CW], bones, row(S_R + t, c * CW, (c + 1) * CW), start=True, stop=True)
                mm.then_inc(sem("gn_mean"), 1)
            pe.wait_ge(sem("gn_ctr"), 1)
            for c in range(NCH):
                for t in range(2):
                    mm = pe.matmul(ps[:, c, 0:CW], ones, row(S_CG + t, c * CW, (c + 1) * CW), start=t == 0, stop=t == 1)
            mm.then_inc(sem("ln_mean"), 1)
            pe.wait_ge(sem("gn_ctr"), 2)
            pe.wait_ge(sem("sm_sq"), 2)
            for c in range(NCH):
                for t in range(2):
                    mm = pe.matmul(ps[:, 3 + c, 0:CW], ones, V5[:, t, chunk(c)], start=t == 0, stop=t == 1)
            mm.then_inc(sem("sm_sum"), 1)
            pe.wait_ge(sem("gn_sq"), 2)
            pe.wait_ge(sem("ln_ctr"), 2)
            for t in range(2):
                if t == 1:
                    pe.wait_ge(sem("sm_var"), 1)
                for c in range(NCH):
                    mm = pe.matmul(ps[:, 3 * t + c, 0:CW], bones, V2[:, t, chunk(c)], start=True, stop=True)
                mm.then_inc(sem("gn_var"), 1)
            pe.wait_ge(sem("ln_sq"), 2)
            pe.wait_ge(sem("gn_v"), 1)
            for c in range(NCH):
                for t in range(2):
                    mm = pe.matmul(ps[:, c, 0:CW], ones, V4[:, t, chunk(c)], start=t == 0, stop=t == 1)
            mm.then_inc(sem("ln_var"), 1)
            for t in range(2):
                pe.wait_ge(sem("gn_v" if t == 0 else "ln_v"), 2 if t == 0 else 1)
                for c in range(NCH):
                    mm = pe.matmul(ps[:, 3 - 3 * t + c, 0:CW], lora_w[64:128, t * P:(t + 1) * P],
                                   PR[64:128, S_LORA, PAD + c * CW:PAD + (c + 1) * CW], start=True, stop=True)
                mm.then_inc(sem("g_mm"), 1)

            pe.wait_ge(sem("br_ready"), 4)
            for dt in range(KT):
                n = N_BR0 + dt
                pe.wait_ge(sem(f"w_in{n % 2}"), 16 * (n // 2 + 1))
                for b in range(BR):
                    for c in range(NCH):
                        m = 12 * dt + 3 * b + c
                        if m >= 6:
                            pe.wait_ge(sem("up_ev"), m - 5)
                        for k in range(2):
                            mm = pe.matmul(ps[:, m % 6, 0:CW], wring[:, n % 2, 2 * b + k, :],
                                           row(2 * b + k, c * CW, (c + 1) * CW), start=k == 0, stop=k == 1)
                        mm.then_inc(sem("up_mm"), 1)
            pe.wait_ge(sem("merged"), KT * 3)
            for dt in range(KT):
                n = N_OUT0 + dt
                pe.wait_ge(sem(f"w_in{n % 2}"), 16 * (n // 2 + 1))
                for c in range(NCH):
                    m = 3 * dt + c
                    if m >= 3:
                        pe.wait_ge(sem("out_ev"), m - 2)
                    for k in range(KT):
                        mm = pe.matmul(ps[:, c, 0:CW], wring[:, n % 2, k, :], H[:, k, chunk(c)], start=k == 0, stop=k == KT - 1)
                    mm.then_inc(sem("out_mm"), 1)
            pe.wait_ge(sem("out_ev"), 24)
            norm_sums("ffn")
            pe.wait_ge(sem("h2_ready"), KT)
            for n in range(9):
                m = P if n < 8 else NSMP
                for k in range(KT):
                    mm = pe.matmul(ps[0:m, 3, 20 * n:20 * n + 20], H[:, k, n * P:n * P + m], w_r[:, k, :], start=k == 0,
                                   stop=k == KT - 1)
            mm.then_inc(sem("r_mm"), 1)
            pe.wait_ge(sem("gates"), 1)
            for n in range(9):
                m = P if n < 8 else NSMP
                mm = pe.transpose(ps[0:NE, 4 + n // 4, (n % 4) * P:(n % 4) * P + m],
                                  GK16[0:m, n, :, :].rearrange("p a b -> p (a b)"), ident[0:m, 0:m])
            mm.then_inc(sem("gates_t"), 1)
            pe.wait_ge(sem("gates_c"), 3)
            with pe.Fori(0, NE // 2) as j:
                for s in range(2):
                    pe.wait_ge(sem("selc"), 2 * j + s + 1)
                    pe.wait_ge(sem(f"gu_in{s}"), 16 * j + 16)
                    for c in range(NCH):
                        pe.wait_ge(sem("gb_ev"), 6 * j + 3 * s + c)
                        pe.matmul(ps[:, 7, 0:CW], bc(SELC[:, s:s + 1], [NE, P]), GT[:, chunk(c)], start=True, stop=True
                                  ).then_inc(sem("gb_mm"), 1)
                        for hh in range(2):
                            m = 6 * s + 2 * c + hh
                            pe.wait_ge(sem("act"), 12 * j + m + 1)
                            for part in range(2):
                                for k in range(KT):
                                    mm = pe.matmul(ps[:, 2 * part + m % 2, 0:CW], GU[s][:, k, (2 * part + hh) * P:(2 * part + hh + 1) * P],
                                                   H[:, k, chunk(c)], start=k == 0, stop=k == KT - 1)
                                mm.then_inc(sem("gu_mm"), 1)
                    pe.wait_ge(sem(f"dn_in{s}"), 16 * j + 16)
                    for c in range(NCH):
                        pe.wait_ge(sem("act"), 12 * j + 6 * s + 2 * c + 2 + 2)
                        for dt in range(KT):
                            m = 8 * c + dt
                            pe.wait_ge(sem("down_ev"), 48 * j + 24 * s + m + 1)
                            for k in range(2):
                                mm = pe.matmul(ps[:, 4 + m % 3, 0:CW], DN[s][:, k, dt * P:(dt + 1) * P],
                                               ACTB[s][:, k, chunk(c)], start=k == 0, stop=k == 1)
                            mm.then_inc(sem("down_mm"), 1)
            pe.wait_ge(sem("act"), 12 * (NE // 2) + 2)
            norm_sums("fin")

        @block.scalar
        def _(act):
            A = nc.scalar.activation

            def norm_act(tag):
                for k in range(KT):
                    if k >= 2:
                        act.wait_ge(sem("norm_sum"), KT * NORMS[tag][1] + k - 1)
                    if tag == "mix" and k % 4 == 0:
                        act.wait_ge(sem(f"x_in{k // 4}"), 16)
                    if tag == "fin":
                        act.wait_ge(sem("down_ev"), 3 + 24 * NE)
                    A(NORMS[tag][0][:, k % 2, :], xk(tag, k), ACT.Square).then_inc(sem("norm_sq"), 1)
                rs = RS if tag != "mix" else RS0
                act.wait_ge(sem("norm_var"), NORMS[tag][1] + 1)
                A(rs, rs, ACT.Sqrt).then_inc(sem("norm_std"), 1)

            norm_act("mix")

            def evac(n, m):
                for c in range(NCH):
                    act.wait_ge(sem("dense"), m + c + 1)
                    act.wait_ge(sem("small_in"), 16)
                    A(PR[:, bass.ds(n, 1), PAD + c * CW:PAD + (c + 1) * CW], ps[:, c, 0:CW].unsqueeze(1), ACT.Copy
                      ).then_inc(sem("evac"), 1)

            evac(S_R, 0)
            with act.Fori(0, 3) as j:
                evac(2 * j + S_R + 1, 6 * j + 3)
                evac(2 * j + S_R + 2, 6 * j + 6)
            with act.Fori(3, 6) as j:
                evac(2 * j - 6, 6 * j + 3)
                evac(2 * j - 5, 6 * j + 6)
            act.wait_ge(sem("lerp"), 7)
            A(PR[0:32, S_LORA, PAD:], PR[0:32, S_LORA, PAD:], ACT.Tanh).then_inc(sem("lora_act"), 1)
            A(PR[64:128, S_LORA, PAD:], PR[64:128, S_LORA, PAD:], ACT.Sigmoid).then_inc(sem("lora_act"), 1)
            for t in range(2):
                A(TM[:, t, :], row(S_K + t), ACT.Square, scale=v("kkw", t)).then_inc(sem("k_sq"), 1)
            for t in range(2):
                act.wait_ge(sem("evac"), 39)
                A(row(S_CG + t), row(S_CG + t), ACT.Sigmoid).then_inc(sem("glu"), 1)
            for n in range(4):
                act.wait_ge(sem("lora_mm"), n + 1)
                dst, b = ((SG, "w0"), (AA, "a0"))[n // 2]
                A(as3(dst[:, n % 2, :]), ps3(3), ACT.Sigmoid, bias=v(b, n % 2)).then_inc(sem("lora_ev"), 1)
            for t in range(2):
                act.wait_ge(sem("k_ss"), t + 1)
                A(LL[:, t, :], LL[:, t, :], ACT.Sqrt).then_inc(sem("k_std"), 1)
            with act.Fori(6, 10) as j:
                evac(2 * j - 6, 6 * j + 3)
                evac(2 * j - 5, 6 * j + 6)
            for t in range(2):
                act.wait_ge(sem("cum"), t + 1)
                act.wait_ge(sem("bonus"), 2)
                A(TM[:, t, 0:TP], LL[:, t, 0:TP], ACT.Exp, scale=-DECAY_SCALE).then_inc(sem("dec_p"), 1)
            A(smp[:, 5, :, :], smp[:, 5, :, :], ACT.Exp, scale=-DECAY_SCALE).then_inc(sem("smp_dec"), 1)
            for t in range(2):
                act.wait_ge(sem("dec_lm"), t + 1)
                A(SG[:, t, 0:TP], SG[:, t, 0:TP], ACT.Exp, scale=-DECAY_SCALE).then_inc(sem("dec_q"), 1)
                A(AA[:, t, 0:TP], LL[:, t, 0:TP], ACT.Exp, scale=DECAY_SCALE).then_inc(sem("dec_q"), 1)
            for t in range(2):
                act.wait_ge(sem("pool_mm"), t + 1)
                A(as3(row(S_POOL + t)), ps3(0), ACT.Copy, scale=v("pool_scale", t)).then_inc(sem("pool_ev"), 1)
            act.wait_ge(sem("dt_neg"), 1)
            A(da_t[:, :, :], da_t[:, :, :], ACT.Exp).then_inc(sem("dt_e"), 1)
            act.wait_ge(sem("dt_e"), 1)
            A(da_t[:, :, :], da_t[:, :, :], ACT.Ln, bias=1.0).then_inc(sem("dt_l"), 1)
            A(smallv[:, 0:4], v("a_log", 0, 4), ACT.Exp).then_inc(sem("a_exp"), 1)
            act.wait_ge(sem("xs_pre"), 1)
            A(XSS, XS, ACT.Sigmoid).then_inc(sem("xs_sig"), 1)
            act.wait_ge(sem("evac"), 3 * NSLOT)
            A(dsm[:, 8:10, 0:8], PR[:, S_Z:S_Z + 2, PAD + TP:PAD + T], ACT.Sigmoid).then_inc(sem("zs_sig"), 1)
            act.wait_ge(sem("dt_bcc"), 1)
            A(dsm[:, 2:4, 0:8], dsm[:, 2:4, 0:8], ACT.Exp).then_inc(sem("smp_da"), 1)

            act.wait_ge(sem("pre_done"), 1)
            with act.Fori(0, NITER) as i:
                fill = [(j, c) for j in range(4) for c in range(NCH)]
                done = [0]

                def filler(k=1):
                    for _ in range(k):
                        done[0] += 1
                        if done[0] % 2:
                            continue
                        j, c = fill.pop(0)
                        act.wait_ge(sem("dense"), 12 * i + 3 * NSLOT + 3 * j + c + 1)
                        act.wait_ge(sem(f"gate_out{c}"), 16 * (4 * i + j))
                        A(stage[:, c, :], ps[:, c, 0:CW], ACT.Sigmoid).then_inc(sem("evac"), 1)

                for w, src in enumerate((kk, PR)):
                    for h in range(2):
                        a = (kk[64 * h:64 * h + 64, :, bass.ds(i * SC, SC)] if w == 0 else
                             PR[64 * h:64 * h + 64, S_R:S_R + 2, bass.ds(i * SC + PAD, SC)])
                        ins_ = A(KR[64 * h:64 * h + 64, :, w, 64 * h:64 * h + 64].rearrange("p (c t) j -> p c t j", c=2),
                                 a.rearrange("p t (c j) -> p c t j", c=2), ACT.Copy)
                ins_.then_inc(sem("kr"), 1)
                act.wait_ge(sem("prod"), 5 * i + 1)
                A(NL.rearrange("p a b -> p (a b)"), ps[:, 3, :], ACT.Copy).then_inc(sem("nl"), 1)
                filler()
                for n, dst in enumerate((VT, BTT, KTT)):
                    act.wait_ge(sem("turned"), 3 * i + n + 1)
                    A(dst.rearrange("p a b -> p (a b)"), ps[:, 3 + n, :], ACT.Copy).then_inc(sem("turn_c"), 1)
                filler()
                for l in range(5):
                    act.wait_ge(sem("x1"), 5 * i + l + 1)
                    A(X1.rearrange("p a b -> p (a b)"), ps[:, 6, :], ACT.Copy).then_inc(sem("x1c"), 1)
                    filler(2)
                for c2 in range(2):
                    filler(2)
                    for t in range(2):
                        act.wait_ge(sem("yy"), 4 * i + 2 * c2 + t + 1)
                        A(tick[:, 2 * c2 + t:2 * c2 + t + 1], cst[:, 0:1], ACT.Copy)
                        for h in range(2):
                            ins_ = A(PR[64 * h:64 * h + 64, S_R + t:S_R + t + 1, bass.ds(i * SC + c2 * RC + PAD, RC)],
                                     ps[64 * h:64 * h + 64, 6 + t:7 + t, 64 * h:64 * h + 64], ACT.Copy)
                        ins_.then_inc(sem("y_ev"), 1)
                    filler()
                act.wait_ge(sem("xc_raw"), i + 1)
                A(SX, XC, ACT.Sigmoid).then_inc(sem("sx"), 1)
                A(SZ, PR[:, S_Z:S_Z + 2, bass.ds(i * SC + PAD, SC)], ACT.Sigmoid).then_inc(sem("sx"), 1)
                filler()
                act.wait_ge(sem("s1"), 4 * i + 1)
                A(ACB.rearrange("p a b -> p (a b)"), ps[:, 3, :], ACT.Copy).then_inc(sem("acb"), 1)
                act.wait_ge(sem("s1"), 4 * i + 4)
                A(BTOK.rearrange("p a b -> p (a b)"), ps[:, 6, 0:2 * P], ACT.Copy).then_inc(sem("btok"), 1)
                act.wait_ge(sem("acb"), i + 1)
                A(EA, ACB, ACT.Exp).then_inc(sem("ea"), 1)
                act.wait_ge(sem("seg"), i + 1)
                A(EE, EE, ACT.Exp).then_inc(sem("ea"), 1)
                A(TE, TE, ACT.Exp).then_inc(sem("ea"), 1)
                filler(24 - done[0])

            act.wait_ge(sem("st_out"), 32)
            for t in range(2):
                A(V5[:, t, :], row(S_Z + t), ACT.Square).then_inc(sem("sm_sq"), 1)
            for t in range(2):
                act.wait_ge(sem("gn_ctr"), t + 1)
                A(V2[:, t, :], V1[:, t, :], ACT.Square).then_inc(sem("gn_sq"), 1)
            for t in range(2):
                act.wait_ge(sem("ln_ctr"), t + 1)
                A(V4[:, t, :], V3[:, t, :], ACT.Square).then_inc(sem("ln_sq"), 1)
            act.wait_ge(sem("sm_var"), 1)
            A(V5[:, 0, :], V5[:, 0, :], ACT.Sqrt).then_inc(sem("sm_std"), 1)
            for t in range(2):
                act.wait_ge(sem("gn_v"), t + 1)
                A(V2[:, t, :], V2[:, t, :], ACT.Sqrt).then_inc(sem("gn_std"), 1)
            act.wait_ge(sem("ln_v"), 1)
            A(V4[:, 0, :], V4[:, 0, :], ACT.Sqrt).then_inc(sem("ln_std"), 1)
            act.wait_ge(sem("ln_aff"), 2)
            for t in range(2):
                A(V4[:, t, :], V3[:, t, :], ACT.Sigmoid).then_inc(sem("ln_sig"), 1)
            act.wait_ge(sem("out_ev"), 24)
            norm_act("ffn")
            act.wait_ge(sem("r_pre"), 1)
            A(q4[2], q4[2], ACT.Exp).then_inc(sem("r_exp"), 1)
            act.wait_ge(sem("r_pre"), 2)
            A(q1[4], q1[4], ACT.Exp).then_inc(sem("r_exp"), 1)
            act.wait_ge(sem("gates_t"), 1)
            for b in range(3):
                w = 512 if b < 2 else NSMP
                A(GT[:, 512 * b:512 * b + w], ps[0:NE, 4 + b, 0:w], ACT.Copy).then_inc(sem("gates_c"), 1)
            with act.Fori(0, NE // 2) as j:
                for s in range(2):
                    for c in range(NCH):
                        act.wait_ge(sem("gb_mm"), 6 * j + 3 * s + c + 1)
                        A(GBC[s][:, chunk(c)], ps[:, 7, 0:CW], ACT.Copy).then_inc(sem("gb_ev"), 1)
                        for hh in range(2):
                            m = 6 * s + 2 * c + hh
                            act.wait_ge(sem("gu_mm"), 2 * (12 * j + m) + 1)
                            A(SIL[:, m % 2, :], ps[:, m % 2, 0:CW], ACT.Silu).then_inc(sem("silu"), 1)
            norm_act("fin")


        @block.vector
        def _(dve):
            link = Link(dve, sem("dve_self"))
            tt, ts, stt = nc.vector.tensor_tensor, nc.vector.tensor_scalar, nc.vector.scalar_tensor_tensor
            MUL, ADD, SUB, MAX, MIN, EQ = ALU.mult, ALU.add, ALU.subtract, ALU.max, ALU.min, ALU.is_equal

            def norm_apply(tag, gain, out, done):
                rs = RS if tag != "mix" else RS0
                dve.wait_ge(sem("norm_sum"), KT * (NORMS[tag][1] + 1))
                ts(as3(rs), ps3(0), 1.0 / D, NORM_EPS, MUL, ADD).then_inc(sem("norm_var"), 1)
                dve.wait_ge(sem("norm_std"), NORMS[tag][1] + 1)
                link(nc.vector.reciprocal(rs, rs))
                for k in range(KT):
                    ins_ = stt(out(k), xk(tag, k), v(gain, k), rs, MUL, MUL)
                    done(ins_, k)

            dve.wait_ge(sem("small_in"), 16 * NSMALL_IN)
            norm_apply("mix", "g_mix", lambda k: H[:, k, :], lambda x, k: x.then_inc(sem("h_ready"), 1) if k == KT - 1 else None)
            ts(smallv[:, 4:6], v("ka", 0, 2), -1.0, 1.0, MUL, ADD)

            dve.wait_ge(sem("evac"), 21)
            dve.wait_ge(sem("pads"), 1)
            dve.wait_ge(sem("h_ready"), 1)
            nc.vector.tensor_copy(shift_out[:, :, :], PR[:, S_R:S_R + 7, PAD + TP - 1:]).then_inc(sem("shift_saved"), 1)
            dve.wait_ge(sem("shift_saved"), 1)
            for t in range(7):
                s = S_R + t
                tt(TM[:, t % 2, 0:TP], PR[:, s, PAD - 1:PAD + TP - 1], row(s, 0, TP), SUB)
                link(tt(TM[:, t % 2, TP:T], shift_in[:, t, :], row(s, TP, T), SUB))
                stt(row(s), TM[:, t % 2, :], v("mu", t), row(s), MUL, ADD).then_inc(sem("lerp"), 1)
            dve.wait_ge(sem("lerp"), 7)
            for t in range(2):
                dve.wait_ge(sem("k_sum"), t + 1)
                ts(as3(LL[:, t, :]), ps3(3), 1e-24, None, MAX).then_inc(sem("k_ss"), 1)
            for t in range(2):
                dve.wait_ge(sem("k_std"), t + 1)
                link(nc.vector.reciprocal(LL[:, t, :], LL[:, t, :]))
                stt(kk[:, t, :], row(S_K + t, 0, TP), v("kkw", t), LL[:, t, 0:TP], MUL, MUL)
                stt(smp[:, 3, t, :], row(S_K + t, TP, T), v("kkw", t), LL[:, t, TP:T], MUL, MUL)
            dve.wait_ge(sem("lora_ev"), 4)
            link(nc.vector.tensor_copy(smp[:, 5, :, :], SG[:, :, TP:T]))
            for t in range(2):
                tt(bb[:, t, :], kk[:, t, :], AA[:, t, 0:TP], MUL)
                link(tt(smp[:, 4, t, :], smp[:, 3, t, :], AA[:, t, TP:T], MUL))
                link(ts(AA[:, t, :], AA[:, t, :], v("ka", t), smallv[:, 4 + t:5 + t], MUL, ADD))
                link(tt(row(S_K + t), row(S_K + t), AA[:, t, :], MUL))
                stt(TM[:, t, :], row(S_R + t), v("rk", t), row(S_K + t), MUL, MUL).then_inc(sem("rk_prod"), 1)
            nc.vector.tensor_copy(smp[:, 0:3, :, :], rows(S_R, 6, TP, T).rearrange("p (a b) c -> p a b c", a=3))
            dve.wait_ge(sem("reset"), 1)
            for t in range(2):
                nc.vector.tensor_tensor_scan(LL[:, t, 0:TP], RESET, SG[:, t, 0:TP], 0.0, MUL, ADD).then_inc(sem("cum"), 1)
            dve.wait_ge(sem("cum"), 2)
            dve.wait_ge(sem("glu"), 2)
            for t in range(2):
                tt(row(S_CA + t), row(S_CA + t), row(S_CG + t), MUL).then_inc(sem("c_ready"), 1)
            dve.wait_ge(sem("c_ready"), 2)
            link(nc.vector.tensor_copy(conv_h[:, :, :, CONVK - 1], rows(S_CA, 2, TP, T)))
            for t in range(2):
                link(tt(CHW, conv_h[:, t, :, :], mid(v("conv_w", t * CONVK, CONVK), NSMP), MUL))
                link(nc.vector.tensor_reduce(row(S_CG + t, TP, T), CHW, AX, ADD))
                link(ts(row(S_CG + t, TP, T), row(S_CG + t, TP, T), v("conv_b", t), None, ADD))
            for j in range(CONVK):
                for t in range(2):
                    w = v("conv_w", t * CONVK + j)
                    src, dst = PR[:, S_CA + t, j:j + TP], row(S_CG + t, 0, TP)
                    ins_ = ts(dst, src, w, v("conv_b", t), MUL, ADD) if j == 0 else stt(dst, src, w, dst, MUL, ADD)
                link(ins_)
            dve.wait_ge(sem("c_out"), 16)
            for t in range(2):
                dve.wait_ge(sem("rk_sum"), t + 1)
                tt(as3(row(S_CA + t)), ps3(3), as3(row(S_V + t)), MUL).then_inc(sem("bonus"), 1)
            for t in range(2):
                tt(SG[:, t, 0:TP], LL[:, t, 0:TP], SG[:, t, 0:TP], SUB).then_inc(sem("dec_lm"), 1)
            for t in range(2):
                dve.wait_ge(sem("dec_p"), t + 1)
                tt(row(S_R + t, 0, TP), row(S_R + t, 0, TP), TM[:, t, 0:TP], MUL)
                nc.vector.tensor_copy(pc[:, t, :], TM[:, t, RC - 1:TP:RC])
            for t in range(2):
                dve.wait_ge(sem("dec_q"), 2 * t + 1)
                tt(kk[:, t, :], kk[:, t, :], SG[:, t, 0:TP], MUL)
                dve.wait_ge(sem("dec_q"), 2 * t + 2)
                tt(bb[:, t, :], bb[:, t, :], AA[:, t, 0:TP], MUL)
                tt(row(S_K + t, 0, TP), row(S_K + t, 0, TP), AA[:, t, 0:TP], MUL).then_inc(sem("rw_pre"), 1)
            dve.wait_ge(sem("rw_pre"), 2)
            dve.wait_ge(sem("pool_diff"), 2)

            link(nc.vector.memset(dt_t[:, :, :], 0.0))
            dve.wait_ge(sem("dt_mm"), 1)
            tt(dt_t[:, 0:8, :], ps[:, 6, 0:32].rearrange("p (a b) -> p a b", a=8), mid(v("dt_bias", 0, 4), 8), ADD)
            tt(dt_t[0:NSMP, 8, :], ps[0:NSMP, 6, 32:36], vec[0:NSMP, VEC["dt_bias"][0]:VEC["dt_bias"][0] + 4], ADD
               ).then_inc(sem("dt_read"), 1)
            dve.wait_ge(sem("dt_read"), 1)
            stt(da_t[:, :, :], dt_t[:, :, :], -1.0, dt_t[:, :, :], MUL, MIN).then_inc(sem("dt_neg"), 1)
            nc.vector.tensor_copy(ssm_h[:, :, :, SSMK - 1], rows(S_XBC, 6, TP, T)).then_inc(sem("ssm_h"), 1)
            dve.wait_ge(sem("ssm_h"), 1)
            link(tt(XSW, ssm_h[:, :, :, :], v("ssm_w", 0, 24).rearrange("p (a b) -> p a b", a=6).unsqueeze(2).to_broadcast([P, 6, NSMP, SSMK]), MUL))
            link(nc.vector.tensor_reduce(XS, XSW, AX, ADD))
            tt(XS, XS, last(v("ssm_b", 0, 6), NSMP), ADD).then_inc(sem("xs_pre"), 1)

            dve.wait_ge(sem("smp_dec"), 1)
            im = cc("imask").unsqueeze(1).unsqueeze(1).to_broadcast([P, NSMP, 2, HD])

            def by_b(a):
                return a.rearrange("p t b -> p b t")

            def x_exp(n):
                if n >= 2:
                    dve.wait_ge(sem("x_bc"), n - 1)
                tt(XE[n % 2], last(by_b(smp[:, (3, 5, 4, 1, 0)[n], :, :]), HD), im, MUL).then_inc(sem("x_exp"), 1)

            def x_bc(n):
                dve.wait_ge(sem("x_bc"), n + 1)
                b = 3 + 2 * (n % 2)
                return ps[:, b:b + 2, :].rearrange("p a (b c d) -> p (a b) c d", b=4, c=2)

            W = W2[:, 0:4, :, :].rearrange("p a b (c d) -> p (a b c) d", c=2).rearrange("p (a b) d -> p a b d", b=2)
            sa_s = dsm[:, 10, :].rearrange("p (a b) -> p a b", b=2)
            dve.wait_ge(sem("states_in"), 32)
            x_exp(0)
            x_exp(1)
            link(tt(W, SW, x_bc(0), MUL))
            nc.vector.tensor_reduce(sa_s, W, AX, ADD).then_inc(sem("x_use"), 1)
            x_exp(2)
            tt(SW, SW, x_bc(1), MUL).then_inc(sem("x_use"), 1)
            x_exp(3)
            dve.wait_ge(sem("x_use"), 2)
            link(tt(W, x_bc(2), last(sa_s, HD), MUL))
            tt(SW, SW, W, SUB).then_inc(sem("x_use"), 1)
            x_exp(4)
            dve.wait_ge(sem("x_use"), 3)
            link(tt(W, x_bc(3), last(by_b(smp[:, 2, :, :]), HD), MUL))
            tt(SW, SW, W, ADD).then_inc(sem("x_use"), 1)
            dve.wait_ge(sem("x_use"), 4)
            tt(W, SW, x_bc(4), MUL).then_inc(sem("x_use"), 1)
            dve.wait_ge(sem("x_use"), 5)
            link(nc.vector.tensor_reduce(by_b(rows(S_R, 2, TP, T)), W, AX, ADD))

            dve.wait_ge(sem("xs_sig"), 1)
            link(tt(XS, XS, XSS, MUL))
            idn = ident.unsqueeze(1).unsqueeze(1).to_broadcast([P, NSMP, 2, P])
            tt(BE, last(by_b(XS[:, 2:4, :]), P), idn, MUL).then_inc(sem("bc_exp"), 1)
            dve.wait_ge(sem("dt_l"), 1)
            link(stt(dt_t[:, :, :], dt_t[:, :, :], 0.0, da_t[:, :, :], MAX, ADD))
            dve.wait_ge(sem("a_exp"), 1)
            stt(da_t[:, :, :], dt_t[:, :, :], -1.0, mid(smallv[:, 0:4], 9), MUL, MUL).then_inc(sem("dta"), 1)
            dve.wait_ge(sem("dt_bc"), 1)
            for q in range(2):
                for h in range(2):
                    src = ps[64 * h:64 * h + 64, 7, 32 * q:32 * q + 32].rearrange("p (g h b) -> p h g b", g=2, h=2)[:, h, :, :]
                    ins_ = nc.vector.tensor_copy(dsm[64 * h:64 * h + 64, 2 * q:2 * q + 2, 0:8], src)
            ins_.then_inc(sem("dt_bcc"), 1)
            dve.wait_ge(sem("dt_bcc"), 1)
            link(tt(dsm[:, 4:6, 0:8], dsm[:, 0:2, 0:8], XS[:, 0:2, :], MUL))
            dve.wait_ge(sem("smp_da"), 1)
            link(tt(SH, SH, last(by_b(dsm[:, 2:4, 0:8]), P), MUL))
            dve.wait_ge(sem("bc_bc"), 1)
            spread = ps[:, 0:4, :].rearrange("p a (b c d) -> p (a b) c d", b=2, c=2)
            link(tt(W2, spread, last(by_b(dsm[:, 4:6, 0:8]), P), MUL))
            tt(BE, last(by_b(XS[:, 4:6, :]), P), idn, MUL).then_inc(sem("bc_exp"), 1)
            link(tt(SH, SH, W2, ADD))
            dve.wait_ge(sem("bc_bc"), 2)
            link(tt(W2, SH, spread, MUL))
            link(nc.vector.tensor_reduce(by_b(dsm[:, 6:8, 0:8]), W2, AX, ADD))
            for g in range(2):
                link(stt(dsm[:, 6 + g, 0:8], XS[:, g, :], v("ssm_d", g), dsm[:, 6 + g, 0:8], MUL, ADD))
            dve.wait_ge(sem("zs_sig"), 1)
            link(tt(dsm[:, 6:8, 0:8], dsm[:, 6:8, 0:8], rows(S_Z, 2, TP, T), MUL))
            tt(rows(S_Z, 2, TP, T), dsm[:, 6:8, 0:8], dsm[:, 8:10, 0:8], MUL).then_inc(sem("smp_done"), 1)
            dve.wait_ge(sem("s_out"), 32)
            nc.vector.memset(scr[:, 0:2560], 0.0)
            nc.vector.memset(ST, 0.0)
            nc.vector.memset(HT, 0.0).then_inc(sem("pre_done"), 1)
            dve.wait_ge(sem("pre_done"), 1)

            with dve.Fori(0, NITER) as i:
                link.enter(i, PER_TURN)
                nc.vector.tensor_copy(PCS, pc[:, :, bass.ds(2 * i, 2)])
                nc.vector.tensor_copy(DTI, dt_t[:, bass.ds(i, 1), :].rearrange("p a b -> p (a b)"))
                nc.vector.tensor_copy(DAI, da_t[:, bass.ds(i, 1), :].rearrange("p a b -> p (a b)"))
                for n in range(4):
                    dve.wait_ge(sem("prod"), 5 * i + 2 + n)
                    m = cc("m_lev1_incl" if n < 2 else "m_strict_incl")
                    dst = (BM, MK)[n // 2][:, 2 * (n % 2):2 * (n % 2) + 2, :, :].rearrange("p a b c -> p a (b c)")
                    tt(dst, ps[:, 4 + n, :].rearrange("p (a b) -> p a b", a=2), mid(m, 2), MUL).then_inc(sem("masked"), 1)
                dve.wait_ge(sem("nl"), i + 1)
                link(tt(TT, NL, mid(cc("m_lev1_low"), 4), MUL))
                tt(TT, TT, mid(ident, 4), ADD)
                tt(U, BM[:, :, 0, :], mid(ident, 4), ADD)
                tt(NLB, NL, mid(cc("m_lev_low", 0, P), 4), MUL).then_inc(sem("lev"), 1)
                for l in range(5):
                    dve.wait_ge(sem("du"), 5 * i + l + 1)
                    ins_ = tt(U, U, ps[:, 7, :].rearrange("p (a b) -> p a b", a=4), SUB)
                    if l < 4:
                        dve.wait_ge(sem("dt_"), 4 * i + l + 1)
                        tt(TT, TT, ps[:, 3, :].rearrange("p (a b) -> p a b", a=4), SUB)
                        tt(NLB, NL, mid(cc("m_lev_low", (l + 1) * P, P), 4), MUL).then_inc(sem("lev"), 1)
                    else:
                        ins_.then_inc(sem("u_done"), 1)
                for c2 in range(2):
                    for t in range(2):
                        dve.wait_ge(sem("xx"), 4 * i + 2 * c2 + t + 1)
                        ts(XN[:, t, :], ps[:, 4 + t, 0:P], -1.0, None, MUL).then_inc(sem("xn"), 1)
                    for t in range(2):
                        dve.wait_ge(sem("sa"), 4 * i + 2 * c2 + t + 1)
                        nc.vector.tensor_copy(SA[:, t, :], ps[:, 4 + t, P:2 * P]).then_inc(sem("sac"), 1)
                    for t in range(2):
                        dve.wait_ge(sem("ss"), 4 * i + 2 * c2 + t + 1)
                        ts(ST[:, t, :], ps[:, 4 + t, 2 * P:3 * P], PCS[:, t, c2:c2 + 1], None, MUL).then_inc(sem("st"), 1)
                for j in range(SSMK):
                    for t in range(6):
                        w = v("ssm_w", t * SSMK + j)
                        src = PR[:, S_XBC + t, bass.ds(i * SC + PAD - (SSMK - 1) + j, SC)]
                        ins_ = (ts(XC[:, t, :], src, w, v("ssm_b", t), MUL, ADD) if j == 0 else
                                stt(XC[:, t, :], src, w, XC[:, t, :], MUL, ADD))
                    if j < SSMK - 1:
                        link(ins_)
                ins_.then_inc(sem("xc_raw"), 1)
                dve.wait_ge(sem("xc_raw"), i + 1)
                dve.wait_ge(sem("sx"), 2 * i + 1)
                tt(XC, XC, SX, MUL).then_inc(sem("xc"), 1)
                dve.wait_ge(sem("s1"), 4 * i + 2)
                nc.vector.tensor_copy(AT, ps[:, 4, 0:4])
                link(tt(GM, ps[:, 4, P:3 * P].rearrange("p (a b) -> p a b", a=2), mid(tri, 2), MUL))
                dve.wait_ge(sem("acb"), i + 1)
                for hh in range(4):
                    ts(EE[:, hh, :], ACB[:, hh, :], AT[:, hh:hh + 1], 0.0, SUB, MIN)
                tt(TE, ACB[:, :, SC - 1], AT, SUB).then_inc(sem("seg"), 1)
                dve.wait_ge(sem("s1"), 4 * i + 3)
                link(tt(XDT.rearrange("p a (b c) -> p (a b) c", b=2), ps[:, 5, 0:2 * P].rearrange("p (a b) -> p a b", a=4),
                        last(DTI, HD), MUL))
                dve.wait_ge(sem("ea"), 3 * i + 1)
                link(nc.vector.tensor_copy(DEC, EA[:, :, SC - 1]))
                cb = XC[:, 4:6, :].unsqueeze(2).to_broadcast([P, 2, 2, SC])
                tt(EA.rearrange("p (a b) c -> p a b c", a=2), EA.rearrange("p (a b) c -> p a b c", a=2), cb, MUL)
                dve.wait_ge(sem("ea"), 3 * i + 3)
                gmb = GM.unsqueeze(2).to_broadcast([P, 2, 2, SC])
                tt(EE.rearrange("p (a b) c -> p a b c", a=2), EE.rearrange("p (a b) c -> p a b c", a=2), gmb, MUL)
                tt(XTE.rearrange("p a (b c) -> p (a b) c", b=2), XDT.rearrange("p a (b c) -> p (a b) c", b=2), last(TE, HD), MUL
                   ).then_inc(sem("sl"), 1)
                dve.wait_ge(sem("sy"), i + 1)
                for g in range(2):
                    ins_ = stt(XC[:, g, :], XC[:, g, :], v("ssm_d", g), ps[:, 7, g * P:(g + 1) * P], MUL, ADD)
                link(ins_)
                zc = PR[:, S_Z:S_Z + 2, bass.ds(i * SC + PAD, SC)]
                link(tt(XC[:, 0:2, :], XC[:, 0:2, :], zc, MUL))
                dve.wait_ge(sem("sx"), 2 * i + 2)
                tt(zc, XC[:, 0:2, :], SZ, MUL).then_inc(sem("ssm_fin"), 1)
                dve.wait_ge(sem("sh"), i + 1)
                for hh in range(4):
                    hv = HT[:, hh // 2, 64 * (hh % 2):64 * (hh % 2) + 64]
                    ins_ = stt(hv, hv, DEC[:, hh:hh + 1], ps[:, 3, 64 * hh:64 * hh + 64], MUL, ADD)
                ins_.then_inc(sem("ssm_fin"), 1)
                dve.wait_ge(sem("ssm_fin"), 2 * i + 2)
            link.leave(NITER)

            dve.wait_ge(sem("st_out"), 32)
            for t in range(2):
                dve.wait_ge(sem("gn_mean"), t + 1)
                stt(as3(V1[:, t, :]), ps3(3 * t), -1.0 / HD, as3(row(S_R + t)), MUL, ADD).then_inc(sem("gn_ctr"), 1)
            dve.wait_ge(sem("ln_mean"), 1)
            for t in range(2):
                stt(as3(V3[:, t, :]), ps3(0), -1.0 / (2 * P), as3(row(S_CG + t)), MUL, ADD).then_inc(sem("ln_ctr"), 1)
            dve.wait_ge(sem("sm_sum"), 1)
            ts(as3(V5[:, 0, :]), ps3(3), 1.0 / (2 * P), NORM_EPS, MUL, ADD).then_inc(sem("sm_var"), 1)
            for t in range(2):
                dve.wait_ge(sem("gn_var"), t + 1)
                ts(as3(V2[:, t, :]), ps3(3 * t), 1.0 / HD, GN_EPS, MUL, ADD).then_inc(sem("gn_v"), 1)
            dve.wait_ge(sem("ln_var"), 1)
            ts(as3(V4[:, 0, :]), ps3(0), 1.0 / (2 * P), LN_EPS, MUL, ADD).then_inc(sem("ln_v"), 1)
            dve.wait_ge(sem("sm_std"), 1)
            link(nc.vector.reciprocal(V5[:, 0, :], V5[:, 0, :]))
            for t in range(2):
                ins_ = stt(row(S_Z + t), row(S_Z + t), v("ssm_g", t), V5[:, 0, :], MUL, MUL)
            ins_.then_inc(sem("br_ready"), 1)
            dve.wait_ge(sem("ln_std"), 1)
            link(nc.vector.reciprocal(V4[:, 0, :], V4[:, 0, :]))
            for t in range(2):
                link(tt(V3[:, t, :], V3[:, t, :], V4[:, 0, :], MUL))
                ts(V3[:, t, :], V3[:, t, :], v("conv_ln_g", t), v("conv_ln_b", t), MUL, ADD).then_inc(sem("ln_aff"), 1)
            for t in range(2):
                link(nc.vector.reciprocal(V2[:, t, :], V2[:, t, :]))
                link(tt(V1[:, t, :], V1[:, t, :], V2[:, t, :], MUL))
                link(ts(V1[:, t, :], V1[:, t, :], v("ln_g", t), v("ln_b", t), MUL, ADD))
                link(tt(V1[:, t, :], V1[:, t, :], row(S_CA + t), ADD))
                dve.wait_ge(sem("g_mm"), t + 1)
                tt(as3(row(O_RWKV + t)), as3(V1[:, t, :]), ps3(3 - 3 * t), MUL).then_inc(sem("br_ready"), 1)
            dve.wait_ge(sem("ln_sig"), 2)
            for t in range(2):
                ins_ = tt(row(S_CG + t), V3[:, t, :], V4[:, t, :], MUL)
            ins_.then_inc(sem("br_ready"), 1)

            for dt in range(KT):
                if dt:
                    dve.wait_ge(sem("merged"), 3 * dt)
                dve.wait_ge(sem(f"gb_in{dt % 2}"), 16 * (dt // 2 + 1))
                for b in range(BR):
                    for c in range(NCH):
                        m = 12 * dt + 3 * b + c
                        dve.wait_ge(sem("up_mm"), m + 1)
                        dst = H[:, dt, chunk(c)]
                        gate = GB[dt % 2][:, b, chunk(c)]
                        if b == 0:
                            tt(dst, ps[:, m % 6, 0:CW], gate, MUL).then_inc(sem("up_ev"), 1)
                        else:
                            tt(GP[:, m % 2, :], ps[:, m % 6, 0:CW], gate, MUL).then_inc(sem("up_ev"), 1)
                            dve.wait_ge(sem("up_ev"), m + 1)
                            ins_ = tt(dst, dst, GP[:, m % 2, :], ADD)
                            if b == BR - 1:
                                ins_.then_inc(sem("merged"), 1)
            dve.wait_ge(sem("x_re"), 16)
            for dt in range(KT):
                for c in range(NCH):
                    m = 3 * dt + c
                    dve.wait_ge(sem("out_mm"), m + 1)
                    r_ = row(X2 + dt, c * CW, (c + 1) * CW)
                    tt(r_, ps[:, c, 0:CW], r_, ADD).then_inc(sem("out_ev"), 1)
            dve.wait_ge(sem("out_ev"), 24)
            norm_apply("ffn", "g_ffn", lambda k: H[:, k, :], lambda x, k: x.then_inc(sem("h2_ready"), 1))

            nc.vector.memset(GK16, 0.0).then_inc(sem("down_ev"), 3)
            nc.vector.memset(LG, 0.0).then_inc(sem("act"), 2)
            dve.wait_ge(sem("act"), 2)
            dve.wait_ge(sem("r_mm"), 1)
            rb = VEC["r_bias"][0]
            tt(LG[:, 0:8, :], ps[:, 3, 0:160].rearrange("p (a b) -> p a b", a=8), mid(vec[:, rb:rb + 20], 8), ADD)
            link(tt(LG[0:NSMP, 8, :], ps[0:NSMP, 3, 160:180], vec[0:NSMP, rb:rb + 20], ADD))
            GL = LG[:, :, 0:4]
            EL = LG[:, :, 4:20].rearrange("p n (g k) -> p n g k", g=4)
            rank = mid(cc("rank4"), 9)

            def first_max(dst, val, top, tmp, mx):
                link(nc.vector.tensor_reduce(top, val, AX, MAX))
                link(tt(tmp, val, last(top, 4), EQ))
                link(tt(tmp, tmp, rank, MUL))
                link(nc.vector.tensor_reduce(mx, tmp, AX, MAX))
                link(tt(dst, tmp, last(mx, 4), EQ))

            first_max(q4[0], GL, q1[0], q4[1], q1[1])
            tt(q4[2], GL, last(q1[0], 4), SUB).then_inc(sem("r_pre"), 1)
            link(tt(TE16, EL, last(q4[0], 4), MUL))
            link(nc.vector.tensor_reduce(q4[3], TE16.rearrange("p n g k -> p n k g"), AX, ADD))
            first_max(q4[4], q4[3], q1[2], q4[1], q1[1])
            link(stt(q4[3], q4[4], -3e38, q4[3], MUL, ADD))
            first_max(q4[5], q4[3], q1[3], q4[1], q1[1])
            tt(q1[4], q1[3], q1[2], SUB).then_inc(sem("r_pre"), 1)
            dve.wait_ge(sem("r_exp"), 2)
            link(nc.vector.tensor_reduce(q1[5], q4[2], AX, ADD))
            link(ts(q1[6], q1[4], 1.0, None, ADD))
            link(tt(q1[5], q1[5], q1[6], MUL))
            link(nc.vector.reciprocal(q1[5], q1[5]))
            link(tt(q1[6], q1[5], q1[4], MUL))
            link(tt(q4[4], q4[4], last(q1[5], 4), MUL))
            link(tt(q4[5], q4[5], last(q1[6], 4), MUL))
            link(tt(q4[4], q4[4], q4[5], ADD))
            tt(GK16, last(q4[0], 4), q4[4].unsqueeze(2).to_broadcast([P, 9, 4, 4]), MUL).then_inc(sem("gates"), 1)

            with dve.Fori(0, NE // 2) as j:
                link.enter(j, 12)
                for s in range(2):
                    nc.vector.tensor_copy(SELC[:, s:s + 1], cst[0:NE, bass.ds(2 * j + s, 1)]).then_inc(sem("selc"), 1)
                for s in range(2):
                    for c in range(NCH):
                        for hh in range(2):
                            m = 6 * s + 2 * c + hh
                            dve.wait_ge(sem("silu"), 12 * j + m + 1)
                            dve.wait_ge(sem("gu_mm"), 2 * (12 * j + m) + 2)
                            link(tt(SIL[:, m % 2, :], SIL[:, m % 2, :], ps[:, 2 + m % 2, 0:CW], MUL))
                            dve.wait_ge(sem("gb_ev"), 6 * j + 3 * s + c + 1)
                            tt(ACTB[s][:, hh, chunk(c)], SIL[:, m % 2, :], GBC[s][:, chunk(c)], MUL).then_inc(sem("act"), 1)
                    for c in range(NCH):
                        for dt in range(KT):
                            m = 8 * c + dt
                            dve.wait_ge(sem("down_mm"), 48 * j + 24 * s + m + 1)
                            r_ = row(X2 + dt, c * CW, (c + 1) * CW)
                            tt(r_, ps[:, 4 + m % 3, 0:CW], r_, ADD).then_inc(sem("down_ev"), 1)
                    dve.wait_ge(sem("down_ev"), 48 * j + 24 * s + 24 + 3)
            link.leave(NE // 2)
            norm_apply("fin", "g_fin", lambda k: H[:, k, :], lambda x, k: x.then_inc(sem("y_ready"), 1))

        @block.gpsimd
        def _(pool):
            link = Link(pool, sem("pool_self"))
            tt, ts = nc.gpsimd.tensor_tensor, nc.gpsimd.tensor_scalar
            for dst, name in ((vec, "vec"), (cst, "cst"), (lora_w, "lora_w"), (pool_w, "pool_w"), (w_dt, "w_dt"), (w_r, "w_r"),
                              (shift_in, "shift_in")):
                pool.dma_start(dst[:], ins[name]).then_inc(sem("small_in"), 16)
            for dst, name, n in ((pool_h, "pool_h", POOLH), (conv_h, "conv_h", CONVK - 1), (ssm_h, "ssm_h", SSMK - 1)):
                for t in range(dst.shape[1]):
                    pool.dma_start(dst[:, t, :, 0:n], ins[name][:, t, :, :]).then_inc(sem("small_in"), 16)
            nc.gpsimd.memset(PR[:, :, 0:PAD], 0.0).then_inc(sem("pads"), 1)

            pool.wait_ge(sem("h_ready"), 1)
            link(nc.gpsimd.memset(RESET, 1.0))
            nc.gpsimd.memset(RESET[:, 0:TP:RC], 0.0).then_inc(sem("reset"), 1)
            pool.wait_ge(sem("evac"), 27)
            pool.wait_ge(sem("small_in"), 16 * NSMALL_IN)
            pool.wait_ge(sem("pads"), 1)
            link(nc.gpsimd.tensor_copy(pool_tail[:, :, :], rows(S_POOL, 2, TP - POOLH, TP)))
            link(nc.gpsimd.tensor_copy(pool_h[:, :, :, POOLH], rows(S_POOL, 2, TP, T)))
            end = PAD + TP
            for t in range(2):
                u = PR[:, S_POOL + t, :]
                lo, hi = slice(0, 64), slice(64, 128)
                link(tt(PA[:, 14:end], u[:, 14:end], u[:, 13:end - 1], ALU.add))
                if t == 0:
                    link(tt(PB[hi, 16:end], PA[hi, 16:end], PA[hi, 14:end - 2], ALU.add))
                else:
                    link(tt(PB[:, 16:end], PA[:, 16:end], PA[:, 14:end - 2], ALU.add))
                    link(tt(PA[:, 20:end], PB[:, 20:end], PB[:, 16:end - 4], ALU.add))
                    link(tt(PB[hi, 28:end], PA[hi, 28:end], PA[hi, 20:end - 8], ALU.add))
                for q, src in ((lo, PA), (hi, PB)):
                    m = src[q, PAD:end]
                    head = src[q, PAD:PAD + 16]
                    o = CST["rcount"][0] + 16 * t
                    w = CST["rwin"][0] + t
                    link(ts(src[q, PAD + 16:end], src[q, PAD + 16:end], cst[q, w:w + 1], None, ALU.mult))
                    link(tt(head, head, cst[q, o:o + 16], ALU.mult))
                    link(tt(u[q, PAD:end], m, u[q, PAD:end], ALU.subtract))
                    n = (2, 4, 8, 16)[2 * t + (1 if q is hi else 0)]
                    link(nc.gpsimd.tensor_copy(dsum[q, :], pool_h[q, t, :, 16 - n]))
                    for k_ in range(17 - n, 16):
                        link(tt(dsum[q, :], dsum[q, :], pool_h[q, t, :, k_], ALU.add))
                    link(ts(dsum[q, :], dsum[q, :], cst[q, w:w + 1], None, ALU.mult))
                    ins_ = tt(u[q, end:], dsum[q, :], u[q, end:], ALU.subtract)
                    if q is lo:
                        link(ins_)
                    else:
                        ins_.then_inc(sem("pool_diff"), 1)
                        pool.wait_ge(sem("pool_diff"), t + 1)
            pool.wait_ge(sem("pool_diff"), 2)

            def out(name, src, name_sem="small_out"):
                pool.dma_start(outs[name], src).then_inc(sem(name_sem), 16)

            out("pool_tail", pool_tail[:, :, :])
            for t in range(2):
                pool.dma_start(outs["pool_h"][:, t], pool_h[:, t, :, 1:]).then_inc(sem("small_out"), 16)
            pool.wait_ge(sem("shift_saved"), 1)
            out("shift", shift_out[:, :, :])
            pool.wait_ge(sem("c_ready"), 2)
            out("conv_tail", rows(S_CA, 2, TP - CONVK + 1, TP), "c_out")
            pool.wait_ge(sem("rw_pre"), 2)
            pool.dma_start(SW, ins["wkv"]).then_inc(sem("states_in"), 16)
            pool.dma_start(SH, ins["ssm"]).then_inc(sem("states_in"), 16)
            pool.wait_ge(sem("ssm_h"), 1)
            for t in range(2):
                pool.dma_start(outs["conv_h"][:, t], conv_h[:, t, :, 1:]).then_inc(sem("small_out"), 16)
            for t in range(6):
                pool.dma_start(outs["ssm_h"][:, t], ssm_h[:, t, :, 1:]).then_inc(sem("small_out"), 16)
            out("ssm_tail", rows(S_XBC, 6, TP - SSMK + 1, TP))
            pool.wait_ge(sem("smp_done"), 1)
            out("wkv_s", SW, "s_out")
            out("ssm_s", SH, "s_out")

            pool.wait_ge(sem("pre_done"), 1)
            with pool.Fori(0, NITER) as i:
                for dst, src in ((BT, bb), (KTB, S_K), (VV, S_V)):
                    for h in range(2):
                        a = (bb[64 * h:64 * h + 64, :, bass.ds(i * SC, SC)] if src is bb else
                             PR[64 * h:64 * h + 64, src:src + 2, bass.ds(i * SC + PAD, SC)])
                        ins_ = nc.gpsimd.tensor_copy(dst[64 * h:64 * h + 64, :, 64 * h:64 * h + 64].rearrange("p (c t) j -> p c t j", c=2),
                                                     a.rearrange("p t (c j) -> p c t j", c=2))
                ins_.then_inc(sem("bkv"), 1)
                for j in range(4):
                    for c in range(NCH):
                        pool.wait_ge(sem("evac"), 12 * i + 3 * NSLOT + 3 * j + c + 1)
                        pool.dma_start(gate_scratch[:, bass.ds(4 * i + j, 1), chunk(c)], stage[:, c:c + 1, :]
                                       ).then_inc(sem(f"gate_out{c}"), 16)
            pool.wait_ge(sem("ssm_fin"), 2 * NITER)
            out("wkv_p", ST, "st_out")
            out("ssm_p", HT, "st_out")
            pool.wait_ge(sem("br_ready"), 4)
            for c in range(NCH):
                pool.wait_ge(sem(f"gate_out{c}"), 16 * BR * KT)
            for dt in range(KT):
                if dt >= 2:
                    pool.wait_ge(sem("up_ev"), 12 * (dt - 1))
                pool.dma_start(GB[dt % 2], gate_scratch[:, 4 * dt:4 * dt + 4, :]
                               ).then_inc(sem(f"gb_in{dt % 2}"), 16)
                if dt == 1:
                    pool.dma_start(rows(X2, KT), ins["x_t"]).then_inc(sem("x_re"), 16)


SPECS = [
    ("x_t", (P, KT, T)), ("w_all", (P, N_W, KT * P)), ("vec", (P, NVEC)), ("cst", (P, NCST)), ("lora_w", (P, 2 * P)),
    ("pool_w", (P, 2, P)), ("w_dt", (P, KT, 4)), ("w_r", (P, KT, 20)), ("shift_in", (P, 7, NSMP)),
    ("pool_h", (P, 2, NSMP, POOLH)), ("conv_h", (P, 2, NSMP, CONVK - 1)), ("ssm_h", (P, 6, NSMP, SSMK - 1)),
    ("wkv", (P, NSMP, 2, HD)), ("ssm", (P, NSMP, 2, P)), ("w_gu", (NE, P, KT * 2 * HID)), ("w_dn", (NE, P, 2 * D)),
]
OUTS = [
    ("y_t", (P, KT, T)), ("shift", (P, 7, 1 + NSMP)), ("pool_tail", (P, 2, POOLH)), ("pool_h", (P, 2, NSMP, POOLH)),
    ("conv_tail", (P, 2, CONVK - 1)), ("conv_h", (P, 2, NSMP, CONVK - 1)), ("ssm_tail", (P, 6, SSMK - 1)),
    ("ssm_h", (P, 6, NSMP, SSMK - 1)), ("wkv_p", (P, 2, P)), ("wkv_s", (P, NSMP, 2, HD)), ("ssm_p", (P, 2, P)),
    ("ssm_s", (P, NSMP, 2, P)),
]


def pack(I):
    A = {k: np.asarray(x) for k, x in I.items()}

    def fm(a):
        a = np.moveaxis(a, -1, 0)
        return np.moveaxis(a.reshape((a.shape[0] // P, P) + a.shape[1:]), 1, 0)

    x = np.concatenate([A["x_prompt"][0], A["x_sample"][:, 0]], 0)
    w_in = A["w_in"][0]
    off_pool = 896
    off_conv, off_ssm = off_pool + 256, off_pool + 256 + 512
    off_dt = off_ssm + 256 + 768
    off_gate = off_dt + 4

    def tiles(w):
        return w.reshape(KT, P, -1, P).transpose(1, 2, 0, 3)

    gate = w_in[:, off_gate:].reshape(D, BR, KT, P)[:, [1, 0, 2, 3]].transpose(0, 2, 1, 3).reshape(D, -1)
    br = A["w_branch"][0][[1, 0, 2, 3]].reshape(BR, 2, P, KT, P).transpose(2, 3, 0, 1, 4).reshape(P, KT, KT, P)
    w_all = np.concatenate([tiles(w_in[:, :off_dt]), tiles(gate), br, tiles(A["w_out"][0])], 1).reshape(P, N_W, KT * P)

    vec = np.zeros((P, NVEC), np.float32)

    def put(name, a):
        o, w = VEC[name]
        vec[:, o:o + w] = np.broadcast_to(a, (P, w)) if a.ndim == 1 else a.reshape(P, w)

    for name, key in [("mu", "rwkv_mu"), ("w0", "rwkv_w0"), ("a0", "rwkv_a0"), ("kkw", "rwkv_kk"), ("ka", "rwkv_ka"),
                      ("ln_g", "rwkv_ln_g"), ("ln_b", "rwkv_ln_b"), ("pool_scale", "pool_scale"), ("conv_b", "conv_b"),
                      ("conv_ln_g", "conv_ln_g"), ("conv_ln_b", "conv_ln_b"), ("ssm_b", "ssm_conv_b"), ("ssm_g", "ssm_norm_g"),
                      ("g_mix", "norm_mix_g"), ("g_ffn", "norm_ffn_g")]:
        put(name, fm(A[key][0]))
    put("g_fin", fm(A["final_norm_g"]))
    put("rk", fm(A["rwkv_rk"][0].reshape(-1)))
    put("ssm_d", fm(np.repeat(A["ssm_d"][0], HD)))
    put("conv_w", fm(A["conv_w"][0]))
    put("ssm_w", fm(A["ssm_conv_w"][0]))
    put("dt_bias", A["ssm_dt_bias"][0])
    put("a_log", A["ssm_a_log"][0])
    put("r_bias", np.concatenate([A["moe_router_group_b"][0], A["moe_router_expert_b"][0]]))

    pool_w = np.zeros((P, 2, P), np.float32)
    for g in range(4):
        o = 64 * (g % 2)
        pool_w[o:o + 64, g // 2, o:o + 64] = A["pool_w"][0, g]

    def state(a):
        return a.reshape(NSMP, 2, 2, HD, -1).transpose(2, 3, 0, 1, 4).reshape(P, NSMP, 2, -1)

    gu = np.concatenate([A["moe_w_gate"][0], A["moe_w_up"][0]], 2)
    out = {
        "x_t": fm(x), "w_all": w_all, "vec": vec, "cst": constants(),
        "lora_w": np.concatenate([A["rwkv_w2"][0], A["rwkv_a2"][0], A["rwkv_g2"][0]], 0), "pool_w": pool_w,
        "w_dt": w_in[:, off_dt:off_gate].reshape(KT, P, 4).transpose(1, 0, 2),
        "w_r": np.concatenate([A["moe_router_group_w"][0], A["moe_router_expert_w"][0]], 1).reshape(KT, P, 20).transpose(1, 0, 2),
        "shift_in": fm(A["state_rwkv_shift"][0]), "pool_h": fm(A["state_pool"][0]), "conv_h": fm(A["state_conv"][0]),
        "ssm_h": fm(A["state_ssm_conv"][0]), "wkv": state(A["state_rwkv_wkv"][0]), "ssm": state(A["state_ssm"][0]),
        "w_gu": gu.reshape(NE, KT, P, 2 * HID).transpose(0, 2, 1, 3).reshape(NE, P, -1),
        "w_dn": A["moe_w_down"][0].reshape(NE, 2, P, D).transpose(0, 2, 1, 3).reshape(NE, P, -1),
    }
    return {k: np.ascontiguousarray(a, dtype=np.float32) for k, a in out.items()}


def unpack(r):
    def ft(a):
        a = np.moveaxis(a, 0, 1)
        return np.moveaxis(a.reshape((-1,) + a.shape[2:]), 0, -1)

    def heads(a):
        return a.reshape(2, HD, NSMP, 2, -1).transpose(2, 3, 0, 1, 4).reshape(NSMP, 4, HD, -1)

    y = ft(r["y_t"])
    shift = ft(r["shift"])
    st = r["wkv_p"].reshape(2, HD, 2, 2, HD)
    wkv_p = np.stack([st[h % 2, :, h // 2, h % 2, :].T for h in range(4)])
    ssm_p = r["ssm_p"].reshape(P, 4, HD).transpose(1, 2, 0)
    res = (y[None, :TP], y[TP:, None], shift[None, :1], wkv_p[None, None], ft(r["pool_tail"])[None, None],
           ft(r["conv_tail"])[None, None], ft(r["ssm_tail"])[None, None], ssm_p[None, None],
           shift[None, 1:], heads(r["wkv_s"])[None], ft(r["pool_h"])[None], ft(r["conv_h"])[None], ft(r["ssm_h"])[None],
           heads(r["ssm_s"])[None])
    return tuple(np.ascontiguousarray(a) for a in res)


def kernel(**inputs):
    import concourse.bacc as bacc
    from concourse.bass_utils import run_bass_kernel_spmd

    nc = bacc.Bacc("TRN2", target_bir_lowering=False, num_devices=1)
    arrays = pack(inputs)
    ins = {n: nc.dram_tensor("in_" + n, s, F32, kind="ExternalInput").ap() for n, s in SPECS}
    outs = {n: nc.dram_tensor("out_" + n, s, F32, kind="ExternalOutput").ap() for n, s in OUTS}
    build(nc, ins, outs)
    r = run_bass_kernel_spmd(nc, [{"in_" + n: arrays[n] for n, _ in SPECS}], core_ids=[0])
    return unpack({n: r.results[0]["out_" + n] for n, _ in OUTS})
```

```python
from contextlib import ExitStack

import numpy as np

import concourse.bass as bass
from concourse import mybir

F32 = mybir.dt.float32
I32 = mybir.dt.int32
ALU = mybir.AluOpType
ACT = mybir.ActivationFunctionType
AX = mybir.AxisListType.X

P = 128
D = 1024
TP = 1024
NSMP = 8
T = TP + NSMP
KT = D // P
NCH = 3
CW = T // NCH
PAD = 30
PW = PAD + T
HD = 64
RC = 64
SC = 128
NITER = TP // SC
CONVK = 31
SSMK = 4
POOLH = 15
NE = 16
NG = 4
HID = 256
BR = 4
DECAY_SCALE = float(np.exp(-0.5))

S_POOL, S_CA, S_CG, S_Z, S_XBC, S_R, S_K, S_V, S_LORA = 0, 2, 4, 6, 8, 14, 16, 18, 20
NSLOT = 21
O_POOL, O_RWKV, O_CONV, O_SSM = 0, 2, 4, 6
N_GATE0 = NSLOT
N_BR0 = N_GATE0 + BR * KT
N_OUT0 = N_BR0 + KT
N_W = N_OUT0

NTT = (T + P - 1) // P
NSLOTS = (2 * T + NE * (P - 1)) // P
HALF = D // 2

VEC = {}
_n = 0
for _name, _w in [("mu", 7), ("w0", 2), ("a0", 2), ("kkw", 2), ("ka", 2), ("rk", 2), ("ln_g", 2), ("ln_b", 2),
                  ("pool_scale", 2), ("conv_b", 2), ("conv_ln_g", 2), ("conv_ln_b", 2), ("ssm_b", 6), ("ssm_d", 2),
                  ("ssm_g", 2), ("g_mix", 8), ("conv_w", 2 * CONVK), ("ssm_w", 6 * SSMK),
                  ("dt_bias", 4), ("a_log", 4), ("r_bias", 20)]:
    VEC[_name] = (_n, _w)
    _n += _w
NVEC = _n

CST = {}
_n = 0
for _name, _w in [("ident", P), ("ones", P), ("bones", P), ("tri", P), ("m_strict_incl", 2 * P), ("m_lev1_incl", 2 * P),
                  ("m_lev1_low", P), ("m_lev_low", 5 * P), ("imask", HD), ("rcount", 2 * 16), ("rwin", 2), ("rank4", 4),
                  ("valid", NTT), ("token", NTT), ("count", P), ("count128", NSLOTS), ("part", 1)]:
    CST[_name] = (_n, _w)
    _n += _w
NCST = _n
NORM_EPS, LN_EPS, GN_EPS = 1e-6, 1e-5, 64e-5
NSMALL_IN = 7 + 2 + 2 + 6
NSMALL_OUT = 1 + 2 + 1 + 2 + 3 + 1
PER_TURN = 9
LEVELS = (2, 4, 8, 16, 32)


def constants():
    c = np.zeros((P, NCST), np.float32)

    def put(name, a):
        o, w = CST[name]
        c[:a.shape[0], o:o + w] = a.reshape(a.shape[0], w)

    i = np.arange(P)
    same = (i[:, None] // RC) == (i[None, :] // RC)
    upper = (same & (i[:, None] < i[None, :])).astype(np.float32)
    incl = (same & (i[:, None] <= i[None, :])).astype(np.float32)

    def level_up(b):
        return (((i[:, None] // (2 * b)) == (i[None, :] // (2 * b))) & ((i[:, None] // b) % 2 == 0)
                & ((i[None, :] // b) % 2 == 1)).astype(np.float32)

    put("ident", np.eye(P))
    put("ones", np.ones((P, P)))
    put("bones", same.astype(np.float32))
    put("tri", (i[:, None] <= i[None, :]).astype(np.float32))
    put("m_strict_incl", np.stack([upper, incl], 1))
    put("m_lev1_incl", np.stack([-level_up(1), incl], 1))
    put("m_lev1_low", -level_up(1).T)
    put("m_lev_low", np.stack([level_up(b).T for b in LEVELS], 1))
    put("imask", np.eye(HD)[i % HD])
    win = np.array([[2, 8], [4, 16]])[i // HD]
    put("rcount", 1.0 / np.minimum(np.arange(16)[None, None, :] + 1, win[:, :, None]))
    put("rwin", 1.0 / win)
    put("rank4", np.broadcast_to(np.array([4.0, 3.0, 2.0, 1.0]), (P, 4)))
    token = P * np.arange(NTT)[None, :] + i[:, None]
    put("valid", token < T)
    put("token", np.where(token < T, token, 0))
    put("count", np.broadcast_to(i, (P, P)))
    put("count128", np.broadcast_to(P * np.arange(NSLOTS), (P, NSLOTS)))
    put("part", i[:, None])
    return c


class Link:

    def __init__(self, eng, sem):
        self.eng, self.sem, self.n, self.base = eng, sem, 0, 0

    def __call__(self, ins):
        ins.then_inc(self.sem, 1)
        self.n += 1
        self.eng.wait_ge(self.sem, self.base + self.n)

    def enter(self, i, per):
        self.n0, self.per = self.n, per
        self.base = i * per

    def leave(self, turns):
        assert self.n - self.n0 == self.per, (self.n - self.n0, self.per)
        self.n += self.per * (turns - 1)
        self.base = 0


def build(nc, ins, outs):
    ctx = ExitStack()
    with ctx:
        def sb(name, shape):
            return ctx.enter_context(nc.sbuf_tensor(name, shape, F32))

        sems = {}

        def sem(name):
            if name not in sems:
                sems[name] = ctx.enter_context(nc.semaphore(name))
            return sems[name]

        gate_scratch = nc.dram_tensor("gate_scratch", (P, BR * KT, T), F32, kind="Internal").ap()

        h2_rows = nc.dram_tensor("h2_rows", (T, D), F32, kind="Internal").ap()
        slot_rows = nc.dram_tensor("slot_rows", (NSLOTS * P, D), F32, kind="Internal").ap()

        vec = sb("vec", [P, NVEC])
        cst = sb("cst", [P, NCST])
        wring = sb("wring", [P, 2, KT, P])
        H = sb("H", [P, KT, T])
        PR = sb("PR", [P, NSLOT, PW])
        lora_w = sb("lora_w", [P, 2 * P])
        pool_w = sb("pool_w", [P, 2, P])
        w_dt = sb("w_dt", [P, KT, 4])
        w_r = sb("w_r", [P, KT, 20])
        pool_tail = sb("pool_tail", [P, 2, POOLH])
        pool_h = sb("pool_h", [P, 2, NSMP, 16])
        conv_h = sb("conv_h", [P, 2, NSMP, CONVK])
        ssm_h = sb("ssm_h", [P, 6, NSMP, SSMK])
        shift_in = sb("shift_in", [P, 7, NSMP])
        shift_out = sb("shift_out", [P, 7, 1 + NSMP])
        stage = sb("stage", [P, 3, CW])
        kk = sb("kk", [P, 2, TP])
        bb = sb("bb", [P, 2, TP])
        pc = sb("pc", [P, 2, TP // RC])
        dt_t = sb("dt_t", [P, 9, 4])
        da_t = sb("da_t", [P, 9, 4])
        smallv = sb("smallv", [P, 16])
        smallv2 = sb("smallv2", [P, 20])
        dsum = sb("dsum", [P, NSMP])
        smp = sb("smp", [P, 6, 2, NSMP])
        SCRW = 10700
        scr = sb("scr", [P, SCRW])
        tick = sb("tick", [P, 4])
        idx = ctx.enter_context(nc.sbuf_tensor("idx", [P, 2 * NSLOTS + 2 * NTT], I32))
        idx_now = ctx.enter_context(nc.sbuf_tensor("idx_now", [P, 8], I32))
        ps = ctx.enter_context(nc.psum_tensor("ps", [P, 8, 512], F32))

        def carve(start, *shape):
            n = int(np.prod(shape))
            assert start + n <= SCRW, (start, shape)
            a = scr[:, start:start + n]
            if len(shape) == 1:
                return a
            names = "abcd"[:len(shape)]
            return a.rearrange(f"p ({' '.join(names)}) -> p {' '.join(names)}",
                               **{k: v for k, v in zip(names, shape)})

        def v(name, j=0, w=1):
            o = VEC[name][0] + j
            return vec[:, o:o + w]

        def cc(name, j=0, w=None):
            o, full = CST[name]
            return cst[:, o + j:o + (j + w if w else full)]

        ident, ones, bones, tri = cc("ident"), cc("ones"), cc("bones"), cc("tri")

        def chunk(c):
            return slice(c * CW, (c + 1) * CW)

        def row(slot, a=0, b=T):
            return PR[:, slot, PAD + a:PAD + b]

        def rows(slot, n, a=0, b=T):
            return PR[:, slot:slot + n, PAD + a:PAD + b]

        def ps3(b, w=CW):
            return ps[:, b:b + 3, 0:w]

        def as3(ap):
            return ap.rearrange("p (c w) -> p c w", c=NCH)

        x_t = carve(0, KT, T)
        sq = carve(8 * T, 2, T)
        STG = stage[:, :, :].rearrange("p a b -> p (a b)")
        RS0 = STG
        SG, AA, LL, TM = carve(0, 2, T), carve(2 * T, 2, T), carve(4 * T, 2, T), carve(6 * T, 2, T)
        PA, PB = carve(8 * T, PW), carve(8 * T + PW, PW)
        RESET = STG[:, 0:TP]

        SW = carve(0, NSMP, 2, HD)
        XE = [carve(1024 * (1 + j), NSMP, 2, HD) for j in range(2)]
        SH = carve(3072, NSMP, 2, P)
        BE = carve(5120, NSMP, 2, P)
        W2 = carve(7168, NSMP, 2, P)
        dsm = carve(9216, 16, 16)
        XS = carve(9472, 6, NSMP)
        XSS = carve(9520, 6, NSMP)
        XSW = carve(9568, 6, NSMP, SSMK)
        CHW = carve(8 * T + 2 * PW, NSMP, CONVK)

        KR = carve(0, 4, 2, P)
        BT, KTB, VV = carve(1024, 4, P), carve(1536, 4, P), carve(2048, 4, P)
        NL, NLB, X1, TT, U = (carve(2560 + 512 * j, 4, P) for j in range(5))
        BM, MK = carve(5120, 4, 2, P), carve(6144, 4, 2, P)
        VT, BTT, KTT = (carve(7168 + 512 * j, 4, P) for j in range(3))
        XN, SA, ST = (carve(8704 + 256 * j, 2, P) for j in range(3))
        PCS = carve(9472, 2, 2)
        XC = carve(9480, 6, SC)
        HT = carve(10248, 2, P)
        ACB, EE, EA = NL, NLB, X1
        XDT, XTE = carve(7168, 2, P), carve(7424, 2, P)
        BTOK, GM = carve(7680, 2, P), carve(8192, 2, P)
        SX, SZ = carve(6144, 6, SC), carve(6912, 2, SC)
        DAI, DTI, AT, TE, DEC = (smallv2[:, 4 * j:4 * j + 4] for j in range(5))

        V1, V2, V3, V4, V5 = (carve(2 * j * T, 2, T) for j in range(5))

        block = ctx.enter_context(nc.Block())

        def bc(ap, shape):
            return ap.to_broadcast(shape)

        def mid(ap, n):
            return ap.unsqueeze(1).to_broadcast([ap.shape[0], n, ap.shape[1]])

        def last(ap, n):
            return ap.unsqueeze(len(ap.shape)).to_broadcast(list(ap.shape) + [n])


        PRF = PR[:, :, :].rearrange("p s w -> p (s w)")
        GB = [carve(s * 4 * T, BR, T) for s in range(2)]
        GP = carve(8 * T, 2, CW)
        X2 = PRF[:, 8 * PW:8 * PW + NTT * D].rearrange("p (n d) -> p n d", n=NTT)
        WO = [PRF[:, o:o + KT * HALF].rearrange("p (k m) -> p k m", k=KT) for o in (17 * PW, 0)]
        GAIN = kk
        H2 = bb
        HF = carve(0, 2, KT, P)
        RO = 3 * T
        LG, EX = carve(RO, NTT, 20), carve(RO + 180, NTT, 4, 4)
        q4 = [carve(RO + 324 + 36 * j, NTT, 4) for j in range(6)]
        q1 = [carve(RO + 540 + NTT * j, NTT) for j in range(7)]
        SS, RSTD = carve(RO + 603, NTT), carve(RO + 612, NTT)
        OH = carve(RO + 621, 2, NTT * NE)
        MEMB = carve(RO + 909, NTT * NE)
        CMP = carve(RO + 1053, NE * NTT)
        NB, INC, START = (carve(RO + 1197 + NE * j, NE) for j in range(3))
        POSE = carve(RO + 1245, NTT * NE)
        POS, POSQ, POSS = (carve(RO + 1389 + 2 * NTT * j, 2 * NTT) for j in range(3))
        EID = carve(RO + 1443, NSLOTS)
        OS = carve(RO + 1475, 2 * NTT, NSLOTS)
        CMP2 = carve(RO + 2051, 2 * NTT, NSLOTS)
        OQ = carve(RO + 2627, 2 * NTT, P)
        IDX_W, IDX_T = idx[:, 0:NSLOTS], idx[:, NSLOTS:2 * NSLOTS]
        IDX_Y = idx[:, 2 * NSLOTS:2 * NSLOTS + 2 * NTT]
        HFLAT = H[:, :, :].rearrange("p k t -> p (k t)")
        GU = [HFLAT[:, s * KT * 2 * HID:(s + 1) * KT * 2 * HID] for s in range(2)]
        DN = [PRF[:, s * 2 * D:(s + 1) * 2 * D] for s in range(2)]
        XG = [PRF[:, 4 * D + s * D:4 * D + (s + 1) * D] for s in range(2)]
        XT = [PRF[:, 6 * D + s * D:6 * D + (s + 1) * D] for s in range(2)]
        SIL, ACTB = carve(0, 2, 2 * P), carve(4 * P, 2, 2 * P)
        YO = [carve(8 * P + s * D, D) for s in range(2)]
        YG = [[HFLAT[:, (2 * s + c) * D:(2 * s + c + 1) * D] for c in range(2)] for s in range(4)]
        YB = [PRF[:, s * D:(s + 1) * D] for s in range(2)]

        def rows_of(n):
            return P if n < NTT - 1 else T - P * (NTT - 1)

        @block.sync
        def _(sp):
            for h in range(2):
                sp.dma_start(x_t[:, 4 * h:4 * h + 4, :], ins["x_t"][:, 4 * h:4 * h + 4, :]).then_inc(sem(f"x_in{h}"), 16)

            def load(n, slot):
                sp.dma_start(wring[:, slot:slot + 1, :, :].rearrange("p a k m -> p a (k m)"),
                             ins["w_all"][:, bass.ds(n, 1), :]).then_inc(sem(f"w_in{slot}"), 16)
            load(0, 0)
            load(1, 1)
            with sp.Fori(1, N_BR0 // 2 + 1) as j:
                sp.wait_ge(sem("dense"), 6 * j - 3)
                load(2 * j, 0)
                sp.wait_ge(sem("dense"), 6 * j)
                load(2 * j + 1, 1)
            sp.wait_ge(sem("dense"), 3 * N_BR0)
            load(N_BR0 + 1, 0)
            sp.wait_ge(sem("up_mm"), 12)
            load(N_BR0 + 2, (N_BR0 + 2) % 2)
            sp.dma_start(WO[0].rearrange("p k m -> p (k m)"), ins["w_out"][:, 0, :]).then_inc(sem("wo_in"), 16)
            for n in range(N_BR0 + 3, N_W):
                sp.wait_ge(sem("up_mm"), 12 * (n - N_BR0 - 1))
                load(n, n % 2)
            sp.wait_ge(sem("up_mm"), 12 * KT)
            sp.wait_ge(sem("wo_in"), 16)
            sp.dma_start(WO[1].rearrange("p k m -> p (k m)"), ins["w_out"][:, 1, :]).then_inc(sem("wo_in"), 16)
            for n in range(NTT):
                m = rows_of(n)
                sp.wait_ge(sem("h2_row"), n + 1)
                sp.dma_start(h2_rows[n * P:n * P + m, :], H2[0:m, n % 2, :]).then_inc(sem(f"h2_out{n % 2}"), 16)
            with sp.Fori(0, NSLOTS // 2) as i:
                for s in range(2):
                    sp.wait_ge(sem("yo_act"), 2 * i + s + 1)
                    sp.wait_ge(sem("yo_dve"), 2 * i + s + 1)
                    sp.dma_start(slot_rows.rearrange("(n p) d -> p n d", p=P)[:, bass.ds(2 * i + s, 1), :], YO[s].unsqueeze(1)
                                 ).then_inc(sem(f"yo_out{s}"), 16)
            for n in range(NTT):
                m = rows_of(n)
                sp.wait_ge(sem("y_ready"), n + 1)
                sp.dma_start(outs["y"][n * P:n * P + m, :], YB[n % 2][0:m, :]).then_inc(sem(f"y_out{n % 2}"), 16)
            sp.wait_ge(sem("y_out0"), 16 * 5)
            sp.wait_ge(sem("y_out1"), 16 * 4)
            sp.wait_ge(sem("small_out"), 16 * NSMALL_OUT)
            for c in range(3):
                sp.wait_ge(sem(f"gate_out{c}"), 16 * (BR * KT + 1))

        @block.tensor
        def _(pe):
            def norm_sums():
                for k in range(KT):
                    pe.wait_ge(sem("norm_sq"), k + 1)
                    for c in range(NCH):
                        mm = pe.matmul(ps[:, c, 0:CW], ones, sq[:, k % 2, chunk(c)], start=k == 0, stop=k == KT - 1)
                    mm.then_inc(sem("norm_sum"), 1)

            def half(slot, c, lo, hi, evac, loaded):
                if lo == 0 and evac is not None:
                    pe.wait_ge(sem("evac"), evac)
                if lo == 0 and c == 0:
                    pe.wait_ge(sem(f"w_in{slot}"), loaded)
                for k in range(lo, hi):
                    mm = pe.matmul(ps[:, c, 0:CW], wring[:, slot, k, :], H[:, k, chunk(c)], start=k == 0, stop=k == KT - 1)
                if hi == KT:
                    mm.then_inc(sem("dense"), 1)

            def pairs(j0, j1):
                with pe.Fori(j0, j1) as j:
                    for c in range(NCH):
                        half(1, c, 0, KT, 6 * j + 3 + c - 2, 16 * j + 16)
                    for c in range(NCH):
                        half(0, c, 0, KT, 6 * j + 6 + c - 2, 16 * j + 32)

            pe.wait_ge(sem("small_in"), 16 * NSMALL_IN)
            norm_sums()
            pe.wait_ge(sem("h_ready"), 1)
            for c in range(NCH):
                half(0, c, 0, KT, None, 16)
            pairs(0, 3)
            pairs(3, 6)

            for t in range(2):
                pe.wait_ge(sem("k_sq"), t + 1)
                if t == 1:
                    pe.wait_ge(sem("k_ss"), 1)
                for c in range(NCH):
                    mm = pe.matmul(ps[:, 3 + c, 0:CW], bones, TM[:, t, chunk(c)], start=True, stop=True)
                mm.then_inc(sem("head_sum"), 1)
            pe.wait_ge(sem("lora_act"), 2)
            pe.wait_ge(sem("k_ss"), 2)
            for n in range(4):
                lo, t = 32 * (n // 2), n % 2
                if n:
                    pe.wait_ge(sem("lora_ev"), n)
                for c in range(NCH):
                    mm = pe.matmul(ps[:, 3 + c, 0:CW], lora_w[lo:lo + 32, t * P:(t + 1) * P],
                                   PR[lo:lo + 32, S_LORA, PAD + c * CW:PAD + (c + 1) * CW], start=True, stop=True)
                mm.then_inc(sem("lora_mm"), 1)

            pairs(6, 10)

            for n in range(9):
                m = P if n < 8 else NSMP
                for k in range(KT):
                    mm = pe.matmul(ps[0:m, 6, 4 * n:4 * n + 4], H[:, k, n * P:n * P + m], w_dt[:, k, :], start=k == 0,
                                   stop=k == KT - 1)
            mm.then_inc(sem("dt_mm"), 1)
            pe.wait_ge(sem("lora_ev"), 4)
            for t in range(2):
                pe.wait_ge(sem("rk_prod"), t + 1)
                if t == 1:
                    pe.wait_ge(sem("bonus"), 1)
                for c in range(NCH):
                    mm = pe.matmul(ps[:, 3 + c, 0:CW], bones, TM[:, t, chunk(c)], start=True, stop=True)
                mm.then_inc(sem("head_sum"), 1)
            pe.wait_ge(sem("pool_diff"), 2)
            for t in range(2):
                pe.wait_ge(sem("evac"), 3 * NSLOT) if t == 0 else pe.wait_ge(sem("pool_ev"), 1)
                for c in range(NCH):
                    mm = pe.matmul(ps[:, c, 0:CW], pool_w[:, t, :], row(S_POOL + t, c * CW, (c + 1) * CW), start=True, stop=True)
                mm.then_inc(sem("pool_mm"), 1)

            pe.wait_ge(sem("bonus"), 2)
            for n in range(5):
                pe.wait_ge(sem("x_exp"), n + 1)
                b = 3 + 2 * (n % 2)
                if n == 1:
                    pe.wait_ge(sem("dt_read"), 1)
                for h in range(2):
                    mm = pe.matmul(ps[:, b + h, :], bones, XE[n % 2][:, 4 * h:4 * h + 4, :, :].rearrange("p a b c -> p (a b c)"),
                                   start=True, stop=True)
                mm.then_inc(sem("x_bc"), 1)
            pe.wait_ge(sem("dta"), 1)
            pe.wait_ge(sem("pool_ev"), 2)
            for hh in range(4):
                for q, src in enumerate((dt_t, da_t)):
                    mm = pe.matmul(ps[:, 7, (q * 4 + hh) * 8:(q * 4 + hh) * 8 + 8], bc(src[0:NSMP, 8, hh:hh + 1], [NSMP, P]),
                                   ident[0:NSMP, 0:NSMP], start=True, stop=True)
            mm.then_inc(sem("dt_bc"), 1)
            for n in range(2):
                pe.wait_ge(sem("bc_exp"), n + 1)
                if n == 0:
                    pe.wait_ge(sem("x_use"), 5)
                for h in range(4):
                    mm = pe.matmul(ps[:, h, :], ones, BE[:, 2 * h:2 * h + 2, :, :].rearrange("p a b c -> p (a b c)"),
                                   start=True, stop=True)
                mm.then_inc(sem("bc_bc"), 1)
            pe.wait_ge(sem("pre_done"), 1)

            with pe.Fori(0, NITER) as i:
                fill = [(j, c, h) for j in range(4) for c in range(NCH) for h in range(2)]

                def filler(k=1):
                    for _ in range(k):
                        j, c, h = fill.pop(0)
                        half((NSLOT + j) % 2, c, 4 * h, 4 * h + 4, 12 * i + 3 * NSLOT + 3 * j + c - 2,
                             16 * (2 * i + (NSLOT + j) // 2 + 1))

                pe.wait_ge(sem("kr"), i + 1)
                pe.wait_ge(sem("bkv"), i + 1)
                pe.wait_ge(sem("ssm_fin"), 2 * i + 2)
                for q in range(4):
                    mm = pe.matmul(ps[:, 3, q * P:(q + 1) * P], KR[:, q, 0, :], BT[:, q, :], start=True, stop=True)
                mm.then_inc(sem("prod"), 1)
                for n in range(4):
                    for q in range(2 * (n % 2), 2 * (n % 2) + 2):
                        mm = pe.matmul(ps[:, 4 + n, (q % 2) * 256:(q % 2) * 256 + 256], (BT if n < 2 else KTB)[:, q, :],
                                       KR[:, q, :, :].rearrange("p a b -> p (a b)"), start=True, stop=True)
                    mm.then_inc(sem("prod"), 1)
                filler()
                for n, src in enumerate((VV, BT, KTB)):
                    if n == 0:
                        pe.wait_ge(sem("nl"), i + 1)
                    else:
                        pe.wait_ge(sem("masked"), 4 * i + n)
                    for q in range(4):
                        mm = pe.transpose(ps[:, 3 + n, q * P:(q + 1) * P], src[:, q, :], ident)
                    mm.then_inc(sem("turned"), 1)
                filler()
                for l in range(5):
                    pe.wait_ge(sem("lev"), 5 * i + l + 1)
                    pe.wait_ge(sem("masked"), 4 * i + 4)
                    for q in range(4):
                        mm = pe.matmul(ps[:, 6, q * P:(q + 1) * P], NLB[:, q, :], U[:, q, :], start=True, stop=True)
                    mm.then_inc(sem("x1"), 1)
                    filler()
                    pe.wait_ge(sem("x1c"), 5 * i + l + 1)
                    for q in range(4):
                        mm = pe.matmul(ps[:, 7, q * P:(q + 1) * P], TT[:, q, :], X1[:, q, :], start=True, stop=True)
                    mm.then_inc(sem("du"), 1)
                    if l < 4:
                        pe.wait_ge(sem("turn_c"), 3 * i + 1)
                        for q in range(4):
                            mm = pe.matmul(ps[:, 3, q * P:(q + 1) * P], X1[:, q, :], TT[:, q, :], start=True, stop=True)
                        mm.then_inc(sem("dt_"), 1)
                    filler()
                pe.wait_ge(sem("u_done"), i + 1)
                pe.wait_ge(sem("turn_c"), 3 * i + 3)
                for c2 in range(2):
                    for t in range(2):
                        q = 2 * c2 + t
                        pe.wait_ge(sem("st"), 4 * i + 2 * c2 + 2)
                        pe.matmul(ps[:, 4 + t, 0:P], KR[:, q, 0, :], ST[:, t, :], start=True, stop=False)
                        pe.matmul(ps[:, 4 + t, 0:P], MK[:, q, 0, :], VT[:, q, :], start=False, stop=True
                                  ).then_inc(sem("xx"), 1)
                        pe.wait_ge(sem("y_ev"), 4 * i + 2 * c2 + 1)
                        pe.matmul(ps[:, 6 + t, 0:P], ST[:, t, :], KR[:, q, 1, :], start=True, stop=False)
                        pe.matmul(ps[:, 6 + t, 0:P], VT[:, q, :], MK[:, q, 1, :], start=False, stop=False)
                    filler()
                    for t in range(2):
                        q = 2 * c2 + t
                        pe.wait_ge(sem("xn"), 4 * i + 2 * c2 + t + 1)
                        pe.matmul(ps[:, 4 + t, P:2 * P], U[:, q, :], XN[:, t, :], start=True, stop=True
                                  ).then_inc(sem("sa"), 1)
                    filler()
                    for t in range(2):
                        q = 2 * c2 + t
                        pe.wait_ge(sem("sac"), 4 * i + 2 * c2 + t + 1)
                        pe.matmul(ps[:, 4 + t, 2 * P:3 * P], BTT[:, q, :], SA[:, t, :], start=True, stop=False)
                        pe.matmul(ps[:, 4 + t, 2 * P:3 * P], KTT[:, q, :], VT[:, q, :], start=False, stop=False)
                        pe.matmul(ps[:, 4 + t, 2 * P:3 * P], ident, ST[:, t, :], start=False, stop=True
                                  ).then_inc(sem("ss"), 1)
                        pe.matmul(ps[:, 6 + t, 0:P], SA[:, t, :], BM[:, q, 1, :], start=False, stop=True
                                  ).then_inc(sem("yy"), 1)
                    filler()
                filler()
                pe.wait_ge(sem("xc"), i + 1)
                for hh in range(4):
                    mm = pe.matmul(ps[:, 3, hh * P:(hh + 1) * P], bc(DAI[:, hh:hh + 1], [P, P]), tri, start=True, stop=True)
                mm.then_inc(sem("s1"), 1)
                pe.wait_ge(sem("st"), 4 * i + 6)
                pe.matmul(ps[:, 4, 0:4], tri, DAI, start=True, stop=True)
                for g in range(2):
                    mm = pe.matmul(ps[:, 4, P + g * P:2 * P + g * P], XC[:, 2 + g, :], XC[:, 4 + g, :], start=True, stop=True)
                mm.then_inc(sem("s1"), 1)
                pe.wait_ge(sem("st"), 4 * i + 6)
                for g in range(2):
                    mm = pe.transpose(ps[:, 5, g * P:(g + 1) * P], XC[:, g, :], ident)
                mm.then_inc(sem("s1"), 1)
                pe.wait_ge(sem("y_ev"), 4 * i + 5)
                for g in range(2):
                    mm = pe.transpose(ps[:, 6, g * P:(g + 1) * P], XC[:, 2 + g, :], ident)
                mm.then_inc(sem("s1"), 1)
                filler(3)
                pe.wait_ge(sem("sl"), i + 1)
                pe.wait_ge(sem("btok"), i + 1)
                pe.wait_ge(sem("y_ev"), 4 * i + 5)
                for hh in range(4):
                    g, o = hh // 2, 64 * (hh % 2)
                    pe.matmul(ps[o:o + 64, 7, g * P:(g + 1) * P], XDT[:, g, o:o + 64], EE[:, hh, :], start=True, stop=False)
                    mm = pe.matmul(ps[o:o + 64, 7, g * P:(g + 1) * P], HT[:, g, o:o + 64], EA[:, hh, :], start=False, stop=True)
                mm.then_inc(sem("sy"), 1)
                for g in range(2):
                    mm = pe.matmul(ps[:, 3, g * P:(g + 1) * P], BTOK[:, g, :], XTE[:, g, :], start=True, stop=True)
                mm.then_inc(sem("sh"), 1)
                filler(len(fill))

            pe.wait_ge(sem("ssm_fin"), 2 * NITER + 2)
            pe.wait_ge(sem("y_ev"), 4 * NITER + 1)
            pe.wait_ge(sem("evac"), 3 * N_BR0)
            for t in range(2):
                for c in range(NCH):
                    mm = pe.matmul(ps[:, 3 * t + c, 0:CW], bones, row(S_R + t, c * CW, (c + 1) * CW), start=True, stop=True)
                mm.then_inc(sem("br_sum"), 1)
            pe.wait_ge(sem("gn_ctr"), 1)
            for c in range(NCH):
                for t in range(2):
                    mm = pe.matmul(ps[:, c, 0:CW], ones, row(S_CG + t, c * CW, (c + 1) * CW), start=t == 0, stop=t == 1)
            mm.then_inc(sem("br_sum"), 1)
            pe.wait_ge(sem("gn_ctr"), 2)
            pe.wait_ge(sem("br_sq"), 2)
            for c in range(NCH):
                for t in range(2):
                    mm = pe.matmul(ps[:, 3 + c, 0:CW], ones, V5[:, t, chunk(c)], start=t == 0, stop=t == 1)
            mm.then_inc(sem("br_sum"), 1)
            pe.wait_ge(sem("br_sq"), 4)
            pe.wait_ge(sem("ln_ctr"), 2)
            for t in range(2):
                if t == 1:
                    pe.wait_ge(sem("sm_var"), 1)
                for c in range(NCH):
                    mm = pe.matmul(ps[:, 3 * t + c, 0:CW], bones, V2[:, t, chunk(c)], start=True, stop=True)
                mm.then_inc(sem("br_sum"), 1)
            pe.wait_ge(sem("br_sq"), 6)
            pe.wait_ge(sem("gn_v"), 1)
            for c in range(NCH):
                for t in range(2):
                    mm = pe.matmul(ps[:, c, 0:CW], ones, V4[:, t, chunk(c)], start=t == 0, stop=t == 1)
            mm.then_inc(sem("br_sum"), 1)
            for t in range(2):
                pe.wait_ge(sem("gn_v" if t == 0 else "ln_v"), 2 if t == 0 else 1)
                for c in range(NCH):
                    mm = pe.matmul(ps[:, 3 - 3 * t + c, 0:CW], lora_w[64:128, t * P:(t + 1) * P],
                                   PR[64:128, S_LORA, PAD + c * CW:PAD + (c + 1) * CW], start=True, stop=True)
                mm.then_inc(sem("br_sum"), 1)

            pe.wait_ge(sem("br_ready"), 4)
            for dt in range(KT):
                n = N_BR0 + dt
                pe.wait_ge(sem(f"w_in{n % 2}"), 16 * (n // 2 + 1))
                for b in range(BR):
                    for c in range(NCH):
                        m = 12 * dt + 3 * b + c
                        if m >= 6:
                            pe.wait_ge(sem("up_ev"), m - 5)
                        for k in range(2):
                            mm = pe.matmul(ps[:, m % 6, 0:CW], wring[:, n % 2, 2 * b + k, :],
                                           row(2 * b + k, c * CW, (c + 1) * CW), start=k == 0, stop=k == 1)
                        mm.then_inc(sem("up_mm"), 1)
            def turn(n):
                m, b = rows_of(n), 4 + 2 * (n % 2)
                pe.wait_ge(sem("h2_row"), n + 1)
                if n >= 2:
                    pe.wait_ge(sem("hf_ev"), n - 1)
                for k in range(KT):
                    mm = pe.transpose(ps[:, b + k // 4, (k % 4) * P:(k % 4) * P + m], H2[0:m, n % 2, k * P:(k + 1) * P],
                                      ident[0:m, 0:m])
                mm.then_inc(sem("h2_turn"), 1)

            def logits(n):
                m = rows_of(n)
                pe.wait_ge(sem("hf_ev"), n + 1)
                for k in range(KT):
                    mm = pe.matmul(ps[0:m, 3, 20 * n:20 * n + 20], HF[:, n % 2, k, 0:m], w_r[:, k, :], start=k == 0,
                                   stop=k == KT - 1)
                mm.then_inc(sem("r_mm"), 1)

            pe.wait_ge(sem("merged"), KT * 3)
            for h in range(2):
                pe.wait_ge(sem("wo_in"), 16 * (h + 1))
                for n in range(NTT):
                    m, q = rows_of(n), NTT * h + n
                    if q >= 3:
                        pe.wait_ge(sem("out_ev"), q - 2)
                    for k in range(KT):
                        mm = pe.matmul(ps[0:m, q % 3, :], H[:, k, n * P:n * P + m], WO[h][:, k, :], start=k == 0, stop=k == KT - 1)
                    mm.then_inc(sem("out_mm"), 1)
                    if h == 1 and n >= 2:
                        turn(n - 2)
                    if h == 1 and n >= 3:
                        logits(n - 3)
            turn(NTT - 2)
            logits(NTT - 3)
            turn(NTT - 1)
            logits(NTT - 2)
            logits(NTT - 1)
            pe.wait_ge(sem("choices"), 1)
            for n in range(NTT):
                for n0 in range(n + 1):
                    mm = pe.matmul(ps[:, 4, NE * n:NE * (n + 1)], ones if n0 < n else tri, MEMB[:, NE * n0:NE * (n0 + 1)],
                                   start=n0 == 0, stop=n0 == n)
            for n in range(NTT):
                mm = pe.matmul(ps[:, 5, 0:NE], ones, MEMB[:, NE * n:NE * (n + 1)], start=n == 0, stop=n == NTT - 1)
            mm.then_inc(sem("slot_mm"), 1)
            pe.wait_ge(sem("choices"), 2)
            for a in range(2 * NTT):
                mm = pe.matmul(ps[:, 6, 0:NSLOTS], OQ[:, a, :], OS[:, a, :], start=a == 0, stop=a == 2 * NTT - 1)
            mm.then_inc(sem("slot_mm"), 1)

            def turn_rows(s, loaded, free):
                pe.wait_ge(sem(f"xg_in{s}"), loaded)
                if free is not None:
                    pe.wait_ge(sem("xt_ev"), free)
                for k in range(KT):
                    mm = pe.transpose(ps[:, 2 + k // 4, (k % 4) * P:(k % 4 + 1) * P], XG[s][:, k * P:(k + 1) * P], ident)
                mm.then_inc(sem("xt_mm"), 1)

            def slot(i, s, more):
                pe.wait_ge(sem(f"gu_in{s}"), 16 * i + 16)
                pe.wait_ge(sem("xt_ev"), 2 * i + s + 1)
                for q in range(4):
                    for k in range(KT):
                        mm = pe.matmul(ps[:, s, q * P:(q + 1) * P], GU[s][:, k * 4 * P + q * P:k * 4 * P + (q + 1) * P],
                                       XT[s][:, k * P:(k + 1) * P], start=k == 0, stop=k == KT - 1)
                mm.then_inc(sem("gu_mm"), 1)
                if more:
                    turn_rows(1 - s, 16 * i + 16 + 16 * s, None)
                pe.wait_ge(sem(f"dn_in{s}"), 16 * i + 16)
                pe.wait_ge(sem("act"), 2 * i + s + 1)
                for h in range(2):
                    for k in range(2):
                        mm = pe.matmul(ps[:, 4 + 2 * s + h, :], ACTB[:, s, k * P:(k + 1) * P],
                                       DN[s][:, k * D + h * HALF:k * D + (h + 1) * HALF], start=k == 0, stop=k == 1)
                    mm.then_inc(sem("dn_mm"), 1)

            turn_rows(0, 16, None)
            with pe.Fori(0, NSLOTS // 2 - 1) as i:
                for s in range(2):
                    slot(i, s, True)
            slot(NSLOTS // 2 - 1, 0, True)
            slot(NSLOTS // 2 - 1, 1, False)

        @block.scalar
        def _(act):
            A = nc.scalar.activation
            roots = [0]

            def inverse_root(dst, src, name):
                roots[0] += 1
                A(dst, src, ACT.Ln).then_inc(sem("logs"), 1)
                act.wait_ge(sem("logs"), roots[0])
                A(dst, dst, ACT.Exp, scale=-0.5).then_inc(sem(name), 1)

            for k in range(KT):
                if k >= 2:
                    act.wait_ge(sem("norm_sum"), k - 1)
                if k % 4 == 0:
                    act.wait_ge(sem(f"x_in{k // 4}"), 16)
                A(sq[:, k % 2, :], x_t[:, k, :], ACT.Square).then_inc(sem("norm_sq"), 1)
            act.wait_ge(sem("norm_var"), 1)
            inverse_root(RS0, RS0, "norm_std")

            def evac(n, m):
                for c in range(NCH):
                    act.wait_ge(sem("dense"), m + c + 1)
                    act.wait_ge(sem("small_in"), 16)
                    A(PR[:, bass.ds(n, 1), PAD + c * CW:PAD + (c + 1) * CW], ps[:, c, 0:CW].unsqueeze(1), ACT.Copy
                      ).then_inc(sem("evac"), 1)

            evac(S_R, 0)
            with act.Fori(0, 3) as j:
                evac(2 * j + S_R + 1, 6 * j + 3)
                evac(2 * j + S_R + 2, 6 * j + 6)
            with act.Fori(3, 6) as j:
                evac(2 * j - 6, 6 * j + 3)
                evac(2 * j - 5, 6 * j + 6)
            act.wait_ge(sem("lerp"), 7)
            A(PR[0:32, S_LORA, PAD:], PR[0:32, S_LORA, PAD:], ACT.Tanh).then_inc(sem("lora_act"), 1)
            A(PR[64:128, S_LORA, PAD:], PR[64:128, S_LORA, PAD:], ACT.Sigmoid).then_inc(sem("lora_act"), 1)
            for t in range(2):
                A(TM[:, t, :], row(S_K + t), ACT.Square, scale=v("kkw", t)).then_inc(sem("k_sq"), 1)
            for t in range(2):
                act.wait_ge(sem("evac"), 39)
                A(row(S_CG + t), row(S_CG + t), ACT.Sigmoid).then_inc(sem("glu"), 1)
            for n in range(4):
                act.wait_ge(sem("lora_mm"), n + 1)
                dst, b = ((SG, "w0"), (AA, "a0"))[n // 2]
                A(as3(dst[:, n % 2, :]), ps3(3), ACT.Sigmoid, bias=v(b, n % 2)).then_inc(sem("lora_ev"), 1)
            for t in range(2):
                act.wait_ge(sem("k_ss"), t + 1)
                inverse_root(LL[:, t, :], LL[:, t, :], "k_std")
            with act.Fori(6, 10) as j:
                evac(2 * j - 6, 6 * j + 3)
                evac(2 * j - 5, 6 * j + 6)
            for t in range(2):
                act.wait_ge(sem("cum"), t + 1)
                act.wait_ge(sem("bonus"), 2)
                A(TM[:, t, 0:TP], LL[:, t, 0:TP], ACT.Exp, scale=-DECAY_SCALE).then_inc(sem("dec_p"), 1)
            A(smp[:, 5, :, :], smp[:, 5, :, :], ACT.Exp, scale=-DECAY_SCALE).then_inc(sem("pre_act"), 1)
            for t in range(2):
                act.wait_ge(sem("dec_lm"), t + 1)
                A(SG[:, t, 0:TP], SG[:, t, 0:TP], ACT.Exp, scale=-DECAY_SCALE).then_inc(sem("dec_q"), 1)
                A(AA[:, t, 0:TP], LL[:, t, 0:TP], ACT.Exp, scale=DECAY_SCALE).then_inc(sem("dec_q"), 1)
            for t in range(2):
                act.wait_ge(sem("pool_mm"), t + 1)
                A(as3(row(S_POOL + t)), ps3(0), ACT.Copy, scale=v("pool_scale", t)).then_inc(sem("pool_ev"), 1)
            act.wait_ge(sem("dt_neg"), 1)
            A(da_t[:, :, :], da_t[:, :, :], ACT.Exp).then_inc(sem("pre_act"), 1)
            act.wait_ge(sem("pre_act"), 2)
            A(da_t[:, :, :], da_t[:, :, :], ACT.Ln, bias=1.0).then_inc(sem("pre_act"), 1)
            A(smallv[:, 0:4], v("a_log", 0, 4), ACT.Exp).then_inc(sem("pre_act"), 1)
            act.wait_ge(sem("xs_pre"), 1)
            A(XSS, XS, ACT.Sigmoid).then_inc(sem("pre_act"), 1)
            act.wait_ge(sem("evac"), 3 * NSLOT)
            A(dsm[:, 8:10, 0:8], PR[:, S_Z:S_Z + 2, PAD + TP:PAD + T], ACT.Sigmoid).then_inc(sem("pre_act"), 1)
            act.wait_ge(sem("dt_bcc"), 1)
            A(dsm[:, 2:4, 0:8], dsm[:, 2:4, 0:8], ACT.Exp).then_inc(sem("pre_act"), 1)

            act.wait_ge(sem("pre_done"), 1)
            def spread(i):
                for w, src in enumerate((kk, PR)):
                    for h in range(2):
                        a = (kk[64 * h:64 * h + 64, :, bass.ds(i * SC, SC)] if w == 0 else
                             PR[64 * h:64 * h + 64, S_R:S_R + 2, bass.ds(i * SC + PAD, SC)])
                        ins_ = A(KR[64 * h:64 * h + 64, :, w, 64 * h:64 * h + 64].rearrange("p (c t) j -> p c t j", c=2),
                                 a.rearrange("p t (c j) -> p c t j", c=2), ACT.Copy)
                ins_.then_inc(sem("kr"), 1)

            def turn(i, more):
                fill = [(j, c) for j in range(4) for c in range(NCH)]
                done = [0]

                def filler(k=1):
                    for _ in range(k):
                        done[0] += 1
                        if done[0] % 2:
                            continue
                        j, c = fill.pop(0)
                        act.wait_ge(sem("dense"), 12 * i + 3 * NSLOT + 3 * j + c + 1)
                        act.wait_ge(sem(f"gate_out{c}"), 16 * (4 * i + j + 1))
                        A(stage[:, c, :], ps[:, c, 0:CW], ACT.Sigmoid).then_inc(sem("evac"), 1)

                act.wait_ge(sem("prod"), 5 * i + 1)
                A(NL.rearrange("p a b -> p (a b)"), ps[:, 3, :], ACT.Copy).then_inc(sem("nl"), 1)
                filler()
                for n, dst in enumerate((VT, BTT, KTT)):
                    act.wait_ge(sem("turned"), 3 * i + n + 1)
                    A(dst.rearrange("p a b -> p (a b)"), ps[:, 3 + n, :], ACT.Copy).then_inc(sem("turn_c"), 1)
                filler()
                for l in range(5):
                    act.wait_ge(sem("x1"), 5 * i + l + 1)
                    A(X1.rearrange("p a b -> p (a b)"), ps[:, 6, :], ACT.Copy).then_inc(sem("x1c"), 1)
                    filler(2)
                for c2 in range(2):
                    filler(2)
                    for t in range(2):
                        act.wait_ge(sem("yy"), 4 * i + 2 * c2 + t + 1)
                        A(tick[:, 2 * c2 + t:2 * c2 + t + 1], cst[:, 0:1], ACT.Copy)
                        for h in range(2):
                            ins_ = A(PR[64 * h:64 * h + 64, S_R + t:S_R + t + 1, bass.ds(i * SC + c2 * RC + PAD, RC)],
                                     ps[64 * h:64 * h + 64, 6 + t:7 + t, 64 * h:64 * h + 64], ACT.Copy)
                        ins_.then_inc(sem("y_ev"), 1)
                    filler()
                act.wait_ge(sem("xc_raw"), i + 1)
                A(SX, XC, ACT.Sigmoid).then_inc(sem("sx"), 1)
                A(SZ, PR[:, S_Z:S_Z + 2, bass.ds(i * SC + PAD, SC)], ACT.Sigmoid).then_inc(sem("sx"), 1)
                filler()
                act.wait_ge(sem("s1"), 4 * i + 1)
                A(ACB.rearrange("p a b -> p (a b)"), ps[:, 3, :], ACT.Copy).then_inc(sem("acb"), 1)
                act.wait_ge(sem("s1"), 4 * i + 4)
                A(BTOK.rearrange("p a b -> p (a b)"), ps[:, 6, 0:2 * P], ACT.Copy).then_inc(sem("btok"), 1)
                act.wait_ge(sem("acb"), i + 1)
                A(EA, ACB, ACT.Exp).then_inc(sem("ea"), 1)
                act.wait_ge(sem("seg"), i + 1)
                A(EE, EE, ACT.Exp).then_inc(sem("ea"), 1)
                A(TE, TE, ACT.Exp).then_inc(sem("ea"), 1)
                if more:
                    spread(i + 1)
                filler(24 - done[0])

            spread(0)
            with act.Fori(0, NITER - 1) as i:
                turn(i, True)
            turn(NITER - 1, False)

            act.wait_ge(sem("st_out"), 32)
            for t in range(2):
                A(V5[:, t, :], row(S_Z + t), ACT.Square).then_inc(sem("br_sq"), 1)
            for t in range(2):
                act.wait_ge(sem("gn_ctr"), t + 1)
                A(V2[:, t, :], V1[:, t, :], ACT.Square).then_inc(sem("br_sq"), 1)
            for t in range(2):
                act.wait_ge(sem("ln_ctr"), t + 1)
                A(V4[:, t, :], V3[:, t, :], ACT.Square).then_inc(sem("br_sq"), 1)
            act.wait_ge(sem("sm_var"), 1)
            inverse_root(V5[:, 0, :], V5[:, 0, :], "br_std")
            for t in range(2):
                act.wait_ge(sem("gn_v"), t + 1)
                inverse_root(V2[:, t, :], V2[:, t, :], "br_std")
            act.wait_ge(sem("ln_v"), 1)
            inverse_root(V4[:, 0, :], V4[:, 0, :], "br_std")
            act.wait_ge(sem("ln_aff"), 2)
            for t in range(2):
                A(V4[:, t, :], V3[:, t, :], ACT.Sigmoid).then_inc(sem("br_std"), 1)
            def turned_out(n):
                m, b = rows_of(n), 4 + 2 * (n % 2)
                act.wait_ge(sem("h2_turn"), n + 1)
                if n >= 2:
                    act.wait_ge(sem("r_mm"), n - 1)
                A(HF[:, n % 2, :, 0:m].rearrange("p (a k) m -> p a k m", a=2),
                  ps[:, b:b + 2, :].rearrange("p a (k m) -> p a k m", k=4)[:, :, :, 0:m], ACT.Copy).then_inc(sem("hf_ev"), 1)

            def norm_row(n, done):
                m = rows_of(n)
                act.wait_ge(*done)
                if n:
                    act.wait_ge(sem("row_sq"), n)
                A(STG[0:m, 0:D], X2[0:m, n, :], ACT.Square, accum_out=SS[0:m, n:n + 1]).then_inc(sem("row_sq"), 1)
                act.wait_ge(sem("rs_v"), n + 1)
                A(RSTD[0:m, n:n + 1], RSTD[0:m, n:n + 1], ACT.Sqrt).then_inc(sem("rs_s"), 1)

            for n in range(NTT):
                norm_row(n, (sem("out_ev"), NTT + n + 1))
                if n >= 2:
                    turned_out(n - 2)
            turned_out(NTT - 2)
            turned_out(NTT - 1)
            act.wait_ge(sem("r_pre"), 1)
            A(q4[2], q4[2], ACT.Exp).then_inc(sem("r_exp"), 1)
            act.wait_ge(sem("r_pre"), 2)
            A(q1[4], q1[4], ACT.Exp).then_inc(sem("r_exp"), 1)

            def rows_turned(s, n):
                act.wait_ge(sem("xt_mm"), n)
                A(XT[s], ps[:, 2:4, :].rearrange("p a b -> p (a b)"), ACT.Copy).then_inc(sem("xt_ev"), 1)

            def slot(i, s, more):
                act.wait_ge(sem("gu_mm"), 2 * i + s + 1)
                A(SIL[:, s, :], ps[:, s, 0:2 * P], ACT.Silu).then_inc(sem("silu"), 1)
                if more:
                    rows_turned(1 - s, 2 * i + s + 2)
                act.wait_ge(sem("dn_mm"), 4 * i + 2 * s + 1)
                act.wait_ge(sem(f"yo_out{s}"), 16 * i + 16)
                A(YO[s][:, 0:HALF], ps[:, 4 + 2 * s, :], ACT.Copy).then_inc(sem("yo_act"), 1)

            rows_turned(0, 1)
            with act.Fori(0, NSLOTS // 2 - 1) as i:
                for s in range(2):
                    slot(i, s, True)
            slot(NSLOTS // 2 - 1, 0, True)
            slot(NSLOTS // 2 - 1, 1, False)
            for n in range(NTT):
                m = rows_of(n)
                act.wait_ge(sem("comb"), n + 1)
                act.wait_ge(sem("row_sq"), NTT + n)
                A(STG[0:m, 0:D], X2[0:m, n, :], ACT.Square, accum_out=SS[0:m, n:n + 1]).then_inc(sem("row_sq"), 1)
                act.wait_ge(sem("rs_v"), NTT + n + 1)
                A(RSTD[0:m, n:n + 1], RSTD[0:m, n:n + 1], ACT.Sqrt).then_inc(sem("rs_s"), 1)

        @block.vector
        def _(dve):
            link = Link(dve, sem("dve_self"))
            tt, ts, stt = nc.vector.tensor_tensor, nc.vector.tensor_scalar, nc.vector.scalar_tensor_tensor
            MUL, ADD, SUB, MAX, MIN, EQ = ALU.mult, ALU.add, ALU.subtract, ALU.max, ALU.min, ALU.is_equal

            dve.wait_ge(sem("small_in"), 16 * NSMALL_IN)
            dve.wait_ge(sem("norm_sum"), KT)
            ts(as3(RS0), ps3(0), 1.0 / D, NORM_EPS, MUL, ADD).then_inc(sem("norm_var"), 1)
            dve.wait_ge(sem("norm_std"), 1)
            for k in range(KT):
                ins_ = stt(H[:, k, :], x_t[:, k, :], v("g_mix", k), RS0, MUL, MUL)
            ins_.then_inc(sem("h_ready"), 1)
            ts(smallv[:, 4:6], v("ka", 0, 2), -1.0, 1.0, MUL, ADD)

            dve.wait_ge(sem("evac"), 21)
            dve.wait_ge(sem("pads"), 1)
            dve.wait_ge(sem("h_ready"), 1)
            nc.vector.tensor_copy(shift_out[:, :, :], PR[:, S_R:S_R + 7, PAD + TP - 1:]).then_inc(sem("shift_saved"), 1)
            dve.wait_ge(sem("shift_saved"), 1)
            for t in range(7):
                s = S_R + t
                tt(TM[:, t % 2, 0:TP], PR[:, s, PAD - 1:PAD + TP - 1], row(s, 0, TP), SUB)
                link(tt(TM[:, t % 2, TP:T], shift_in[:, t, :], row(s, TP, T), SUB))
                stt(row(s), TM[:, t % 2, :], v("mu", t), row(s), MUL, ADD).then_inc(sem("lerp"), 1)
            dve.wait_ge(sem("lerp"), 7)
            for t in range(2):
                dve.wait_ge(sem("head_sum"), t + 1)
                ts(as3(LL[:, t, :]), ps3(3), 1e-24, None, MAX).then_inc(sem("k_ss"), 1)
            for t in range(2):
                dve.wait_ge(sem("k_std"), t + 1)
                stt(kk[:, t, :], row(S_K + t, 0, TP), v("kkw", t), LL[:, t, 0:TP], MUL, MUL)
                stt(smp[:, 3, t, :], row(S_K + t, TP, T), v("kkw", t), LL[:, t, TP:T], MUL, MUL)
            dve.wait_ge(sem("lora_ev"), 4)
            link(nc.vector.tensor_copy(smp[:, 5, :, :], SG[:, :, TP:T]))
            for t in range(2):
                tt(bb[:, t, :], kk[:, t, :], AA[:, t, 0:TP], MUL)
                link(tt(smp[:, 4, t, :], smp[:, 3, t, :], AA[:, t, TP:T], MUL))
                link(ts(AA[:, t, :], AA[:, t, :], v("ka", t), smallv[:, 4 + t:5 + t], MUL, ADD))
                link(tt(row(S_K + t), row(S_K + t), AA[:, t, :], MUL))
                stt(TM[:, t, :], row(S_R + t), v("rk", t), row(S_K + t), MUL, MUL).then_inc(sem("rk_prod"), 1)
            nc.vector.tensor_copy(smp[:, 0:3, :, :], rows(S_R, 6, TP, T).rearrange("p (a b) c -> p a b c", a=3))
            dve.wait_ge(sem("reset"), 1)
            for t in range(2):
                nc.vector.tensor_tensor_scan(LL[:, t, 0:TP], RESET, SG[:, t, 0:TP], 0.0, MUL, ADD).then_inc(sem("cum"), 1)
            dve.wait_ge(sem("cum"), 2)
            dve.wait_ge(sem("glu"), 2)
            for t in range(2):
                tt(row(S_CA + t), row(S_CA + t), row(S_CG + t), MUL).then_inc(sem("c_ready"), 1)
            dve.wait_ge(sem("c_ready"), 2)
            link(nc.vector.tensor_copy(conv_h[:, :, :, CONVK - 1], rows(S_CA, 2, TP, T)))
            for t in range(2):
                link(tt(CHW, conv_h[:, t, :, :], mid(v("conv_w", t * CONVK, CONVK), NSMP), MUL))
                link(nc.vector.tensor_reduce(row(S_CG + t, TP, T), CHW, AX, ADD))
                link(ts(row(S_CG + t, TP, T), row(S_CG + t, TP, T), v("conv_b", t), None, ADD))
            for j in range(CONVK):
                for t in range(2):
                    w = v("conv_w", t * CONVK + j)
                    src, dst = PR[:, S_CA + t, j:j + TP], row(S_CG + t, 0, TP)
                    ins_ = ts(dst, src, w, v("conv_b", t), MUL, ADD) if j == 0 else stt(dst, src, w, dst, MUL, ADD)
                link(ins_)
            dve.wait_ge(sem("c_out"), 16)
            for t in range(2):
                dve.wait_ge(sem("head_sum"), t + 3)
                tt(as3(row(S_CA + t)), ps3(3), as3(row(S_V + t)), MUL).then_inc(sem("bonus"), 1)
            for t in range(2):
                tt(SG[:, t, 0:TP], LL[:, t, 0:TP], SG[:, t, 0:TP], SUB).then_inc(sem("dec_lm"), 1)
            for t in range(2):
                dve.wait_ge(sem("dec_p"), t + 1)
                tt(row(S_R + t, 0, TP), row(S_R + t, 0, TP), TM[:, t, 0:TP], MUL)
                nc.vector.tensor_copy(pc[:, t, :], TM[:, t, RC - 1:TP:RC])
            for t in range(2):
                dve.wait_ge(sem("dec_q"), 2 * t + 1)
                tt(kk[:, t, :], kk[:, t, :], SG[:, t, 0:TP], MUL)
                dve.wait_ge(sem("dec_q"), 2 * t + 2)
                tt(bb[:, t, :], bb[:, t, :], AA[:, t, 0:TP], MUL)
                tt(row(S_K + t, 0, TP), row(S_K + t, 0, TP), AA[:, t, 0:TP], MUL).then_inc(sem("rw_pre"), 1)
            dve.wait_ge(sem("rw_pre"), 2)
            dve.wait_ge(sem("pool_diff"), 2)

            link(nc.vector.memset(dt_t[:, :, :], 0.0))
            dve.wait_ge(sem("dt_mm"), 1)
            tt(dt_t[:, 0:8, :], ps[:, 6, 0:32].rearrange("p (a b) -> p a b", a=8), mid(v("dt_bias", 0, 4), 8), ADD)
            tt(dt_t[0:NSMP, 8, :], ps[0:NSMP, 6, 32:36], vec[0:NSMP, VEC["dt_bias"][0]:VEC["dt_bias"][0] + 4], ADD
               ).then_inc(sem("dt_read"), 1)
            dve.wait_ge(sem("dt_read"), 1)
            stt(da_t[:, :, :], dt_t[:, :, :], -1.0, dt_t[:, :, :], MUL, MIN).then_inc(sem("dt_neg"), 1)
            nc.vector.tensor_copy(ssm_h[:, :, :, SSMK - 1], rows(S_XBC, 6, TP, T)).then_inc(sem("ssm_h"), 1)
            dve.wait_ge(sem("ssm_h"), 1)
            link(tt(XSW, ssm_h[:, :, :, :], v("ssm_w", 0, 24).rearrange("p (a b) -> p a b", a=6).unsqueeze(2).to_broadcast([P, 6, NSMP, SSMK]), MUL))
            link(nc.vector.tensor_reduce(XS, XSW, AX, ADD))
            tt(XS, XS, last(v("ssm_b", 0, 6), NSMP), ADD).then_inc(sem("xs_pre"), 1)

            dve.wait_ge(sem("pre_act"), 1)
            im = cc("imask").unsqueeze(1).unsqueeze(1).to_broadcast([P, NSMP, 2, HD])

            def by_b(a):
                return a.rearrange("p t b -> p b t")

            def x_exp(n):
                if n >= 2:
                    dve.wait_ge(sem("x_bc"), n - 1)
                tt(XE[n % 2], last(by_b(smp[:, (3, 5, 4, 1, 0)[n], :, :]), HD), im, MUL).then_inc(sem("x_exp"), 1)

            def x_bc(n):
                dve.wait_ge(sem("x_bc"), n + 1)
                b = 3 + 2 * (n % 2)
                return ps[:, b:b + 2, :].rearrange("p a (b c d) -> p (a b) c d", b=4, c=2)

            W = W2[:, 0:4, :, :].rearrange("p a b (c d) -> p (a b c) d", c=2).rearrange("p (a b) d -> p a b d", b=2)
            sa_s = dsm[:, 10, :].rearrange("p (a b) -> p a b", b=2)
            dve.wait_ge(sem("states_in"), 32)
            x_exp(0)
            x_exp(1)
            link(tt(W, SW, x_bc(0), MUL))
            nc.vector.tensor_reduce(sa_s, W, AX, ADD).then_inc(sem("x_use"), 1)
            x_exp(2)
            tt(SW, SW, x_bc(1), MUL).then_inc(sem("x_use"), 1)
            x_exp(3)
            dve.wait_ge(sem("x_use"), 2)
            link(tt(W, x_bc(2), last(sa_s, HD), MUL))
            tt(SW, SW, W, SUB).then_inc(sem("x_use"), 1)
            x_exp(4)
            dve.wait_ge(sem("x_use"), 3)
            link(tt(W, x_bc(3), last(by_b(smp[:, 2, :, :]), HD), MUL))
            tt(SW, SW, W, ADD).then_inc(sem("x_use"), 1)
            dve.wait_ge(sem("x_use"), 4)
            tt(W, SW, x_bc(4), MUL).then_inc(sem("x_use"), 1)
            dve.wait_ge(sem("x_use"), 5)
            link(nc.vector.tensor_reduce(by_b(rows(S_R, 2, TP, T)), W, AX, ADD))

            dve.wait_ge(sem("pre_act"), 5)
            link(tt(XS, XS, XSS, MUL))
            idn = ident.unsqueeze(1).unsqueeze(1).to_broadcast([P, NSMP, 2, P])
            tt(BE, last(by_b(XS[:, 2:4, :]), P), idn, MUL).then_inc(sem("bc_exp"), 1)
            dve.wait_ge(sem("pre_act"), 3)
            link(stt(dt_t[:, :, :], dt_t[:, :, :], 0.0, da_t[:, :, :], MAX, ADD))
            dve.wait_ge(sem("pre_act"), 4)
            stt(da_t[:, :, :], dt_t[:, :, :], -1.0, mid(smallv[:, 0:4], 9), MUL, MUL).then_inc(sem("dta"), 1)
            dve.wait_ge(sem("dt_bc"), 1)
            for q in range(2):
                for h in range(2):
                    src = ps[64 * h:64 * h + 64, 7, 32 * q:32 * q + 32].rearrange("p (g h b) -> p h g b", g=2, h=2)[:, h, :, :]
                    ins_ = nc.vector.tensor_copy(dsm[64 * h:64 * h + 64, 2 * q:2 * q + 2, 0:8], src)
            ins_.then_inc(sem("dt_bcc"), 1)
            dve.wait_ge(sem("dt_bcc"), 1)
            link(tt(dsm[:, 4:6, 0:8], dsm[:, 0:2, 0:8], XS[:, 0:2, :], MUL))
            dve.wait_ge(sem("pre_act"), 7)
            link(tt(SH, SH, last(by_b(dsm[:, 2:4, 0:8]), P), MUL))
            dve.wait_ge(sem("bc_bc"), 1)
            spread = ps[:, 0:4, :].rearrange("p a (b c d) -> p (a b) c d", b=2, c=2)
            link(tt(W2, spread, last(by_b(dsm[:, 4:6, 0:8]), P), MUL))
            tt(BE, last(by_b(XS[:, 4:6, :]), P), idn, MUL).then_inc(sem("bc_exp"), 1)
            link(tt(SH, SH, W2, ADD))
            dve.wait_ge(sem("bc_bc"), 2)
            link(tt(W2, SH, spread, MUL))
            link(nc.vector.tensor_reduce(by_b(dsm[:, 6:8, 0:8]), W2, AX, ADD))
            for g in range(2):
                link(stt(dsm[:, 6 + g, 0:8], XS[:, g, :], v("ssm_d", g), dsm[:, 6 + g, 0:8], MUL, ADD))
            dve.wait_ge(sem("pre_act"), 6)
            link(tt(dsm[:, 6:8, 0:8], dsm[:, 6:8, 0:8], rows(S_Z, 2, TP, T), MUL))
            tt(rows(S_Z, 2, TP, T), dsm[:, 6:8, 0:8], dsm[:, 8:10, 0:8], MUL).then_inc(sem("smp_done"), 1)
            dve.wait_ge(sem("s_out"), 32)
            for n, (name, ahead) in enumerate((("ssm_fin", 2), ("y_ev", 1))):
                nc.vector.memset(scr[:, 1280 * n:1280 * (n + 1)], 0.0).then_inc(sem(name), ahead)
            nc.vector.memset(ST, 0.0).then_inc(sem("st"), 2)
            nc.vector.memset(HT, 0.0).then_inc(sem("pre_done"), 1)
            dve.wait_ge(sem("pre_done"), 1)

            with dve.Fori(0, NITER) as i:
                link.enter(i, PER_TURN)
                nc.vector.tensor_copy(PCS, pc[:, :, bass.ds(2 * i, 2)])
                nc.vector.tensor_copy(DTI, dt_t[:, bass.ds(i, 1), :].rearrange("p a b -> p (a b)"))
                nc.vector.tensor_copy(DAI, da_t[:, bass.ds(i, 1), :].rearrange("p a b -> p (a b)"))
                for n in range(4):
                    dve.wait_ge(sem("prod"), 5 * i + 2 + n)
                    m = cc("m_lev1_incl" if n < 2 else "m_strict_incl")
                    dst = (BM, MK)[n // 2][:, 2 * (n % 2):2 * (n % 2) + 2, :, :].rearrange("p a b c -> p a (b c)")
                    tt(dst, ps[:, 4 + n, :].rearrange("p (a b) -> p a b", a=2), mid(m, 2), MUL).then_inc(sem("masked"), 1)
                dve.wait_ge(sem("nl"), i + 1)
                link(tt(TT, NL, mid(cc("m_lev1_low"), 4), MUL))
                tt(TT, TT, mid(ident, 4), ADD)
                tt(U, BM[:, :, 0, :], mid(ident, 4), ADD)
                tt(NLB, NL, mid(cc("m_lev_low", 0, P), 4), MUL).then_inc(sem("lev"), 1)
                for l in range(5):
                    dve.wait_ge(sem("du"), 5 * i + l + 1)
                    ins_ = tt(U, U, ps[:, 7, :].rearrange("p (a b) -> p a b", a=4), SUB)
                    if l < 4:
                        dve.wait_ge(sem("dt_"), 4 * i + l + 1)
                        tt(TT, TT, ps[:, 3, :].rearrange("p (a b) -> p a b", a=4), SUB)
                        tt(NLB, NL, mid(cc("m_lev_low", (l + 1) * P, P), 4), MUL).then_inc(sem("lev"), 1)
                        for t in range(6):
                            w = v("ssm_w", t * SSMK + l)
                            src = PR[:, S_XBC + t, bass.ds(i * SC + PAD - (SSMK - 1) + l, SC)]
                            ins_ = (ts(XC[:, t, :], src, w, v("ssm_b", t), MUL, ADD) if l == 0 else
                                    stt(XC[:, t, :], src, w, XC[:, t, :], MUL, ADD))
                        if l < SSMK - 1:
                            link(ins_)
                        else:
                            ins_.then_inc(sem("xc_raw"), 1)
                    else:
                        ins_.then_inc(sem("u_done"), 1)
                for c2 in range(2):
                    for t in range(2):
                        dve.wait_ge(sem("xx"), 4 * i + 2 * c2 + t + 1)
                        ts(XN[:, t, :], ps[:, 4 + t, 0:P], -1.0, None, MUL).then_inc(sem("xn"), 1)
                    for t in range(2):
                        dve.wait_ge(sem("sa"), 4 * i + 2 * c2 + t + 1)
                        nc.vector.tensor_copy(SA[:, t, :], ps[:, 4 + t, P:2 * P]).then_inc(sem("sac"), 1)
                    for t in range(2):
                        dve.wait_ge(sem("ss"), 4 * i + 2 * c2 + t + 1)
                        ts(ST[:, t, :], ps[:, 4 + t, 2 * P:3 * P], PCS[:, t, c2:c2 + 1], None, MUL).then_inc(sem("st"), 1)
                dve.wait_ge(sem("xc_raw"), i + 1)
                dve.wait_ge(sem("sx"), 2 * i + 1)
                tt(XC, XC, SX, MUL).then_inc(sem("xc"), 1)
                dve.wait_ge(sem("s1"), 4 * i + 2)
                nc.vector.tensor_copy(AT, ps[:, 4, 0:4])
                link(tt(GM, ps[:, 4, P:3 * P].rearrange("p (a b) -> p a b", a=2), mid(tri, 2), MUL))
                dve.wait_ge(sem("acb"), i + 1)
                for hh in range(4):
                    ts(EE[:, hh, :], ACB[:, hh, :], AT[:, hh:hh + 1], 0.0, SUB, MIN)
                tt(TE, ACB[:, :, SC - 1], AT, SUB).then_inc(sem("seg"), 1)
                dve.wait_ge(sem("s1"), 4 * i + 3)
                link(tt(XDT.rearrange("p a (b c) -> p (a b) c", b=2), ps[:, 5, 0:2 * P].rearrange("p (a b) -> p a b", a=4),
                        last(DTI, HD), MUL))
                dve.wait_ge(sem("ea"), 3 * i + 1)
                link(nc.vector.tensor_copy(DEC, EA[:, :, SC - 1]))
                cb = XC[:, 4:6, :].unsqueeze(2).to_broadcast([P, 2, 2, SC])
                tt(EA.rearrange("p (a b) c -> p a b c", a=2), EA.rearrange("p (a b) c -> p a b c", a=2), cb, MUL)
                dve.wait_ge(sem("ea"), 3 * i + 3)
                gmb = GM.unsqueeze(2).to_broadcast([P, 2, 2, SC])
                tt(EE.rearrange("p (a b) c -> p a b c", a=2), EE.rearrange("p (a b) c -> p a b c", a=2), gmb, MUL)
                tt(XTE.rearrange("p a (b c) -> p (a b) c", b=2), XDT.rearrange("p a (b c) -> p (a b) c", b=2), last(TE, HD), MUL
                   ).then_inc(sem("sl"), 1)
                dve.wait_ge(sem("sy"), i + 1)
                for g in range(2):
                    ins_ = stt(XC[:, g, :], XC[:, g, :], v("ssm_d", g), ps[:, 7, g * P:(g + 1) * P], MUL, ADD)
                link(ins_)
                zc = PR[:, S_Z:S_Z + 2, bass.ds(i * SC + PAD, SC)]
                link(tt(XC[:, 0:2, :], XC[:, 0:2, :], zc, MUL))
                dve.wait_ge(sem("sx"), 2 * i + 2)
                tt(zc, XC[:, 0:2, :], SZ, MUL).then_inc(sem("ssm_fin"), 1)
                dve.wait_ge(sem("sh"), i + 1)
                for hh in range(4):
                    hv = HT[:, hh // 2, 64 * (hh % 2):64 * (hh % 2) + 64]
                    ins_ = stt(hv, hv, DEC[:, hh:hh + 1], ps[:, 3, 64 * hh:64 * hh + 64], MUL, ADD)
                ins_.then_inc(sem("ssm_fin"), 1)
                dve.wait_ge(sem("ssm_fin"), 2 * i + 4)
            link.leave(NITER)

            dve.wait_ge(sem("st_out"), 32)
            for t in range(2):
                dve.wait_ge(sem("br_sum"), t + 1)
                stt(as3(V1[:, t, :]), ps3(3 * t), -1.0 / HD, as3(row(S_R + t)), MUL, ADD).then_inc(sem("gn_ctr"), 1)
            dve.wait_ge(sem("br_sum"), 3)
            for t in range(2):
                stt(as3(V3[:, t, :]), ps3(0), -1.0 / (2 * P), as3(row(S_CG + t)), MUL, ADD).then_inc(sem("ln_ctr"), 1)
            dve.wait_ge(sem("br_sum"), 4)
            ts(as3(V5[:, 0, :]), ps3(3), 1.0 / (2 * P), NORM_EPS, MUL, ADD).then_inc(sem("sm_var"), 1)
            for t in range(2):
                dve.wait_ge(sem("br_sum"), t + 5)
                ts(as3(V2[:, t, :]), ps3(3 * t), 1.0 / HD, GN_EPS, MUL, ADD).then_inc(sem("gn_v"), 1)
            dve.wait_ge(sem("br_sum"), 7)
            ts(as3(V4[:, 0, :]), ps3(0), 1.0 / (2 * P), LN_EPS, MUL, ADD).then_inc(sem("ln_v"), 1)
            dve.wait_ge(sem("br_std"), 1)
            for t in range(2):
                ins_ = stt(row(S_Z + t), row(S_Z + t), v("ssm_g", t), V5[:, 0, :], MUL, MUL)
            ins_.then_inc(sem("br_ready"), 1)
            dve.wait_ge(sem("br_std"), 4)
            for t in range(2):
                link(tt(V3[:, t, :], V3[:, t, :], V4[:, 0, :], MUL))
                ts(V3[:, t, :], V3[:, t, :], v("conv_ln_g", t), v("conv_ln_b", t), MUL, ADD).then_inc(sem("ln_aff"), 1)
            for t in range(2):
                link(tt(V1[:, t, :], V1[:, t, :], V2[:, t, :], MUL))
                link(ts(V1[:, t, :], V1[:, t, :], v("ln_g", t), v("ln_b", t), MUL, ADD))
                link(tt(V1[:, t, :], V1[:, t, :], row(S_CA + t), ADD))
                dve.wait_ge(sem("br_sum"), t + 8)
                tt(as3(row(O_RWKV + t)), as3(V1[:, t, :]), ps3(3 - 3 * t), MUL).then_inc(sem("br_ready"), 1)
            dve.wait_ge(sem("br_std"), 6)
            for t in range(2):
                ins_ = tt(row(S_CG + t), V3[:, t, :], V4[:, t, :], MUL)
            ins_.then_inc(sem("br_ready"), 1)

            for dt in range(KT):
                if dt:
                    dve.wait_ge(sem("merged"), 3 * dt)
                dve.wait_ge(sem(f"gb_in{dt % 2}"), 16 * (dt // 2 + 1))
                for b in range(BR):
                    for c in range(NCH):
                        m = 12 * dt + 3 * b + c
                        dve.wait_ge(sem("up_mm"), m + 1)
                        dst = H[:, dt, chunk(c)]
                        gate = GB[dt % 2][:, b, chunk(c)]
                        if b == 0:
                            tt(dst, ps[:, m % 6, 0:CW], gate, MUL).then_inc(sem("up_ev"), 1)
                        else:
                            tt(GP[:, m % 2, :], ps[:, m % 6, 0:CW], gate, MUL).then_inc(sem("up_ev"), 1)
                            dve.wait_ge(sem("up_ev"), m + 1)
                            ins_ = tt(dst, dst, GP[:, m % 2, :], ADD)
                            if b == BR - 1:
                                ins_.then_inc(sem("merged"), 1)
            def norm_row(n, base, gain, dst, sem_name, free):
                m = rows_of(n)
                rs = RSTD[0:m, n:n + 1]
                dve.wait_ge(sem("row_sq"), base + n + 1)
                ts(rs, SS[0:m, n:n + 1], 1.0 / D, NORM_EPS, MUL, ADD).then_inc(sem("rs_v"), 1)
                dve.wait_ge(sem("rs_s"), base + n + 1)
                link(nc.vector.reciprocal(rs, rs))
                for name, value in free:
                    dve.wait_ge(sem(name), value)
                stt(dst[0:m, :], X2[0:m, n, :], rs, GAIN[0:m, gain, :], MUL, MUL).then_inc(sem(sem_name), 1)

            dve.wait_ge(sem("x_re"), 48)
            for h in range(2):
                for n in range(NTT):
                    m, q = rows_of(n), NTT * h + n
                    dve.wait_ge(sem("out_mm"), q + 1)
                    r_ = X2[0:m, n, h * HALF:(h + 1) * HALF]
                    tt(r_, ps[0:m, q % 3, :], r_, ADD).then_inc(sem("out_ev"), 1)
                    if h == 1:
                        norm_row(n, 0, 0, H2[:, n % 2, :], "h2_row",
                                 [("h2_turn", n - 1), (f"h2_out{n % 2}", 16 * (n // 2))] if n >= 2 else [])

            for s in range(2):
                nc.vector.memset(idx_now[:, 4 * s:4 * s + 4], 0).then_inc(sem(f"yo_out{s}"), 16)
            link(nc.vector.memset(LG, 0.0))
            dve.wait_ge(sem("r_mm"), NTT)
            rb = VEC["r_bias"][0]
            tt(LG[:, 0:8, :], ps[:, 3, 0:160].rearrange("p (a b) -> p a b", a=8), mid(vec[:, rb:rb + 20], 8), ADD)
            link(tt(LG[0:NSMP, 8, :], ps[0:NSMP, 3, 160:180], vec[0:NSMP, rb:rb + 20], ADD))
            GL = LG[:, :, 0:4]
            EL = LG[:, :, 4:20].rearrange("p n (g k) -> p n g k", g=4)
            rank = mid(cc("rank4"), 9)

            def first_max(dst, val, top, tmp, mx):
                link(nc.vector.tensor_reduce(top, val, AX, MAX))
                link(tt(tmp, val, last(top, 4), EQ))
                link(tt(tmp, tmp, rank, MUL))
                link(nc.vector.tensor_reduce(mx, tmp, AX, MAX))
                link(tt(dst, tmp, last(mx, 4), EQ))

            first_max(q4[0], GL, q1[0], q4[1], q1[1])
            tt(q4[2], GL, last(q1[0], 4), SUB).then_inc(sem("r_pre"), 1)
            link(tt(EX, EL, last(q4[0], 4), MUL))
            link(nc.vector.tensor_reduce(q4[3], EX.rearrange("p n g k -> p n k g"), AX, ADD))
            first_max(q4[4], q4[3], q1[2], q4[1], q1[1])
            link(stt(q4[3], q4[4], -3e38, q4[3], MUL, ADD))
            first_max(q4[5], q4[3], q1[3], q4[1], q1[1])
            tt(q1[4], q1[3], q1[2], SUB).then_inc(sem("r_pre"), 1)
            link(tt(q4[0], q4[0], last(cc("valid"), 4), MUL))
            for c, choice in enumerate((q4[4], q4[5])):
                ins_ = tt(OH[:, c, :].rearrange("p (n g k) -> p n g k", n=NTT, g=4), last(q4[0], 4),
                          choice.unsqueeze(2).to_broadcast([P, NTT, 4, 4]), MUL)
            link(ins_)
            tt(MEMB, OH[:, 0, :], OH[:, 1, :], ADD).then_inc(sem("choices"), 1)
            dve.wait_ge(sem("r_exp"), 2)
            link(nc.vector.tensor_reduce(q1[5], q4[2], AX, ADD))
            link(ts(q1[6], q1[4], 1.0, None, ADD))
            link(tt(q1[5], q1[5], q1[6], MUL))
            link(nc.vector.reciprocal(q1[5], q1[5]))
            link(tt(q1[6], q1[5], q1[4], MUL))

            dve.wait_ge(sem("slot_mm"), 1)
            GT_, GE, LE = ALU.is_gt, ALU.is_ge, ALU.is_le
            link(tt(CMP.rearrange("p (e j) -> p e j", e=NE), last(ps[:, 5, 0:NE], NTT), mid(cc("count128", 0, NTT), NE), GT_))
            link(nc.vector.tensor_reduce(NB, CMP.rearrange("p (e j) -> p e j", e=NE), AX, ADD))
            link(nc.vector.tensor_tensor_scan(INC, ones[:, 0:NE], NB, 0.0, MUL, ADD))
            link(tt(START, INC, NB, SUB))
            link(ts(START, START, float(P), -1.0, MUL, ADD))
            link(tt(POSE.rearrange("p (n e) -> p n e", n=NTT), ps[:, 4, 0:NTT * NE].rearrange("p (n e) -> p n e", n=NTT),
                    mid(START, NTT), ADD))
            for c in range(2):
                ins_ = tt(OH[:, c, :], OH[:, c, :], POSE, MUL)
            link(ins_)
            link(nc.vector.tensor_reduce(POS, OH.rearrange("p c (n e) -> p (c n) e", n=NTT), AX, ADD))
            link(tt(CMP2, last(POS, NSLOTS), mid(cc("count128"), 2 * NTT), GE))
            link(nc.vector.tensor_reduce(POSS, CMP2[:, :, 1:], AX, ADD))
            link(stt(POSQ, POSS, -float(P), POS, MUL, ADD))
            tt(OQ, last(POSQ, P), mid(cc("count"), 2 * NTT), EQ)
            link(tt(OS, last(POSS, NSLOTS), mid(cc("count", 0, NSLOTS), 2 * NTT), EQ))
            for c in range(2):
                ins_ = tt(OS[:, NTT * c:NTT * (c + 1), :], OS[:, NTT * c:NTT * (c + 1), :], last(cc("token"), NSLOTS), MUL)
            ins_.then_inc(sem("choices"), 1)
            e_cmp = CMP2.rearrange("p a b -> p (a b)")[:, 0:NSLOTS * NE].rearrange("p (s e) -> p s e", s=NSLOTS)
            link(tt(e_cmp, mid(INC, NSLOTS), last(cc("count", 0, NSLOTS), NE), LE))
            link(nc.vector.tensor_reduce(EID, e_cmp, AX, ADD))
            link(ts(EID, EID, float(NE - 1), float(P), MIN, MUL))
            link(ts(EID, EID, cc("part"), None, ADD))
            nc.vector.tensor_copy(IDX_W, EID).then_inc(sem("index"), 1)
            nc.vector.tensor_copy(IDX_Y, POS).then_inc(sem("index"), 1)
            dve.wait_ge(sem("slot_mm"), 2)
            nc.vector.tensor_copy(IDX_T, ps[:, 6, 0:NSLOTS]).then_inc(sem("index"), 1)

            with dve.Fori(0, NSLOTS // 2) as i:
                for s in range(2):
                    dve.wait_ge(sem("silu"), 2 * i + s + 1)
                    tt(ACTB[:, s, :], SIL[:, s, :], ps[:, s, 2 * P:4 * P], MUL).then_inc(sem("act"), 1)
                    dve.wait_ge(sem("dn_mm"), 4 * i + 2 * s + 2)
                    dve.wait_ge(sem(f"yo_out{s}"), 16 * i + 16)
                    nc.vector.tensor_copy(YO[s][:, HALF:D], ps[:, 5 + 2 * s, :]).then_inc(sem("yo_dve"), 1)
            for n in range(NTT):
                m = rows_of(n)
                for c in range(2):
                    dve.wait_ge(sem(f"yg_in{n % 4}"), 32 * (n // 4 + 1))
                    r_ = X2[0:m, n, :]
                    ins_ = stt(r_, YG[n % 4][c][0:m, :], q1[5 + c][0:m, n:n + 1], r_, MUL, ADD)
                    if c == 0:
                        link(ins_)
                    else:
                        ins_.then_inc(sem("comb"), 1)
                if n:
                    norm_row(n - 1, NTT, 1, YB[(n - 1) % 2], "y_ready", [(f"y_out{(n - 1) % 2}", 16 * ((n - 1) // 2))] if n >= 3 else [])
            norm_row(NTT - 1, NTT, 1, YB[(NTT - 1) % 2], "y_ready", [(f"y_out{(NTT - 1) % 2}", 16 * ((NTT - 1) // 2))])

        @block.gpsimd
        def _(pool):
            link = Link(pool, sem("pool_self"))
            tt, ts = nc.gpsimd.tensor_tensor, nc.gpsimd.tensor_scalar
            for dst, name in ((vec, "vec"), (cst, "cst"), (lora_w, "lora_w"), (pool_w, "pool_w"), (w_dt, "w_dt"), (w_r, "w_r"),
                              (shift_in, "shift_in")):
                pool.dma_start(dst[:], ins[name]).then_inc(sem("small_in"), 16)
            for dst, name, n in ((pool_h, "pool_h", POOLH), (conv_h, "conv_h", CONVK - 1), (ssm_h, "ssm_h", SSMK - 1)):
                for t in range(dst.shape[1]):
                    pool.dma_start(dst[:, t, :, 0:n], ins[name][:, t, :, :]).then_inc(sem("small_in"), 16)
            nc.gpsimd.memset(PR[:, :, 0:PAD], 0.0).then_inc(sem("pads"), 1)

            pool.wait_ge(sem("h_ready"), 1)
            link(nc.gpsimd.memset(RESET, 1.0))
            nc.gpsimd.memset(RESET[:, 0:TP:RC], 0.0).then_inc(sem("reset"), 1)
            pool.wait_ge(sem("evac"), 27)
            pool.wait_ge(sem("small_in"), 16 * NSMALL_IN)
            pool.wait_ge(sem("pads"), 1)
            link(nc.gpsimd.tensor_copy(pool_tail[:, :, :], rows(S_POOL, 2, TP - POOLH, TP)))
            link(nc.gpsimd.tensor_copy(pool_h[:, :, :, POOLH], rows(S_POOL, 2, TP, T)))
            end = PAD + TP
            for t in range(2):
                u = PR[:, S_POOL + t, :]
                lo, hi = slice(0, 64), slice(64, 128)
                link(tt(PA[:, 14:end], u[:, 14:end], u[:, 13:end - 1], ALU.add))
                if t == 0:
                    link(tt(PB[hi, 16:end], PA[hi, 16:end], PA[hi, 14:end - 2], ALU.add))
                else:
                    link(tt(PB[:, 16:end], PA[:, 16:end], PA[:, 14:end - 2], ALU.add))
                    link(tt(PA[:, 20:end], PB[:, 20:end], PB[:, 16:end - 4], ALU.add))
                    link(tt(PB[hi, 28:end], PA[hi, 28:end], PA[hi, 20:end - 8], ALU.add))
                for q, src in ((lo, PA), (hi, PB)):
                    m = src[q, PAD:end]
                    head = src[q, PAD:PAD + 16]
                    o = CST["rcount"][0] + 16 * t
                    w = CST["rwin"][0] + t
                    link(ts(src[q, PAD + 16:end], src[q, PAD + 16:end], cst[q, w:w + 1], None, ALU.mult))
                    link(tt(head, head, cst[q, o:o + 16], ALU.mult))
                    link(tt(u[q, PAD:end], m, u[q, PAD:end], ALU.subtract))
                    n = (2, 4, 8, 16)[2 * t + (1 if q is hi else 0)]
                    link(nc.gpsimd.tensor_copy(dsum[q, :], pool_h[q, t, :, 16 - n]))
                    for k_ in range(17 - n, 16):
                        link(tt(dsum[q, :], dsum[q, :], pool_h[q, t, :, k_], ALU.add))
                    link(ts(dsum[q, :], dsum[q, :], cst[q, w:w + 1], None, ALU.mult))
                    ins_ = tt(u[q, end:], dsum[q, :], u[q, end:], ALU.subtract)
                    if q is lo:
                        link(ins_)
                    else:
                        ins_.then_inc(sem("pool_diff"), 1)
                        pool.wait_ge(sem("pool_diff"), t + 1)
            pool.wait_ge(sem("pool_diff"), 2)

            def out(name, src, name_sem="small_out"):
                pool.dma_start(outs[name], src).then_inc(sem(name_sem), 16)

            out("pool_tail", pool_tail[:, :, :])
            for t in range(2):
                pool.dma_start(outs["pool_h"][:, t], pool_h[:, t, :, 1:]).then_inc(sem("small_out"), 16)
            pool.wait_ge(sem("shift_saved"), 1)
            out("shift", shift_out[:, :, :])
            pool.wait_ge(sem("c_ready"), 2)
            out("conv_tail", rows(S_CA, 2, TP - CONVK + 1, TP), "c_out")
            pool.wait_ge(sem("rw_pre"), 2)
            pool.dma_start(SW, ins["wkv"]).then_inc(sem("states_in"), 16)
            pool.dma_start(SH, ins["ssm"]).then_inc(sem("states_in"), 16)
            pool.wait_ge(sem("ssm_h"), 1)
            for t in range(2):
                pool.dma_start(outs["conv_h"][:, t], conv_h[:, t, :, 1:]).then_inc(sem("small_out"), 16)
            for t in range(6):
                pool.dma_start(outs["ssm_h"][:, t], ssm_h[:, t, :, 1:]
                               ).then_inc(sem("small_out" if t >= NCH else f"gate_out{t}"), 16)
            out("ssm_tail", rows(S_XBC, 6, TP - SSMK + 1, TP))
            pool.wait_ge(sem("smp_done"), 1)
            out("wkv_s", SW, "s_out")
            out("ssm_s", SH, "s_out")

            pool.wait_ge(sem("pre_done"), 1)
            def spread(i):
                for dst, src in ((BT, bb), (KTB, S_K), (VV, S_V)):
                    for h in range(2):
                        a = (bb[64 * h:64 * h + 64, :, bass.ds(i * SC, SC)] if src is bb else
                             PR[64 * h:64 * h + 64, src:src + 2, bass.ds(i * SC + PAD, SC)])
                        ins_ = nc.gpsimd.tensor_copy(dst[64 * h:64 * h + 64, :, 64 * h:64 * h + 64].rearrange("p (c t) j -> p c t j", c=2),
                                                     a.rearrange("p t (c j) -> p c t j", c=2))
                ins_.then_inc(sem("bkv"), 1)

            def turn(i, more):
                for j in range(4):
                    if j == 2 and more:
                        pool.wait_ge(sem("turned"), 3 * i + 3)
                        spread(i + 1)
                    for c in range(NCH):
                        pool.wait_ge(sem("evac"), 12 * i + 3 * NSLOT + 3 * j + c + 1)
                        pool.dma_start(gate_scratch[:, bass.ds(4 * i + j, 1), chunk(c)], stage[:, c:c + 1, :]
                                       ).then_inc(sem(f"gate_out{c}"), 16)

            spread(0)
            with pool.Fori(0, NITER - 1) as i:
                turn(i, True)
            turn(NITER - 1, False)
            pool.wait_ge(sem("ssm_fin"), 2 * NITER + 2)
            out("wkv_p", ST, "st_out")
            out("ssm_p", HT, "st_out")
            pool.wait_ge(sem("br_ready"), 4)
            for c in range(NCH):
                pool.wait_ge(sem(f"gate_out{c}"), 16 * (BR * KT + 1))
            for dt in range(KT):
                if dt >= 2:
                    pool.wait_ge(sem("up_ev"), 12 * (dt - 1))
                pool.dma_start(GB[dt % 2], gate_scratch[:, 4 * dt:4 * dt + 4, :]
                               ).then_inc(sem(f"gb_in{dt % 2}"), 16)
                if dt == 1:
                    pool.wait_ge(sem("small_out"), 16 * NSMALL_OUT)
                    pool.dma_start(X2[:, 0:NTT - 1, :], ins["x"][0:TP, :].rearrange("(n p) d -> p n d", p=P)
                                   ).then_inc(sem("x_re"), 16)
                    pool.dma_start(X2[0:NSMP, NTT - 1, :], ins["x"][TP:T, :]).then_inc(sem("x_re"), 16)
                    pool.dma_start(GAIN[:, :, :], ins["gains"]).then_inc(sem("x_re"), 16)

            def gather(dst, src, index, name):
                pool.indirect_dma_start(out=dst, out_offset=None, in_=src,
                                        in_offset=bass.IndirectOffsetOnAxis(ap=index, axis=0)).then_inc(sem(name), 16)

            pool.wait_ge(sem("h2_out0"), 16 * 5)
            pool.wait_ge(sem("h2_out1"), 16 * 4)
            pool.wait_ge(sem("index"), 1)
            pool.wait_ge(sem("index"), 3)
            def index(b, column):
                for o, table in enumerate((IDX_T, IDX_W)):
                    nc.gpsimd.tensor_copy(idx_now[:, 4 * o + b:4 * o + b + 1], table[:, column]).then_inc(sem("idx_set"), 1)

            for q in range(4):
                index(q, slice(q, q + 1))

            def gathers(s, b):
                gather(XG[s], h2_rows, idx_now[:, b:b + 1], f"xg_in{s}")
                gather(GU[s], ins["w_gu"], idx_now[:, 4 + b:5 + b], f"gu_in{s}")
                gather(DN[s], ins["w_dn"], idx_now[:, 4 + b:5 + b], f"dn_in{s}")

            def used(q):
                pool.wait_ge(sem("idx_set"), 2 * q + 2)
                pool.wait_ge(sem("gu_mm"), q - 1)
                pool.wait_ge(sem("dn_mm"), 2 * q - 2)

            for q in range(2):
                pool.wait_ge(sem("idx_set"), 2 * q + 2)
                gathers(q, q)
            with pool.Fori(0, (NSLOTS - 4) // 4) as i:
                for u in range(2, 6):
                    used(4 * i + u)
                    index((u + 2) % 4, bass.ds(4 * i + u + 2, 1))
                    gathers(u % 2, u % 4)
            for q in range(NSLOTS - 2, NSLOTS):
                used(q)
                gathers(q % 2, q % 4)
            pool.wait_ge(sem("index"), 2)
            pool.wait_ge(sem("gu_mm"), NSLOTS)
            for s in range(2):
                pool.wait_ge(sem(f"yo_out{s}"), 16 * (NSLOTS // 2 + 1))
            for n in range(NTT):
                m = rows_of(n)
                if n >= 4:
                    pool.wait_ge(sem("comb"), n - 3)
                for c in range(2):
                    gather(YG[n % 4][c][0:m, :], slot_rows, IDX_Y[0:m, NTT * c + n:NTT * c + n + 1], f"yg_in{n % 4}")


SPECS = [
    ("x_t", (P, KT, T)), ("w_all", (P, N_W, KT * P)), ("vec", (P, NVEC)), ("cst", (P, NCST)), ("lora_w", (P, 2 * P)),
    ("pool_w", (P, 2, P)), ("w_dt", (P, KT, 4)), ("w_r", (P, KT, 20)), ("shift_in", (P, 7, NSMP)),
    ("pool_h", (P, 2, NSMP, POOLH)), ("conv_h", (P, 2, NSMP, CONVK - 1)), ("ssm_h", (P, 6, NSMP, SSMK - 1)),
    ("wkv", (P, NSMP, 2, HD)), ("ssm", (P, NSMP, 2, P)), ("w_gu", (NE * P, KT * 2 * HID)), ("w_dn", (NE * P, 2 * D)),
    ("x", (T, D)), ("gains", (P, 2, D)), ("w_out", (P, 2, KT * HALF)),
]
OUTS = [
    ("y", (T, D)), ("shift", (P, 7, 1 + NSMP)), ("pool_tail", (P, 2, POOLH)), ("pool_h", (P, 2, NSMP, POOLH)),
    ("conv_tail", (P, 2, CONVK - 1)), ("conv_h", (P, 2, NSMP, CONVK - 1)), ("ssm_tail", (P, 6, SSMK - 1)),
    ("ssm_h", (P, 6, NSMP, SSMK - 1)), ("wkv_p", (P, 2, P)), ("wkv_s", (P, NSMP, 2, HD)), ("ssm_p", (P, 2, P)),
    ("ssm_s", (P, NSMP, 2, P)),
]


def pack(I):
    A = {k: np.asarray(x) for k, x in I.items()}

    def fm(a):
        a = np.moveaxis(a, -1, 0)
        return np.moveaxis(a.reshape((a.shape[0] // P, P) + a.shape[1:]), 1, 0)

    x = np.concatenate([A["x_prompt"][0], A["x_sample"][:, 0]], 0)
    w_in = A["w_in"][0]
    off_pool = 896
    off_conv, off_ssm = off_pool + 256, off_pool + 256 + 512
    off_dt = off_ssm + 256 + 768
    off_gate = off_dt + 4

    def tiles(w):
        return w.reshape(KT, P, -1, P).transpose(1, 2, 0, 3)

    gate = w_in[:, off_gate:].reshape(D, BR, KT, P)[:, [1, 0, 2, 3]].transpose(0, 2, 1, 3).reshape(D, -1)
    br = A["w_branch"][0][[1, 0, 2, 3]].reshape(BR, 2, P, KT, P).transpose(2, 3, 0, 1, 4).reshape(P, KT, KT, P)
    w_all = np.concatenate([tiles(w_in[:, :off_dt]), tiles(gate), br], 1).reshape(P, N_W, KT * P)

    vec = np.zeros((P, NVEC), np.float32)

    def put(name, a):
        o, w = VEC[name]
        vec[:, o:o + w] = np.broadcast_to(a, (P, w)) if a.ndim == 1 else a.reshape(P, w)

    for name, key in [("mu", "rwkv_mu"), ("w0", "rwkv_w0"), ("a0", "rwkv_a0"), ("kkw", "rwkv_kk"), ("ka", "rwkv_ka"),
                      ("ln_g", "rwkv_ln_g"), ("ln_b", "rwkv_ln_b"), ("pool_scale", "pool_scale"), ("conv_b", "conv_b"),
                      ("conv_ln_g", "conv_ln_g"), ("conv_ln_b", "conv_ln_b"), ("ssm_b", "ssm_conv_b"), ("ssm_g", "ssm_norm_g"),
                      ("g_mix", "norm_mix_g")]:
        put(name, fm(A[key][0]))
    put("rk", fm(A["rwkv_rk"][0].reshape(-1)))
    put("ssm_d", fm(np.repeat(A["ssm_d"][0], HD)))
    put("conv_w", fm(A["conv_w"][0]))
    put("ssm_w", fm(A["ssm_conv_w"][0]))
    put("dt_bias", A["ssm_dt_bias"][0])
    put("a_log", A["ssm_a_log"][0])
    put("r_bias", np.concatenate([A["moe_router_group_b"][0], A["moe_router_expert_b"][0]]))

    pool_w = np.zeros((P, 2, P), np.float32)
    for g in range(4):
        o = 64 * (g % 2)
        pool_w[o:o + 64, g // 2, o:o + 64] = A["pool_w"][0, g]

    def state(a):
        return a.reshape(NSMP, 2, 2, HD, -1).transpose(2, 3, 0, 1, 4).reshape(P, NSMP, 2, -1)

    gu = np.concatenate([A["moe_w_gate"][0], A["moe_w_up"][0]], 2)
    out = {
        "x_t": fm(x), "w_all": w_all, "vec": vec, "cst": constants(),
        "lora_w": np.concatenate([A["rwkv_w2"][0], A["rwkv_a2"][0], A["rwkv_g2"][0]], 0), "pool_w": pool_w,
        "w_dt": w_in[:, off_dt:off_gate].reshape(KT, P, 4).transpose(1, 0, 2),
        "w_r": np.concatenate([A["moe_router_group_w"][0], A["moe_router_expert_w"][0]], 1).reshape(KT, P, 20).transpose(1, 0, 2),
        "shift_in": fm(A["state_rwkv_shift"][0]), "pool_h": fm(A["state_pool"][0]), "conv_h": fm(A["state_conv"][0]),
        "ssm_h": fm(A["state_ssm_conv"][0]), "wkv": state(A["state_rwkv_wkv"][0]), "ssm": state(A["state_ssm"][0]),
        "w_gu": gu.reshape(NE, KT, P, 2 * HID).transpose(0, 2, 1, 3).reshape(NE * P, -1),
        "w_dn": A["moe_w_down"][0].reshape(NE, 2, P, D).transpose(0, 2, 1, 3).reshape(NE * P, -1),
        "x": x, "gains": np.broadcast_to(np.stack([A["norm_ffn_g"][0], A["final_norm_g"]]), (P, 2, D)),
        "w_out": A["w_out"][0].reshape(KT, P, 2, HALF).transpose(1, 2, 0, 3).reshape(P, 2, KT * HALF),
    }
    return {k: np.ascontiguousarray(a, dtype=np.float32) for k, a in out.items()}


def unpack(r):
    def ft(a):
        a = np.moveaxis(a, 0, 1)
        return np.moveaxis(a.reshape((-1,) + a.shape[2:]), 0, -1)

    def heads(a):
        return a.reshape(2, HD, NSMP, 2, -1).transpose(2, 3, 0, 1, 4).reshape(NSMP, 4, HD, -1)

    y = r["y"]
    shift = ft(r["shift"])
    st = r["wkv_p"].reshape(2, HD, 2, 2, HD)
    wkv_p = np.stack([st[h % 2, :, h // 2, h % 2, :].T for h in range(4)])
    ssm_p = r["ssm_p"].reshape(P, 4, HD).transpose(1, 2, 0)
    res = (y[None, :TP], y[TP:, None], shift[None, :1], wkv_p[None, None], ft(r["pool_tail"])[None, None],
           ft(r["conv_tail"])[None, None], ft(r["ssm_tail"])[None, None], ssm_p[None, None],
           shift[None, 1:], heads(r["wkv_s"])[None], ft(r["pool_h"])[None], ft(r["conv_h"])[None], ft(r["ssm_h"])[None],
           heads(r["ssm_s"])[None])
    return tuple(np.ascontiguousarray(a) for a in res)


def kernel(**inputs):
    import concourse.bacc as bacc
    from concourse.bass_utils import run_bass_kernel_spmd

    nc = bacc.Bacc("TRN2", target_bir_lowering=False, num_devices=1)
    arrays = pack(inputs)
    ins = {n: nc.dram_tensor("in_" + n, s, F32, kind="ExternalInput").ap() for n, s in SPECS}
    outs = {n: nc.dram_tensor("out_" + n, s, F32, kind="ExternalOutput").ap() for n, s in OUTS}
    build(nc, ins, outs)
    r = run_bass_kernel_spmd(nc, [{"in_" + n: arrays[n] for n, _ in SPECS}], core_ids=[0])
    return unpack({n: r.results[0]["out_" + n] for n, _ in OUTS})
```
